# Optimizing a Trainium2 kernel written in Bass

```python
import math
import jax
import jax.numpy as jnp
from jax import lax
import numpy as np

D_MODEL = 1024
BATCH = 1
SEQ = 128
DEPTH = 1
DEC_BATCH = 1
DEC_SEQ = 1024
PAST_LEN = 128

GRID_W = 64
GLA_HEADS = 4
GLA_KEY = D_MODEL // 2
GLA_VAL = D_MODEL
GLA_DK = GLA_KEY // GLA_HEADS
GLA_DV = GLA_VAL // GLA_HEADS
GATE_RANK = 16
GLA_TAU = 16.0
GLA_CHUNK = 64
S5_WIDTH = D_MODEL
S5_GROUP = 16
S5_GROUPS = S5_WIDTH // S5_GROUP
S5_STATE = 64
S5_CHUNK = 128
LRU_WIDTH = 3 * D_MODEL // 2
LRU_BLOCK = 128
LRU_BLOCKS = LRU_WIDTH // LRU_BLOCK
LRU_CONV = 4
LRU_C = 8.0
MLP_HIDDEN = 4 * D_MODEL
ALPHA = (2.0 * DEPTH) ** 0.25
BETA = (8.0 * DEPTH) ** -0.25
IN_WIDTHS = (GLA_KEY, GLA_KEY, GLA_VAL, GLA_VAL, 2 * GATE_RANK, S5_WIDTH, LRU_WIDTH, LRU_WIDTH, 3 * D_MODEL)
IN_COLS = sum(IN_WIDTHS)

kernel_name = "hybrid_gla_s5_rglru_flow_step"

F32 = jnp.float32

def _flip(z):
    return jnp.flip(z, axis=1)

def _in_splits():
    return tuple(int(i) for i in np.cumsum(IN_WIDTHS)[:-1])

def layer_norm(x, g, b, eps=1e-5):
    xf = x.astype(F32)
    mu = jnp.mean(xf, axis=-1, keepdims=True)
    var = jnp.mean(jnp.square(xf - mu), axis=-1, keepdims=True)
    y = (xf - mu) * lax.rsqrt(var + eps)
    return (y * g.astype(F32) + b.astype(F32)).astype(x.dtype)

def grid_pos_embed(n_tokens, dim):
    rows = n_tokens // GRID_W
    quarter = dim // 4
    omega = 1.0 / (10000.0 ** (jnp.arange(quarter, dtype=F32) / quarter))
    r = jnp.arange(rows, dtype=F32)[:, None, None] * omega
    cl = jnp.arange(GRID_W, dtype=F32)[None, :, None] * omega
    shape = (rows, GRID_W, quarter)
    emb = jnp.concatenate([jnp.broadcast_to(jnp.sin(r), shape), jnp.broadcast_to(jnp.cos(r), shape),
                           jnp.broadcast_to(jnp.sin(cl), shape), jnp.broadcast_to(jnp.cos(cl), shape)], axis=-1)
    return emb.reshape(rows * GRID_W, dim)

def gla_scan(q, k, v, log_a, s0):
    bsz, T, H, DK = q.shape
    DV = v.shape[-1]
    n = T // GLA_CHUNK

    def chunks(z):
        return z.reshape(bsz, n, GLA_CHUNK, H, z.shape[-1])

    q, k, v, log_a = chunks(q), chunks(k), chunks(v), chunks(log_a)
    cum = jnp.cumsum(log_a, axis=2)
    last = cum[:, :, -1:]
    q_dec = q * jnp.exp(cum)
    k_inv = k * jnp.exp(-cum)
    k_end = k * jnp.exp(last - cum)
    mask = jnp.tril(jnp.ones((GLA_CHUNK, GLA_CHUNK), dtype=bool))
    scores = jnp.where(mask, jnp.einsum("bnthk,bnshk->bnhts", q_dec, k_inv), 0.0)
    o_intra = jnp.einsum("bnhts,bnshv->bnthv", scores, v)
    upd = jnp.einsum("bnshk,bnshv->nbhkv", k_end, v)
    decay = jnp.exp(jnp.moveaxis(last[:, :, 0], 1, 0))

    def step(S, inp):
        d, u = inp
        return d[..., None] * S + u, S

    s_fin, s_start = lax.scan(step, s0, (decay, upd))
    o_inter = jnp.einsum("bnthk,nbhkv->bnthv", q_dec, s_start)
    return (o_intra + o_inter).reshape(bsz, T, H, DV), s_fin

def _complex_combine(e1, e2):
    a1r, a1i, b1r, b1i = e1
    a2r, a2i, b2r, b2i = e2
    return (a2r * a1r - a2i * a1i, a2r * a1i + a2i * a1r,
            a2r * b1r - a2i * b1i + b2r, a2r * b1i + a2i * b1r + b2i)

def _real_combine(e1, e2):
    return (e1[0] * e2[0], e2[0] * e1[1] + e2[1])

def s5_scan(u, lam_re, lam_im, log_step, b_re, b_im, c_re, c_im, s_re0, s_im0):
    bsz, T, G, I = u.shape
    n = T // S5_CHUNK
    step = jnp.exp(log_step)[:, None]
    mag = jnp.exp(lam_re * step)
    ang = lam_im * step
    ab_re, ab_im = mag * jnp.cos(ang), mag * jnp.sin(ang)
    den = jnp.square(lam_re) + jnp.square(lam_im)
    nr = ab_re - 1.0
    f_re = (nr * lam_re + ab_im * lam_im) / den
    f_im = (ab_im * lam_re - nr * lam_im) / den
    bb_re = f_re[..., None] * b_re - f_im[..., None] * b_im
    bb_im = f_re[..., None] * b_im + f_im[..., None] * b_re
    u_chunks = jnp.moveaxis(u.reshape(bsz, n, S5_CHUNK, G, I), 1, 0)

    def chunk_step(carry, u_c):
        s_re, s_im = carry
        x_re = jnp.einsum("bcgi,gpi->bcgp", u_c, bb_re)
        x_im = jnp.einsum("bcgi,gpi->bcgp", u_c, bb_im)
        x_re = x_re.at[:, 0].add(ab_re * s_re - ab_im * s_im)
        x_im = x_im.at[:, 0].add(ab_re * s_im + ab_im * s_re)
        a_re = jnp.broadcast_to(ab_re, x_re.shape)
        a_im = jnp.broadcast_to(ab_im, x_im.shape)
        _, _, h_re, h_im = lax.associative_scan(_complex_combine, (a_re, a_im, x_re, x_im), axis=1)
        y = jnp.einsum("bcgp,gip->bcgi", h_re, c_re) - jnp.einsum("bcgp,gip->bcgi", h_im, c_im)
        return (h_re[:, -1], h_im[:, -1]), y

    (s_re, s_im), ys = lax.scan(chunk_step, (s_re0, s_im0), u_chunks)
    return jnp.moveaxis(ys, 0, 1).reshape(bsz, T, G, I), s_re, s_im

def rglru_scan(x, gate_a, gate_i, lam, h0):
    log_a = -LRU_C * jax.nn.softplus(-lam) * jax.nn.sigmoid(gate_a)
    a = jnp.exp(log_a)
    b = jnp.sqrt(-jnp.expm1(2.0 * log_a)) * (jax.nn.sigmoid(gate_i) * x)
    b = b.at[:, 0].add(a[:, 0] * h0)
    _, h = lax.associative_scan(_real_combine, (a, b), axis=1)
    return h, h[:, -1]

def centred_depthwise_conv(x, w, bias):
    T = x.shape[1]
    left = LRU_CONV // 2
    right = LRU_CONV - 1 - left
    xp = jnp.pad(x, ((0, 0), (left, right), (0, 0)))
    return bias + sum(w[j] * xp[:, j:j + T] for j in range(LRU_CONV))

def mixer(h, lw, init):
    gla0, s5re0, s5im0, lru0 = [s.astype(F32) for s in init]
    bsz, T, _ = h.shape
    dt = h.dtype
    proj = h @ lw["w_in"]
    q, k, v, r, glr, u, lx, ly, gates = jnp.split(proj, _in_splits(), axis=-1)

    qh = q.astype(F32).reshape(bsz, T, GLA_HEADS, GLA_DK) * (GLA_DK ** -0.5)
    kh = k.astype(F32).reshape(bsz, T, GLA_HEADS, GLA_DK)
    vh = v.astype(F32).reshape(bsz, T, GLA_HEADS, GLA_DV)
    logits = jnp.einsum("bter,erk->btek", glr.astype(F32).reshape(bsz, T, 2, GATE_RANK),
                        lw["gla_w_gate"].astype(F32)) + lw["gla_b_gate"].astype(F32)
    log_a = (jax.nn.log_sigmoid(logits) / GLA_TAU).reshape(bsz, T, 2, GLA_HEADS, GLA_DK)
    o_f, sg_f = gla_scan(qh, kh, vh, log_a[:, :, 0], gla0[:, 0])
    o_b, sg_b = gla_scan(_flip(qh), _flip(kh), _flip(vh), _flip(log_a[:, :, 1]), gla0[:, 1])
    o = o_f + _flip(o_b)
    mu = jnp.mean(o, axis=-1, keepdims=True)
    var = jnp.mean(jnp.square(o - mu), axis=-1, keepdims=True)
    on = ((o - mu) * lax.rsqrt(var + 1e-5)).reshape(bsz, T, GLA_VAL)
    y_gla = (on * lw["gla_norm_g"].astype(F32) * jax.nn.silu(r.astype(F32))).astype(dt)

    uf = u.astype(F32)
    ug = uf.reshape(bsz, T, S5_GROUPS, S5_GROUP)
    s5p = [lw[nm].astype(F32) for nm in ("s5_b_re", "s5_b_im", "s5_c_re", "s5_c_im")]
    lam_re = lw["s5_lam_re"].astype(F32)
    lam_im = lw["s5_lam_im"].astype(F32)
    log_step = lw["s5_log_step"].astype(F32)
    ys_f, sr_f, si_f = s5_scan(ug, lam_re[0], lam_im[0], log_step[0], *s5p, s5re0[:, 0], s5im0[:, 0])
    ys_b, sr_b, si_b = s5_scan(_flip(ug), lam_re[1], lam_im[1], log_step[1], *s5p, s5re0[:, 1], s5im0[:, 1])
    ys = (ys_f + _flip(ys_b)).reshape(bsz, T, S5_WIDTH) + lw["s5_d"].astype(F32) * uf
    ys = jax.nn.gelu(ys).astype(dt)
    y_s5 = ys * jax.nn.sigmoid(ys @ lw["s5_w_glu"])

    xc = centred_depthwise_conv(lx, lw["lru_conv_w"], lw["lru_conv_b"]).astype(F32)
    xb = xc.reshape(bsz, T, LRU_BLOCKS, LRU_BLOCK)
    ga = jnp.einsum("btnc,encd->btend", xb, lw["lru_w_a"].astype(F32)).reshape(bsz, T, 2, LRU_WIDTH) \
        + lw["lru_b_a"].astype(F32)
    gi = jnp.einsum("btnc,encd->btend", xb, lw["lru_w_i"].astype(F32)).reshape(bsz, T, 2, LRU_WIDTH) \
        + lw["lru_b_i"].astype(F32)
    lam = lw["lru_lam"].astype(F32)
    hf, lf = rglru_scan(xc, ga[:, :, 0], gi[:, :, 0], lam[0], lru0[:, 0])
    hb, lb = rglru_scan(_flip(xc), _flip(ga[:, :, 1]), _flip(gi[:, :, 1]), lam[1], lru0[:, 1])
    y_lru = ((hf + _flip(hb)) * jax.nn.gelu(ly.astype(F32))).astype(dt)

    g_gla, g_s5, g_lru = jnp.split(jax.nn.sigmoid(gates), 3, axis=-1)
    merged = (g_gla * (y_gla @ lw["w_br_gla"]) + g_s5 * (y_s5 @ lw["w_br_s5"])
              + g_lru * (y_lru @ lw["w_br_lru"]))
    out = merged @ lw["w_out"]
    finals = (jnp.stack([sg_f, sg_b], axis=1), jnp.stack([sr_f, sr_b], axis=1),
              jnp.stack([si_f, si_b], axis=1), jnp.stack([lf, lb], axis=1))
    return out, finals

def trunk_layer(x, mod, lw, init):
    shift1, scale1, gate1, shift2, scale2, gate2 = jnp.split(mod[:, None, :], 6, axis=-1)
    mix, finals = mixer(x * (1 + scale1) + shift1, lw, init)
    x = layer_norm(ALPHA * x + gate1 * mix, lw["ln1_g"], lw["ln1_b"])
    hid = jnp.square(jax.nn.relu((x * (1 + scale2) + shift2) @ lw["w_mlp_in"]))
    x = layer_norm(ALPHA * x + gate2 * (hid @ lw["w_mlp_out"]), lw["ln2_g"], lw["ln2_b"])
    return x, finals

def setup_inputs(seed: int = 0) -> dict:
    key = jax.random.key(seed)
    ks = iter(jax.random.split(key, 64))
    L, D = DEPTH, D_MODEL

    def nrm(shape, scale):
        return scale * jax.random.normal(next(ks), shape, F32)

    def unif(shape, lo, hi):
        return jax.random.uniform(next(ks), shape, F32, lo, hi)

    lru_a8 = unif((L, 2, LRU_WIDTH), 0.9, 0.999)
    lru_s = lru_a8 ** (1.0 / LRU_C)
    inp = {}
    inp["x_prompt"] = nrm((BATCH, SEQ, D), 1.0)
    inp["x_sample"] = nrm((DEC_BATCH, DEC_SEQ, D), 1.0)
    inp["state_gla"] = nrm((DEC_BATCH, L, 2, GLA_HEADS, GLA_DK, GLA_DV), 1.0)
    inp["state_s5_re"] = nrm((DEC_BATCH, L, 2, S5_GROUPS, S5_STATE), 0.1)
    inp["state_s5_im"] = nrm((DEC_BATCH, L, 2, S5_GROUPS, S5_STATE), 0.1)
    inp["state_lru"] = nrm((DEC_BATCH, L, 2, LRU_WIDTH), 0.5)
    inp["c"] = nrm((DEC_BATCH, D), 1.0)
    inp["c_ctx"] = nrm((D,), 1.0)
    inp["w_ada"] = nrm((L, D, 6 * D), 0.5 * D ** -0.5)
    inp["b_ada"] = nrm((L, 6 * D), 0.02)
    inp["w_in"] = nrm((L, D, IN_COLS), D ** -0.5)
    inp["gla_w_gate"] = nrm((L, 2, GATE_RANK, GLA_KEY), GATE_RANK ** -0.5)
    inp["gla_b_gate"] = nrm((L, 2, GLA_KEY), 0.1)
    inp["gla_norm_g"] = 1.0 + nrm((L, GLA_VAL), 0.02)
    inp["s5_lam_re"] = -0.5 + nrm((L, 2, S5_GROUPS, S5_STATE), 0.01)
    inp["s5_lam_im"] = jnp.pi * jnp.arange(S5_STATE, dtype=F32) + nrm((L, 2, S5_GROUPS, S5_STATE), 0.01)
    inp["s5_log_step"] = unif((L, 2, S5_GROUPS), math.log(0.001), math.log(0.1))
    inp["s5_b_re"] = nrm((L, S5_GROUPS, S5_STATE, S5_GROUP), (2 * S5_GROUP) ** -0.5)
    inp["s5_b_im"] = nrm((L, S5_GROUPS, S5_STATE, S5_GROUP), (2 * S5_GROUP) ** -0.5)
    inp["s5_c_re"] = nrm((L, S5_GROUPS, S5_GROUP, S5_STATE), S5_STATE ** -0.5)
    inp["s5_c_im"] = nrm((L, S5_GROUPS, S5_GROUP, S5_STATE), S5_STATE ** -0.5)
    inp["s5_d"] = nrm((L, S5_WIDTH), 1.0)
    inp["s5_w_glu"] = nrm((L, S5_WIDTH, S5_WIDTH), S5_WIDTH ** -0.5)
    inp["lru_conv_w"] = nrm((L, LRU_CONV, LRU_WIDTH), LRU_CONV ** -0.5)
    inp["lru_conv_b"] = nrm((L, LRU_WIDTH), 0.02)
    inp["lru_w_a"] = nrm((L, 2, LRU_BLOCKS, LRU_BLOCK, LRU_BLOCK), LRU_BLOCK ** -0.5)
    inp["lru_b_a"] = nrm((L, 2, LRU_WIDTH), 0.1)
    inp["lru_w_i"] = nrm((L, 2, LRU_BLOCKS, LRU_BLOCK, LRU_BLOCK), LRU_BLOCK ** -0.5)
    inp["lru_b_i"] = nrm((L, 2, LRU_WIDTH), 0.1)
    inp["lru_lam"] = jnp.log(lru_s) - jnp.log1p(-lru_s)
    inp["w_br_gla"] = nrm((L, GLA_VAL, D), GLA_VAL ** -0.5)
    inp["w_br_s5"] = nrm((L, S5_WIDTH, D), S5_WIDTH ** -0.5)
    inp["w_br_lru"] = nrm((L, LRU_WIDTH, D), LRU_WIDTH ** -0.5)
    inp["w_out"] = nrm((L, D, D), BETA * D ** -0.5)
    inp["ln1_g"] = 1.0 + nrm((L, D), 0.02)
    inp["ln1_b"] = nrm((L, D), 0.02)
    inp["ln2_g"] = 1.0 + nrm((L, D), 0.02)
    inp["ln2_b"] = nrm((L, D), 0.02)
    inp["w_mlp_in"] = nrm((L, D, MLP_HIDDEN), D ** -0.5)
    inp["w_mlp_out"] = nrm((L, MLP_HIDDEN, D), BETA * MLP_HIDDEN ** -0.5)
    return inp

def reference(x_prompt, x_sample, state_gla, state_s5_re, state_s5_im, state_lru, c, c_ctx,
              w_ada, b_ada, w_in, gla_w_gate, gla_b_gate, gla_norm_g,
              s5_lam_re, s5_lam_im, s5_log_step, s5_b_re, s5_b_im, s5_c_re, s5_c_im, s5_d, s5_w_glu,
              lru_conv_w, lru_conv_b, lru_w_a, lru_b_a, lru_w_i, lru_b_i, lru_lam,
              w_br_gla, w_br_s5, w_br_lru, w_out, ln1_g, ln1_b, ln2_g, ln2_b, w_mlp_in, w_mlp_out):
    bp = x_prompt.shape[0]
    xp = x_prompt
    xs = x_sample + grid_pos_embed(x_sample.shape[1], D_MODEL).astype(x_sample.dtype)
    silu_ctx = jax.nn.silu(c_ctx)[None]
    silu_c = jax.nn.silu(c)
    zero_init = (jnp.zeros((bp, 2, GLA_HEADS, GLA_DK, GLA_DV), F32),
                 jnp.zeros((bp, 2, S5_GROUPS, S5_STATE), F32),
                 jnp.zeros((bp, 2, S5_GROUPS, S5_STATE), F32),
                 jnp.zeros((bp, 2, LRU_WIDTH), F32))
    fin_gla, fin_s5_re, fin_s5_im, fin_lru = [], [], [], []
    for l in range(DEPTH):
        lw = {"w_in": w_in[l], "gla_w_gate": gla_w_gate[l], "gla_b_gate": gla_b_gate[l],
              "gla_norm_g": gla_norm_g[l], "s5_lam_re": s5_lam_re[l], "s5_lam_im": s5_lam_im[l],
              "s5_log_step": s5_log_step[l], "s5_b_re": s5_b_re[l], "s5_b_im": s5_b_im[l],
              "s5_c_re": s5_c_re[l], "s5_c_im": s5_c_im[l], "s5_d": s5_d[l], "s5_w_glu": s5_w_glu[l],
              "lru_conv_w": lru_conv_w[l], "lru_conv_b": lru_conv_b[l], "lru_w_a": lru_w_a[l],
              "lru_b_a": lru_b_a[l], "lru_w_i": lru_w_i[l], "lru_b_i": lru_b_i[l], "lru_lam": lru_lam[l],
              "w_br_gla": w_br_gla[l], "w_br_s5": w_br_s5[l], "w_br_lru": w_br_lru[l], "w_out": w_out[l],
              "ln1_g": ln1_g[l], "ln1_b": ln1_b[l], "ln2_g": ln2_g[l], "ln2_b": ln2_b[l],
              "w_mlp_in": w_mlp_in[l], "w_mlp_out": w_mlp_out[l]}
        mod_ctx = silu_ctx @ w_ada[l] + b_ada[l]
        xp, fin = trunk_layer(xp, mod_ctx, lw, zero_init)
        fin_gla.append(fin[0])
        fin_s5_re.append(fin[1])
        fin_s5_im.append(fin[2])
        fin_lru.append(fin[3])
        mod_lat = silu_c @ w_ada[l] + b_ada[l]
        cache_l = (state_gla[:, l], state_s5_re[:, l], state_s5_im[:, l], state_lru[:, l])
        xs, _ = trunk_layer(xs, mod_lat, lw, cache_l)
    sdt = x_prompt.dtype
    new_state_gla = jnp.stack(fin_gla, axis=1).astype(sdt)
    new_state_s5_re = jnp.stack(fin_s5_re, axis=1).astype(sdt)
    new_state_s5_im = jnp.stack(fin_s5_im, axis=1).astype(sdt)
    new_state_lru = jnp.stack(fin_lru, axis=1).astype(sdt)
    return (xp, xs, new_state_gla, new_state_s5_re, new_state_s5_im, new_state_lru)


_drawn_inputs = setup_inputs


def setup_inputs(seed=0):
    import zlib

    import numpy as np

    out = dict(_drawn_inputs(seed))
    spreads = {}
    factors = {'state_gla': 8.0,
     'state_s5_re': 41.122,
     'state_s5_im': 42.036,
     'state_lru': 17.913,
     'gla_norm_g': 159.267,
     's5_lam_re': 80.13,
     's5_c_re': 38.1,
     's5_c_im': 37.474,
     's5_w_glu': 21.71,
     'lru_b_a': 3.789,
     'ln1_g': 7.841,
     'ln1_b': 7.992,
     'ln2_g': 7.175,
     'ln2_b': 19.53,
     's5_d': 4.206,
     'w_br_s5': 2.811}
    for name, (base, spread) in spreads.items():
        noise = np.random.default_rng([zlib.crc32(name.encode()), seed]).standard_normal(out[name].shape)
        drawn = base * np.exp(spread * noise) if base else spread * noise
        out[name] = jnp.asarray(drawn.astype(out[name].dtype))
    for name, factor in factors.items():
        out[name] = (out[name] * factor).astype(out[name].dtype)
    return out
```

```python
from contextlib import ExitStack

import numpy as np

import concourse.bass as bass
from concourse import mybir

F32 = mybir.dt.float32
F32R = mybir.dt.float32r
I32 = mybir.dt.int32

ALU = mybir.AluOpType
ACT = mybir.ActivationFunctionType

P = 128
D = 1024
KD = D // P
TC = 128
TS = 1024
T = TC + TS
NB = 3
BW = T // NB
GRID_W = 64
ROWS = TS // GRID_W
ALPHA = 2.0 ** 0.25
LN_EPS = 1e-5
HEADS = 4
DK = 128
DV = 256
RANK = 16
GLA_TAU = 16.0
GCH = 64
NPAIR = T // P
LBLK = 12
CONV = 4
LRU_C = 8.0
LXW = T + 6
LXC = 2
LXS = TC + 5
XCW = LXW - CONV + 1
XCS = LXS - LXC
GROUPS = 64
S5P = 64
S5I = 16
SCH = 8
NCH = T // SCH
NCC = TC // SCH
NCS = TS // SCH
GB = 8
NBATCH = GROUPS // GB
HID = 4 * D
HG = 4
NHG = HID // P // HG

UW = 1024
PROJ0 = 7
(PC_W, PC_B, PC_BA, PC_BI, PC_C, PC_H0, PC_NEG, PC_NEG2) = (0, 4, 5, 7, 9, 11, 13, 15)
NPC = 17


class Chain:

    def __init__(self, eng, sem, i=0, per=0):
        self.eng, self.sem, self.base, self.per, self.n = eng, sem, i * per, per, 0

    def mark(self, ins):
        ins.then_inc(self.sem, 1)
        self.n += 1

    def sync(self):
        self.eng.wait_ge(self.sem, self.base + self.n)

    def __call__(self, ins):
        self.mark(ins)
        self.sync()

    def end(self):
        assert self.n == self.per, (self.n, self.per)


def move(dve, out, in_):
    return dve.tensor_scalar(out, in_, 1.0, None, ALU.mult)


def rev(ap):
    return ap[:, ::-1]


class Core:

    def __init__(self, nc, ctx, dram):
        self.nc, self.ctx, self.dram = nc, ctx, dram
        self.zero = ctx.enter_context(nc.sbuf_tensor("zero", [P, 1], F32))[:, 0:1]
        self.bank = [ctx.enter_context(nc.psum_tensor(f"bank{i}", [P, 512], F32)) for i in range(8)]
        self.stage, self.sems = 1, []

    def sem(self, name):
        self.sems.append(self.nc.alloc_semaphore(name=f"stage{self.stage}_{name}"))
        return self.sems[-1]

    def end_stage(self):
        self.nc.clear_and_free_semaphores(self.sems)
        self.nc.all_engine_barrier()
        self.stage, self.sems = self.stage + 1, []


class Stream:

    def __init__(self, core, ctx, name):
        nc = core.nc
        self.core = core
        self.raw = [ctx.enter_context(nc.sbuf_tensor(f"{name}_raw{s}", [P, UW], F32)) for s in range(2)]
        self.hi = [ctx.enter_context(nc.sbuf_tensor(f"{name}_hi{s}", [P, UW], F32R)) for s in range(2)]
        self.lo = [ctx.enter_context(nc.sbuf_tensor(f"{name}_lo{s}", [P, UW], F32R)) for s in range(2)]
        self.raw_in = [core.sem(f"{name}_raw_in{s}") for s in range(2)]
        self.hi_done = core.sem(f"{name}_hi_done")
        self.split_done = core.sem(f"{name}_split_done")
        self.proj_done = core.sem(f"{name}_proj_done")
        self.bank_free = [core.sem(f"{name}_bank_free{s}") for s in range(2)]

    def prime(self, sync):
        sync.sem_inc(self.split_done, 2)
        sync.sem_inc(self.proj_done, PROJ0)
        sync.sem_inc(self.bank_free[0], 3)
        sync.sem_inc(self.bank_free[1], 3)

    def load(self, sync, u, par, src, width=UW):
        sync.wait_ge(self.split_done, u + 1)
        sync.dma_start(self.raw[par][:, 0:width], src).then_inc(self.raw_in[par], 16)

    def split(self, pool, u, par, q, groups_before, width=UW, used=None):
        pool.wait_ge(self.raw_in[par], 16 * q + 16)
        if used is None:
            pool.wait_ge(self.proj_done, groups_before + PROJ0)
        else:
            pool.wait_ge(used[0], used[1])
        w = slice(0, width)
        pool.tensor_tensor(self.hi[par][:, w], self.raw[par][:, w], self.core.zero.to_broadcast([P, width]),
                           ALU.add).then_inc(self.hi_done, 1)
        pool.wait_ge(self.hi_done, u + 1)
        pool.tensor_tensor(self.lo[par][:, w], self.raw[par][:, w], self.hi[par][:, w].bitcast(F32),
                           ALU.subtract).then_inc(self.split_done, 1)

    def project(self, pe, u, par, q, rhi, rlo, set_=None, nk=KD, k0=0, wait_split=True, start=True, stop=True,
                free=None):
        set_ = par if set_ is None else set_
        if wait_split:
            pe.wait_ge(self.split_done, u + 3)
        for b in range(NB):
            if start:
                sem, base = free or (self.bank_free[set_], 3 * q)
                pe.wait_ge(sem, base + b + 1)
            out = self.core.bank[3 * set_ + b][:, 0:BW]
            cols = slice(b * BW, (b + 1) * BW)
            for k in range(nk):
                w = slice((k0 + k) * P, (k0 + k + 1) * P)
                for n, (wt, r) in enumerate(((self.hi, rhi), (self.hi, rlo), (self.lo, rhi))):
                    mm = pe.matmul(out, wt[par][:, w], r[:, k, cols],
                                   start=(start and k == 0 and n == 0), stop=(stop and k == nk - 1 and n == 2))
            mm.then_inc(self.proj_done, 1)


def modulate(core, hhi, hlo, mod):
    nc, dram = core.nc, core.dram
    with ExitStack() as ctx:
        ctx.callback(core.end_stage)

        def sb(name, shape, dt=F32):
            return ctx.enter_context(nc.sbuf_tensor(name, shape, dt))

        def sem(name):
            return core.sem(name)

        NSLOT = 8
        NADA = 6 * KD
        ada = [sb(f"ada{s}", [P, UW]) for s in range(NSLOT)]
        x = sb("x", [P, KD, T])
        h = [sb(f"h{s}", [P, T]) for s in range(2)]
        cvec = sb("cvec", [P, KD, 2])
        csilu = sb("csilu", [P, KD, 2])
        bada = sb("bada", [P, NADA])
        pos_r = sb("pos_r", [P, KD // 2, ROWS])
        pos_c = sb("pos_c", [P, KD // 2, GRID_W])
        small_in, x_in, silu_done, mod_mm, pos_done, mod_done = (
            sem(n) for n in ("small_in", "x_in", "silu_done", "mod_mm", "pos_done", "mod_done"))
        ada_in = [sem(f"ada_in{s}") for s in range(NSLOT)]
        dve_step, h_done, hi_done, lo_done, xres_out = (
            sem(n) for n in ("dve_step", "h_done", "hi_done", "lo_done", "xres_out"))

        with nc.Block() as block:
            @block.sync
            def _(sync):
                sync.dma_start(cvec[:], dram["cvec"]).then_inc(small_in, 16)
                sync.dma_start(bada[:], dram["bada"]).then_inc(small_in, 16)
                sync.dma_start(pos_r[:], dram["pos_r"]).then_inc(small_in, 16)
                sync.dma_start(pos_c[:], dram["pos_c"]).then_inc(small_in, 16)
                for m in range(NADA):
                    if m == 2 * KD:
                        sync.dma_start(x[:], dram["x_t"].rearrange("k p t -> p k t")).then_inc(x_in, 16)
                    if m >= NSLOT:
                        sync.wait_ge(mod_mm, m - NSLOT + 1)
                    sync.dma_start(ada[m % NSLOT][:], dram["w_ada"][m]).then_inc(ada_in[m % NSLOT], 16)
                sync.wait_ge(pos_done, KD)
                sync.dma_start(dram["x_res"].rearrange("k p t -> p k t"), x[:]).then_inc(xres_out, 16)
                sync.wait_ge(xres_out, 16)

            @block.gpsimd
            def _(pool):
                pool.memset(core.zero, 0.0)

            @block.tensor
            def _(pe):
                pe.wait_ge(silu_done, 1)
                for m in range(NADA):
                    pe.wait_ge(ada_in[m % NSLOT], 16 * (m // NSLOT + 1))
                    for k in range(KD):
                        mm = pe.matmul(core.bank[m // (2 * KD)][:, 2 * m:2 * m + 2], ada[m % NSLOT][:, k * P:(k + 1) * P],
                                       csilu[:, k, :], start=(k == 0), stop=(k == KD - 1))
                    mm.then_inc(mod_mm, 1)

            @block.scalar
            def _(act):
                act.wait_ge(small_in, 64)
                act.activation(csilu[:], cvec[:], ACT.Silu).then_inc(silu_done, 1)
                for k in range(KD):
                    act.wait_ge(h_done, k + 1)
                    act.activation(hhi[:, k, :], h[k % 2][:], ACT.Copy).then_inc(hi_done, 1)

            @block.vector
            def _(dve):
                step = Chain(dve, dve_step)
                dve.wait_ge(small_in, 64)
                dve.wait_ge(x_in, 16)
                for k in range(KD):
                    xs = x[:, k, TC:].rearrange("p (r c) -> p r c", c=GRID_W)
                    if k < KD // 2:
                        tab = pos_r[:, k, :].unsqueeze(2).to_broadcast([P, ROWS, GRID_W])
                    else:
                        tab = pos_c[:, k - KD // 2, :].unsqueeze(1).to_broadcast([P, ROWS, GRID_W])
                    dve.tensor_tensor(xs, xs, tab, ALU.add).then_inc(pos_done, 1)

                def take(bank, lo, hi):
                    dve.wait_ge(mod_mm, hi)
                    step(dve.tensor_tensor(
                        mod[:, lo:hi, :], core.bank[bank][:, 2 * lo:2 * hi].rearrange("p (m c) -> p m c", c=2),
                        bada[:, lo:hi].unsqueeze(2).to_broadcast([P, hi - lo, 2]), ALU.add))

                take(0, 0, 2 * KD)
                step(dve.tensor_scalar(mod[:, KD:2 * KD, :], mod[:, KD:2 * KD, :], 1.0, None, ALU.add))
                dve.wait_ge(pos_done, KD)
                for k in range(KD):
                    hk = h[k % 2]
                    if k >= 2:
                        dve.wait_ge(lo_done, k - 1)
                    for c, cols in ((0, slice(0, TC)), (1, slice(TC, T))):
                        ins = dve.tensor_scalar(hk[:, cols], x[:, k, cols], mod[:, KD + k, c:c + 1],
                                                mod[:, k, c:c + 1], ALU.mult, ALU.add)
                    ins.then_inc(h_done, 1)
                    dve.wait_ge(hi_done, k + 1)
                    dve.tensor_tensor(hlo[:, k, :], hk[:], hhi[:, k, :].bitcast(F32),
                                      ALU.subtract).then_inc(lo_done, 1)
                take(1, 2 * KD, 4 * KD)
                take(2, 4 * KD, NADA)
                step(dve.tensor_scalar(mod[:, 4 * KD:5 * KD, :], mod[:, 4 * KD:5 * KD, :], 1.0, None, ALU.add))


def lru(core, hhi, hlo):
    nc, dram = core.nc, core.dram
    with ExitStack() as ctx:
        ctx.callback(core.end_stage)

        def sb(name, shape, dt=F32):
            return ctx.enter_context(nc.sbuf_tensor(name, shape, dt))

        def sem(name):
            return core.sem(name)

        S = Stream(core, ctx, "lru")
        lw_raw = sb("lw_raw", [P, 4 * P])
        lw_hi = sb("lw_hi", [P, 4 * P], F32R)
        lw_lo = sb("lw_lo", [P, 4 * P], F32R)
        params = sb("lru_params", [P, LBLK, NPC])
        prm = sb("lru_prm", [P, NPC])
        z = sb("lru_z", [P, LBLK, 2])
        s1 = sb("lru_s1", [P, LBLK, 2])
        s2 = sb("lru_s2", [P, LBLK, 2])
        acc = sb("lru_acc", [P, LBLK, 2])
        tiny = sb("lru_tiny", [P, 1])
        lx = sb("lx", [P, LXW])
        ly = sb("ly", [P, T])
        xc = sb("xc", [P, XCW])
        xc_hi = sb("xc_hi", [P, T], F32R)
        xc_lo = sb("xc_lo", [P, T], F32R)
        rt = [sb(f"rt{d}", [P, T]) for d in range(2)]
        it = [sb(f"it{d}", [P, T]) for d in range(2)]
        at = [sb(f"at{d}", [P, T]) for d in range(2)]
        ht = [sb(f"ht{d}", [P, T]) for d in range(2)]
        y = sb("lru_y", [P, T])
        fin = sb("lru_fin", [P, 2, LBLK])
        names = ("params_in", "lru_dve", "lru_act", "lw_in", "lw_hi_done", "lw_done", "conv_done", "xh_done",
                 "xl_done", "lru_mm", "lbank_free", "s_done", "f_done", "y_done", 
                 "y_out", "zero_done", "z_done", "c_done")
        (params_in, dve_s, act_s, lw_in, lw_hi_done, lw_done, conv_done, xh_done, xl_done, lru_mm,
         lbank_free, s_done, f_done, y_done, y_out, zero_done, z_done, c_done) = (
            sem(n) for n in names)
        new_lru = dram["new_lru"]

        with nc.Block() as block:
            @block.sync
            def _(sync):
                S.prime(sync)
                sync.sem_inc(lw_done, 1)
                sync.sem_inc(lru_mm, 2)
                sync.dma_start(params[:, :, 0:PC_NEG], dram["lru_params"]).then_inc(params_in, 16)
                with sync.Fori(0, LBLK) as i:
                    for j in range(2):
                        S.load(sync, 2 * i + j, j, dram["lru_units"][bass.ds(2 * i + j, 1)].rearrange("a p n -> (a p) n"))
                        if j == 0:
                            sync.wait_ge(lw_done, i + 1)
                            sync.dma_start(lw_raw[:], dram["lru_w"][bass.ds(i, 1)].rearrange("a p n -> (a p) n")).then_inc(lw_in, 16)
                        if j == 1:
                            sync.wait_ge(y_done, i + 1)
                            sync.dma_start(dram["y_lru"][bass.ds(i, 1)].rearrange("a p n -> (a p) n"), y[:]).then_inc(y_out, 16)
                sync.wait_ge(y_done, LBLK + 1)
                sync.dma_start(dram["y_lru"][LBLK], y[:]).then_inc(y_out, 16)
                sync.dma_start(new_lru, fin[:]).then_inc(y_out, 16)
                sync.wait_ge(y_out, 16 * LBLK + 32)

            @block.gpsimd
            def _(pool):
                pool.memset(lx[:], 0.0).then_inc(zero_done, 1)
                pool.memset(tiny[:], 1e-30).then_inc(zero_done, 1)
                with pool.Fori(0, LBLK) as i:
                    for j in range(2):
                        S.split(pool, 2 * i + j, j, i, 3 * (2 * i + j) - 3)
                        if j == 1:
                            pool.wait_ge(lw_in, 16 * i + 16)
                            pool.wait_ge(lru_mm, 12 * i + 2)
                            pool.tensor_tensor(lw_hi[:], lw_raw[:], core.zero.to_broadcast([P, 4 * P]),
                                               ALU.add).then_inc(lw_hi_done, 1)
                            pool.wait_ge(lw_hi_done, i + 1)
                            pool.tensor_tensor(lw_lo[:], lw_raw[:], lw_hi[:].bitcast(F32),
                                               ALU.subtract).then_inc(lw_done, 1)

            @block.tensor
            def _(pe):
                with pe.Fori(0, LBLK) as i:
                    for j in range(2):
                        S.project(pe, 2 * i + j, j, i, hhi, hlo)
                    pe.wait_ge(lw_done, i + 2)
                    pe.wait_ge(xl_done, i + 1)
                    for g in range(12):
                        w = slice((g // NB) * P, (g // NB + 1) * P)
                        cols = slice(g % NB * BW, (g % NB + 1) * BW)
                        pe.wait_ge(lbank_free, 12 * i + g + 1)
                        out = core.bank[6 + g % 2][:, 0:BW]
                        pe.matmul(out, lw_hi[:, w], xc_hi[:, cols], start=True, stop=False)
                        pe.matmul(out, lw_hi[:, w], xc_lo[:, cols], start=False, stop=False)
                        pe.matmul(out, lw_lo[:, w], xc_hi[:, cols], start=False, stop=True).then_inc(lru_mm, 1)

            @block.scalar
            def _(act):
                act.sem_inc(lbank_free, 2)
                act.wait_ge(params_in, 16)
                lam = params[:, :, PC_C:PC_C + 2]
                st = Chain(act, act_s)
                st(act.activation(z[:], lam, ACT.Abs))
                act.activation(z[:], z[:], ACT.Exp, scale=-1.0).then_inc(z_done, 1)
                act.wait_ge(zero_done, 2)
                act.wait_ge(z_done, 1)
                act.wait_ge(c_done, 1)
                HEAD, PER = 1, 6
                with act.Fori(0, LBLK) as i:
                    st = Chain(act, act_s, i, PER)
                    st.base = st.base + HEAD
                    proj = 6 * i + PROJ0
                    act.wait_ge(conv_done, i + 1)
                    act.wait_ge(S.proj_done, proj + 1)
                    act.activation(lx[:, LXC:LXC + TC], core.bank[0][:, 0:TC], ACT.Copy)
                    act.activation(lx[:, LXS:LXS + BW - TC], core.bank[0][:, TC:BW], ACT.Copy).then_inc(S.bank_free[0], 1)
                    for b in (1, 2):
                        act.wait_ge(S.proj_done, proj + b + 1)
                        c0 = LXS + b * BW - TC
                        act.activation(lx[:, c0:c0 + BW], core.bank[b][:, 0:BW], ACT.Copy).then_inc(S.bank_free[0], 1)
                    act.wait_ge(y_done, i + 1)
                    for b in range(NB):
                        act.wait_ge(S.proj_done, proj + 3 + b + 1)
                        act.activation(ly[:, b * BW:(b + 1) * BW], core.bank[3 + b][:, 0:BW],
                                       ACT.Gelu_apprx_tanh).then_inc(S.bank_free[1], 1)
                    act.wait_ge(conv_done, i + 2)
                    act.wait_ge(lru_mm, 12 * i + 2)
                    act.activation(xc_hi[:, 0:TC], xc[:, 0:TC], ACT.Copy)
                    act.activation(xc_hi[:, TC:T], xc[:, XCS:XCS + TS], ACT.Copy).then_inc(xh_done, 1)
                    for g in range(12):
                        q = g // NB
                        d = q // 2
                        dst = rt[d] if q % 2 == 0 else it[d]
                        col = (PC_BA if q % 2 == 0 else PC_BI) + d
                        act.wait_ge(lru_mm, 12 * i + g + 3)
                        act.activation(dst[:, g % NB * BW:(g % NB + 1) * BW], core.bank[6 + g % 2][:, 0:BW],
                                       ACT.Sigmoid, bias=prm[:, col:col + 1]).then_inc(lbank_free, 1)
                    act.wait_ge(lbank_free, 12 * i + 14)
                    for d in range(2):
                        st(act.activation(at[d][:], rt[d][:], ACT.Exp, scale=prm[:, PC_NEG + d:PC_NEG + d + 1]))
                        st(act.activation(ht[d][:], rt[d][:], ACT.Exp, scale=prm[:, PC_NEG2 + d:PC_NEG2 + d + 1]))
                        st(act.activation(rt[d][:], rt[d][:], ACT.Tanh, scale=prm[:, PC_C + d:PC_C + d + 1]))
                    for d in range(2):
                        act.wait_ge(s_done, 2 * i + d + 1)
                        act.activation(rt[d][:], ht[d][:], ACT.Sqrt, bias=tiny[:, 0:1]).then_inc(f_done, 1)
                    st.end()

            @block.vector
            def _(dve):
                st = Chain(dve, dve_s)
                dve.wait_ge(z_done, 1)
                dve.wait_ge(params_in, 16)
                lam = params[:, :, PC_C:PC_C + 2]
                st(dve.tensor_scalar(s1[:], z[:], 2.0, None, ALU.add))
                st(dve.reciprocal(s1[:], s1[:]))
                st(dve.tensor_tensor(s1[:], s1[:], z[:], ALU.mult))
                st(dve.tensor_tensor(s2[:], s1[:], s1[:], ALU.mult))
                st(dve.tensor_scalar(acc[:], s2[:], 1.0 / 17, 1.0 / 15, ALU.mult, ALU.add))
                for n in (13, 11, 9, 7, 5, 3, 1):
                    st(dve.tensor_tensor(acc[:], acc[:], s2[:], ALU.mult))
                    st(dve.tensor_scalar(acc[:], acc[:], 1.0 / n, None, ALU.add))
                st(dve.scalar_tensor_tensor(acc[:], acc[:], 2.0, s1[:], ALU.mult, ALU.mult))
                st(dve.tensor_scalar(s2[:], lam, -1.0, 0.0, ALU.mult, ALU.max))
                st(dve.tensor_tensor(acc[:], acc[:], s2[:], ALU.add))
                st(dve.tensor_scalar(lam, acc[:], LRU_C, None, ALU.mult))
                st(dve.tensor_scalar(params[:, :, PC_NEG:PC_NEG + 2], acc[:], -LRU_C, None, ALU.mult))
                st(dve.tensor_scalar(params[:, :, PC_NEG2:PC_NEG2 + 2], acc[:], -2 * LRU_C, None, ALU.mult))
                dve.sem_inc(c_done, 1)
                st(dve.memset(y[:], 0.0))
                dve.sem_inc(y_done, 1)
                dve.sem_inc(conv_done, 1)
                head = st.n
                dve.wait_ge(zero_done, 2)
                PER = 17
                with dve.Fori(0, LBLK) as i:
                    st = Chain(dve, dve_s, i, PER)
                    st.base = st.base + head
                    st(dve.tensor_copy(prm[:], params[:, bass.ds(i, 1), :].rearrange("p a n -> p (a n)")))
                    dve.wait_ge(S.bank_free[0], 3 * i + 6)
                    st(dve.tensor_scalar(xc[:], lx[:, 0:XCW], prm[:, PC_W:PC_W + 1], prm[:, PC_B:PC_B + 1],
                                         ALU.mult, ALU.add))
                    for n in (1, 2, 3):
                        ins = dve.scalar_tensor_tensor(xc[:], lx[:, n:n + XCW], prm[:, PC_W + n:PC_W + n + 1], xc[:],
                                                       ALU.mult, ALU.add)
                        if n < 3:
                            st(ins)
                    ins.then_inc(conv_done, 1)
                    dve.wait_ge(xh_done, i + 1)
                    dve.tensor_tensor(xc_lo[:, 0:TC], xc[:, 0:TC], xc_hi[:, 0:TC].bitcast(F32), ALU.subtract)
                    dve.tensor_tensor(xc_lo[:, TC:T], xc[:, XCS:XCS + TS], xc_hi[:, TC:T].bitcast(F32),
                                      ALU.subtract).then_inc(xl_done, 1)
                    for d in range(2):
                        dve.wait_ge(act_s, 6 * i + 3 * d + 3 + 1)
                        ins = dve.scalar_tensor_tensor(ht[d][:], ht[d][:], 1.0, rt[d][:], ALU.add, ALU.mult)
                        ins.then_inc(s_done, 1)
                    for d in range(2):
                        dve.wait_ge(f_done, 2 * i + d + 1)
                        st(dve.tensor_tensor(it[d][:], it[d][:], rt[d][:], ALU.mult))
                        st(dve.tensor_tensor(it[d][:, 0:TC], it[d][:, 0:TC], xc[:, 0:TC], ALU.mult))
                        st(dve.tensor_tensor(it[d][:, TC:T], it[d][:, TC:T], xc[:, XCS:XCS + TS], ALU.mult))
                        for lo, hi, init in ((0, TC, 0.0), (TC, T, prm[:, PC_H0 + d:PC_H0 + d + 1])):
                            a, b, o = (v[d][:, lo:hi] for v in (at, it, ht))
                            if d:
                                a, b, o = rev(a), rev(b), rev(o)
                            st(dve.tensor_tensor_scan(o, a, b, init, ALU.mult, ALU.add))
                    for d, at_t in ((0, TC - 1), (1, 0)):
                        st(dve.tensor_copy(fin[:, d, bass.ds(i, 1)], ht[d][:, at_t:at_t + 1]))
                    dve.wait_ge(y_out, 16 * i + 16)
                    st(dve.tensor_tensor(y[:], ht[0][:], ht[1][:], ALU.add))
                    dve.wait_ge(S.bank_free[1], 3 * i + 6)
                    dve.tensor_tensor(y[:], y[:], ly[:], ALU.mult).then_inc(y_done, 1)
                    dve.wait_ge(y_done, i + 2)
                    st.end()


def gla(core, hhi, hlo):
    nc, dram = core.nc, core.dram
    with ExitStack() as ctx:
        ctx.callback(core.end_stage)

        def sb(name, shape, dt=F32):
            return ctx.enter_context(nc.sbuf_tensor(name, shape, dt))

        def sem(name):
            return core.sem(name)

        S = Stream(core, ctx, "gla")
        glr = sb("glr", [P, T])
        wgate = sb("wgate", [P, HEADS, DK])
        wg = sb("wg", [P, DK])
        params = sb("gla_params", [P, HEADS, 4])
        prm = sb("gla_prm", [P, 4])
        q, k = sb("q", [P, T]), sb("k", [P, T])
        v, r = sb("v", [P, 2, T]), sb("r", [P, 2, T])
        qd = [sb(f"qd{d}", [P, T]) for d in range(2)]
        ki = [sb(f"ki{d}", [P, T]) for d in range(2)]
        ke = [sb(f"ke{d}", [P, T]) for d in range(2)]
        dec = [sb(f"dec{d}", [P, T // GCH]) for d in range(2)]
        tok = sb("tok", [P, NPAIR, 2 * DV])
        o = sb("o", [P, 2, T])
        state = [sb(f"state{s}", [P, DV]) for s in range(6)]
        cached = [sb(f"cached{d}", [P, DV]) for d in range(2)]
        final = [sb(f"final{d}", [P, DV]) for d in range(2)]
        probs = [[sb(f"probs{d}{s}", [P, P]) for s in range(2)] for d in range(2)]
        keep = sb("keep", [P, 2, P], I32)
        ident = sb("ident", [P, P])
        ones = sb("ones", [P, P])
        run = sb("run", [P, T], mybir.dt.bfloat16)
        eps = sb("gla_eps", [P, 1])
        (small_in, state_in, lg_mm, lg_free, ln_done, cum_done, ec_done, gated, tp_mm, tp_free, sc_mm, st_done,
         o_mm, o_done, ns_mm, ns_free, sq_done, y_done, y_out, head_ready, act_s, dve_s, const_done, final_done,
         ) = (
            sem(n) for n in (
                "small_in", "state_in", "lg_mm", "lg_free", "ln_done", "cum_done", "ec_done", "gated", "tp_mm",
                "tp_free", "sc_mm", "st_done", "o_mm", "o_done", "ns_mm", "ns_free", "sq_done", "y_done", "y_out",
                "head_ready", "act_s", "dve_s", "const_done", "final_done"))
        copy_turn = sem("copy_turn")
        final_out = [sem(f"final_out{d}") for d in range(2)]
        UPH = 6
        NSTEP = 2 * NPAIR
        STEPS = [(0, n) for n in range(NPAIR)] + [(1, 0)] + [(1, n) for n in range(NPAIR - 1, 0, -1)]

        def unit(h, j):
            return UPH * h + 1 + j, (1 + j) % 2, 3 * h + (j + 1) // 2

        def start_state(s, c):
            d, n = STEPS[s]
            if c == 0 and n == 0:
                return None
            if c == 0 and STEPS[s - 1][1] == 0:
                return cached[d]
            return state[(2 * s + c) % 6]

        def end_state(s, c):
            d, n = STEPS[s]
            if c == 1 and n == 0:
                return final[d]
            if c == 1 and (s + 1 == NSTEP or STEPS[s + 1][0] != d):
                return None
            return state[(2 * s + c + 1) % 6]

        def update(s, c):
            return core.bank[3 * (s % 2) + 1 - c][:, P:P + DV]

        with nc.Block() as block:
            @block.sync
            def _(sync):
                S.prime(sync)
                sync.dma_start(wgate[0:64], dram["gla_wgate"]).then_inc(small_in, 16)
                sync.dma_start(params[:], dram["gla_params"]).then_inc(small_in, 16)
                sync.dma_start(keep[:], dram["keep"]).then_inc(small_in, 16)
                sync.dma_start(ident[:], dram["ident"]).then_inc(small_in, 16)
                S.load(sync, 0, 0, dram["gla_units"][0])
                with sync.Fori(0, HEADS) as h:
                    for j in range(UPH):
                        u, par, _ = unit(h, j)
                        S.load(sync, u, par, dram["gla_units"][bass.ds(u, 1)].rearrange("a p n -> (a p) n"))
                        if j == 1:
                            sync.wait_ge(y_done, h + 1)
                            sync.dma_start(dram["y_gla"][bass.ds(2 * h, 2)].rearrange("a p n -> p a n"), o[:]).then_inc(y_out, 16)
                            for d in range(2):
                                sync.dma_start(cached[d][:], dram["state_gla"][bass.ds(HEADS * d + h, 1)]
                                               .rearrange("a p n -> (a p) n")).then_inc(state_in, 16)
                    for d in range(2):
                        sync.wait_ge(final_done, 2 * h + d + 1)
                        sync.dma_start(dram["new_gla"][bass.ds(HEADS * d + h, 1)].rearrange("a p n -> (a p) n"),
                                       final[d][:]).then_inc(final_out[d], 16)
                sync.wait_ge(y_done, HEADS + 1)
                sync.dma_start(dram["y_gla"][2 * HEADS:2 * HEADS + 2].rearrange("a p n -> p a n"), o[:]).then_inc(y_out, 16)
                sync.wait_ge(y_out, 16 * HEADS + 16)
                for d in range(2):
                    sync.wait_ge(final_out[d], 16 * HEADS + 16)

            @block.gpsimd
            def _(pool):
                pool.memset(ones[:], 1.0 / DV).then_inc(const_done, 1)
                pool.memset(eps[:], 1e-5).then_inc(const_done, 1)
                for d in range(2):
                    for s in range(2):
                        pool.memset(probs[d][s][:], 0.0).then_inc(const_done, 1)
                S.split(pool, 0, 0, 0, -3)
                with pool.Fori(0, HEADS) as h:
                    for j in range(UPH):
                        u, par, q_ = unit(h, j)
                        S.split(pool, u, par, q_, 3 * u - 3)

            @block.tensor
            def _(pe):
                pe.wait_ge(const_done, 6)
                S.project(pe, 0, 0, 0, hhi, hlo)
                with pe.Fori(0, HEADS) as h:
                    pe.wait_ge(head_ready, h + 1)
                    pe.wait_ge(S.bank_free[0], 9 * h + 6)
                    for g in range(6):
                        d = g // NB
                        pe.wait_ge(lg_free, 6 * h + g + 1)
                        pe.matmul(core.bank[6 + g % 2][:, 0:BW], wg[32 * d:32 * d + RANK, :],
                                  glr[32 * d:32 * d + RANK, g % NB * BW:(g % NB + 1) * BW],
                                  start=True, stop=True).then_inc(lg_mm, 1)
                    for j in range(UPH):
                        u, par, q_ = unit(h, j)
                        S.project(pe, u, par, q_, hhi, hlo)
                    pe.wait_ge(S.bank_free[1], 9 * h + 9)
                    pe.wait_ge(S.bank_free[0], 9 * h + 12)
                    pe.wait_ge(gated, 2 * h + 2)
                    pe.wait_ge(lg_free, 6 * h + 8)
                    for n in range(NPAIR):
                        cols = slice(n * P, (n + 1) * P)
                        pe.wait_ge(tp_free, NPAIR * h + n + 1)
                        out = core.bank[6 + n % 2]
                        for c, src in enumerate((v[:, 0, cols], v[:, 1, cols], ke[0][:, cols], ke[1][:, cols])):
                            mm = pe.transpose(out[:, c * P:(c + 1) * P], src, ident[:])
                        mm.then_inc(tp_mm, 1)

                    def scores(s):
                        d, n = STEPS[s]
                        cols = slice(n * P, (n + 1) * P)
                        if s < 2:
                            pe.wait_ge(S.bank_free[1], 9 * h + 12)
                            pe.wait_ge(S.bank_free[0], 9 * h + 15)
                            pe.wait_ge(tp_free, NPAIR * h + NPAIR + 2)
                        else:
                            pe.wait_ge(st_done, NSTEP * h + s - 1)
                        pe.matmul(core.bank[3 * (s % 2)][:, 0:P], ki[d][:, cols], qd[d][:, cols], start=True, stop=True)
                        for c in range(2):
                            if end_state(s, c) is None:
                                continue
                            half = c if d == 0 else 1 - c
                            rows = slice(GCH * half, GCH * half + GCH)
                            mm = pe.matmul(update(s, c),
                                           tok[rows, n, DV + d * DK:DV + (d + 1) * DK], tok[rows, n, 0:DV],
                                           start=True, stop=True)
                        mm.then_inc(sc_mm, 1)

                    scores(0)
                    for s, (d, n) in enumerate(STEPS):
                        if s + 1 < NSTEP:
                            scores(s + 1)
                        if s == 0:
                            pe.wait_ge(state_in, 32 * h + 32)
                        pe.wait_ge(st_done, NSTEP * h + s + 1)
                        if s >= 2:
                            pe.wait_ge(o_done, NSTEP * h + s - 1)
                        for vt in range(2):
                            out = core.bank[3 * (s % 2) + 2][:, vt * P:(vt + 1) * P]
                            vc = slice(vt * P, (vt + 1) * P)
                            inter = [c for c in range(2) if start_state(s, c) is not None]
                            mm = pe.matmul(out, tok[:, n, vc], probs[d][s % 2][:], start=True, stop=not inter)
                            for c in inter:
                                half = c if d == 0 else 1 - c
                                t0 = n * P + half * GCH
                                mm = pe.matmul(out[:, half * GCH:(half + 1) * GCH], start_state(s, c)[:, vc],
                                               qd[d][:, t0:t0 + GCH], start=False, stop=(c == inter[-1]))
                        mm.then_inc(o_mm, 1)
                    pe.wait_ge(o_done, NSTEP * h + NSTEP)
                    for g in range(6):
                        b = g % NB
                        cols = slice(b * BW, (b + 1) * BW)
                        src = o if g < NB else v
                        if g >= 2:
                            pe.wait_ge(ns_free, 6 * h + g - 1)
                        if g >= NB:
                            pe.wait_ge(sq_done, NB * h + b + 1)
                        out = core.bank[6 + g % 2][:, 0:BW]
                        pe.matmul(out, ones[:], src[:, 0, cols], start=True, stop=False)
                        pe.matmul(out, ones[:], src[:, 1, cols], start=False, stop=True).then_inc(ns_mm, 1)
                    pe.wait_ge(ns_free, 6 * h + 6)

            @block.scalar
            def _(act):
                act.sem_inc(lg_free, 2)
                act.sem_inc(final_out[0], 16)
                act.sem_inc(final_out[1], 16)
                act.sem_inc(tp_free, 2)
                act.wait_ge(const_done, 6)
                for b in range(NB):
                    act.wait_ge(S.proj_done, PROJ0 + b + 1)
                    act.activation(glr[:, b * BW:(b + 1) * BW], core.bank[b][:, 0:BW], ACT.Copy).then_inc(S.bank_free[0], 1)
                PER = 6
                with act.Fori(0, HEADS) as h:
                    st = Chain(act, act_s, h, PER)

                    def evac(j, dst, func, scale=1.0):
                        u, par, _ = unit(h, j)
                        for b in range(NB):
                            act.wait_ge(S.proj_done, 3 * u + b + 1 + PROJ0)
                            act.activation(dst[:, b * BW:(b + 1) * BW], core.bank[3 * par + b][:, 0:BW], func,
                                           scale=scale).then_inc(S.bank_free[par], 1)

                    for g in range(6):
                        act.wait_ge(lg_mm, 6 * h + g + 1)
                        act.activation(qd[g // NB][:, g % NB * BW:(g % NB + 1) * BW], core.bank[6 + g % 2][:, 0:BW],
                                       ACT.Identity, bias=prm[:, g // NB:g // NB + 1]).then_inc(lg_free, 1)
                    act.wait_ge(lg_free, 6 * h + 8)
                    for d in range(2):
                        st(act.activation(ki[d][:], qd[d][:], ACT.Abs))
                        st(act.activation(ki[d][:], ki[d][:], ACT.Exp, scale=-1.0))
                        act.activation(ki[d][:], ki[d][:], ACT.Ln, bias=1.0).then_inc(ln_done, 1)
                    act.wait_ge(y_done, h + 1)
                    evac(0, q, ACT.Copy, DK ** -0.5)
                    evac(1, k, ACT.Copy)
                    for d in range(2):
                        act.wait_ge(cum_done, 2 * h + d + 1)
                        st(act.activation(qd[d][:], ki[d][:], ACT.Exp, scale=1.0 / GLA_TAU))
                        act.activation(ki[d][:], ki[d][:], ACT.Exp, scale=-1.0 / GLA_TAU).then_inc(ec_done, 1)
                    evac(2, v[:, 0, :], ACT.Copy)
                    evac(3, v[:, 1, :], ACT.Copy)
                    evac(4, r[:, 0, :], ACT.Silu)
                    evac(5, r[:, 1, :], ACT.Silu)
                    for n in range(NPAIR):
                        act.wait_ge(tp_mm, NPAIR * h + n + 1)
                        act.activation(tok[:, n, :], core.bank[6 + n % 2][:, :], ACT.Copy).then_inc(tp_free, 1)
                    for b in range(NB):
                        cols = slice(b * BW, (b + 1) * BW)
                        act.wait_ge(ns_free, 6 * h + b + 1)
                        act.activation(v[:, :, cols], o[:, :, cols], ACT.Square).then_inc(sq_done, 1)
                    for b in range(NB):
                        act.wait_ge(ns_mm, 6 * h + NB + b + 1)
                        act.activation(k[:, b * BW:(b + 1) * BW], core.bank[6 + (NB + b) % 2][:, 0:BW], ACT.Sqrt,
                                       bias=eps[:, 0:1]).then_inc(ns_free, 1)
                    st.end()

            @block.vector
            def _(dve):
                st = Chain(dve, dve_s)
                st(dve.memset(run[:], 1.0))
                st(dve.memset(run[:, ::GCH], 0.0))
                st(dve.memset(o[:], 0.0))
                dve.sem_inc(y_done, 1)
                dve.wait_ge(small_in, 64)
                dve.wait_ge(const_done, 6)
                head = st.n
                PER = 64
                with dve.Fori(0, HEADS) as h:
                    st = Chain(dve, dve_s, h, PER)
                    st.base = st.base + head
                    st(dve.tensor_copy(prm[:], params[:, bass.ds(h, 1), :].rearrange("p a n -> p (a n)")))
                    dve.tensor_copy(wg[0:64, :], wgate[0:64, bass.ds(h, 1), :].rearrange("p a n -> p (a n)")).then_inc(head_ready, 1)
                    for d in range(2):
                        dve.wait_ge(ln_done, 2 * h + d + 1)
                        st(dve.scalar_tensor_tensor(qd[d][:], qd[d][:], 0.0, ki[d][:], ALU.min, ALU.subtract))
                        a, c = qd[d][:], ki[d][:]
                        if d:
                            a, c = rev(a), rev(c)
                        dve.tensor_tensor_scan(c, run[:], a, 0.0, ALU.mult, ALU.add).then_inc(cum_done, 1)
                    dve.wait_ge(S.bank_free[1], 9 * h + 6)
                    dve.wait_ge(S.bank_free[0], 9 * h + 9)
                    for d in range(2):
                        dve.wait_ge(ec_done, 2 * h + d + 1)
                        last = slice(GCH - 1, T, GCH) if d == 0 else slice(0, T, GCH)
                        st(dve.tensor_copy(dec[d][:], qd[d][:, last]))
                        st(dve.tensor_tensor(ki[d][:], k[:], ki[d][:], ALU.mult))
                        st(dve.tensor_tensor(ke[d][:].rearrange("p (c t) -> p c t", t=GCH),
                                             ki[d][:].rearrange("p (c t) -> p c t", t=GCH),
                                             dec[d][:].unsqueeze(2).to_broadcast([P, T // GCH, GCH]), ALU.mult))
                        dve.tensor_tensor(qd[d][:], q[:], qd[d][:], ALU.mult).then_inc(gated, 1)

                    def collect(s):
                        d, n = STEPS[s]
                        dve.wait_ge(o_mm, NSTEP * h + s + 1)
                        ov = o[:, :, n * P:(n + 1) * P]
                        psum = core.bank[3 * (s % 2) + 2][:, 0:2 * P].rearrange("p (v t) -> p v t", v=2)
                        if d == 0:
                            dve.tensor_copy(ov, psum).then_inc(o_done, 1)
                        else:
                            dve.tensor_tensor(ov, ov, psum, ALU.add).then_inc(o_done, 1)

                    dve.wait_ge(y_out, 16 * h + 16)
                    dve.wait_ge(state_in, 32 * h + 32)
                    for s, (d, n) in enumerate(STEPS):
                        dve.wait_ge(sc_mm, NSTEP * h + s + 1)
                        if s >= 2:
                            dve.wait_ge(o_mm, NSTEP * h + s - 1)
                        dve.sem_inc(copy_turn, 1)
                        st(dve.copy_predicated(probs[d][s % 2][:], keep[:, d, :], core.bank[3 * (s % 2)][:, 0:P]))
                        for c in range(2):
                            dst = end_state(s, c)
                            if dst is None:
                                continue
                            half = c if d == 0 else 1 - c
                            ch = 2 * n + half
                            upd = update(s, c)
                            src = start_state(s, c)
                            if src is None:
                                st(dve.tensor_copy(dst[:], upd))
                            else:
                                if c == 1 and n == 0:
                                    dve.wait_ge(final_out[d], 16 * h + 16)
                                st(dve.scalar_tensor_tensor(dst[:], src[:], dec[d][:, ch:ch + 1], upd,
                                                            ALU.mult, ALU.add))
                        dve.sem_inc(st_done, 1)
                        if n == 0:
                            dve.sem_inc(final_done, 1)
                        if s:
                            collect(s - 1)
                    collect(NSTEP - 1)
                    dve.wait_ge(o_done, NSTEP * h + NSTEP)
                    for b in range(NB):
                        ov = o[:, :, b * BW:(b + 1) * BW]
                        dve.wait_ge(ns_mm, 6 * h + b + 1)
                        mean = core.bank[6 + b % 2][:, 0:BW].unsqueeze(1).to_broadcast([P, 2, BW])
                        dve.tensor_tensor(ov, ov, mean, ALU.subtract).then_inc(ns_free, 1)
                    dve.wait_ge(ns_free, 6 * h + 6)
                    st(dve.reciprocal(q[:], k[:]))
                    for vt in range(2):
                        st(dve.scalar_tensor_tensor(o[:, vt, :], o[:, vt, :], prm[:, 2 + vt:3 + vt], q[:],
                                                    ALU.mult, ALU.mult))
                    dve.tensor_tensor(o[:], o[:], r[:], ALU.mult).then_inc(y_done, 1)
                    dve.wait_ge(y_done, h + 2)
                    st.end()


def s5_and_gates(core, hhi, hlo):
    nc, dram = core.nc, core.dram
    with ExitStack() as ctx:
        ctx.callback(core.end_stage)

        def sb(name, shape, dt=F32):
            return ctx.enter_context(nc.sbuf_tensor(name, shape, dt))

        def sem(name):
            return core.sem(name)

        GH = GROUPS // 2
        BPH = GH // GB
        LAGS = SCH + 1
        H1, H2 = slice(0, S5P), slice(S5P, P)
        UNITS_U, UNITS_G = KD, 3 * KD
        S = Stream(core, ctx, "s5")
        lam = sb("lam", [P, 3, GROUPS])
        pw = [sb(f"pw{c}", [P, LAGS, GROUPS]) for c in "ri"]
        sm = [sb(f"sm{n}", [P, GROUPS]) for n in range(8)]
        coef = sb("coef", [P, 2, 2, GROUPS])
        bb = [sb(f"bb{c}", [P, GROUPS, S5I]) for c in "ri"]
        cc = [sb(f"cc{c}", [P, GROUPS, S5I]) for c in "ri"]
        init = sb("s5_init", [P, 2, GROUPS])
        fins = sb("s5_fins", [P, 2, GROUPS])
        cur = [sb(f"cur{s}", [P, 2, GH]) for s in range(2)]
        cofs = [sb(f"cofs{n}", [P, 2, GH]) for n in range(2)]
        t0 = sb("t0", [P, 2, GH])
        t1 = sb("t1", [P, 2, GH])
        hs = sb("hs", [P, NCH, 2, GH])
        ub = sb("ub", [P, GB, NCH])
        work = sb("work", [P, 2 * GB * LAGS * S5I + 2 * GB * NCH])
        NW = GB * SCH * S5I
        wt = [work[:, c * NW:(c + 1) * NW] for c in range(2)]
        win = work[:, 2 * NW:4 * NW].rearrange("p (x m) -> p x m", m=P)
        NCA = GB * LAGS * S5I
        ca = [work[:, c * NCA:(c + 1) * NCA] for c in range(2)]
        hn = work[:, 2 * NCA:2 * NCA + 2 * GB * NCH].rearrange("p (r g c) -> p r g c", r=2, g=GB)
        tmp = sb("s5tmp", [P, NCA])
        ws = [sb(f"ws{c}", [P, GB, SCH]) for c in "ri"]
        cq = [sb(f"cq{c}", [P, GB, LAGS]) for c in "ri"]
        bblk = [sb(f"bblk{c}", [P, GB, 2 * S5I]) for c in "ri"]
        bdup = [sb(f"bdup{c}", [P, GB, 2 * S5I]) for c in "ri"]
        wia = sb("wia", [P, GB, P])
        KW = (LAGS + 1) * S5I
        stage = sb("stage", [P, T + GB * KW])
        gate = [stage[:, s * T:(s + 1) * T] for s in range(2)]
        yb = stage[:, 0:T].rearrange("p (g c) -> p g c", g=GB)
        kst = stage[0:32, T:T + GB * KW].rearrange("p (g a) -> p g a", a=KW)
        ident = sb("s5_ident", [P, P])
        up = [gate[s].rearrange("p (s c) -> p s c", s=SCH) for s in range(2)]
        (p_in, act_p, trig, u_out, ub_in, wt_done, tr_mm, tr_free, w_mm, w_free_f, w_free_b, w_used, new, prod,
         saved, dve_s, act_s, ca_done, k_mm, k_free, kd_out, wia_in, hn_done, y_mm, y_free, yb_out, u_free,
         half_ready, scan_done, fin_out, up_ready, ws_s) = (
            sem(n) for n in (
                "p_in", "act_p", "trig", "u_out", "ub_in", "wt_done", "tr_mm", "tr_free", "w_mm",
                "w_free_f", "w_free_b", "w_used", "new", "prod", "saved", "dve_s", "act_s", "ca_done", "k_mm", "k_free",
                "kd_out", "wia_in", "hn_done", "y_mm", "y_free", "yb_out", "u_free", "half_ready", "scan_done",
                "fin_out", "up_ready", "ws_s"))
        turn = sem("turn")
        gate_out = [sem(f"s5_gate_out{s}") for s in range(2)]
        u_st = [sem(f"u_st{s}") for s in range(2)]

        def v3(ap, a):
            return ap.rearrange("p (g a i) -> p g a i", g=GB, a=a)

        def load_u(eng, n):
            for s in range(SCH):
                src = dram["u_d"][bass.ds(n * P, P)].rearrange("(g j) s c -> j g s c", j=S5I)[:, :, s, :]
                eng.dma_start(ub[s * S5I:(s + 1) * S5I, :, :], src).then_inc(ub_in, 16)

        with nc.Block() as block:
            @block.sync
            def _(sync):
                S.prime(sync)
                for e in range(2):
                    half = slice(e * S5P, (e + 1) * S5P)
                    sync.dma_start(lam[half, 0, :], dram["s5_lam"][0, half]).then_inc(p_in, 16)
                    sync.dma_start(lam[half, 1, :], dram["s5_lam"][1, half]).then_inc(p_in, 16)
                    sync.dma_start(lam[half, 2, :], dram["s5_step"][e].partition_broadcast(S5P)).then_inc(p_in, 16)
                    for c in range(2):
                        sync.dma_start(bb[c][half], dram["s5_b"][c]).then_inc(p_in, 16)
                        sync.dma_start(cc[c][half], dram["s5_c"][c]).then_inc(p_in, 16)
                sync.dma_start(init[:], dram["s5_init"]).then_inc(p_in, 16)
                sync.dma_start(ident[:], dram["ident"]).then_inc(p_in, 16)
                for m in range(UNITS_U):
                    S.load(sync, m, m % 2, dram["s5_units"][m])
                    if m >= 1:
                        sync.wait_ge(S.bank_free[(m - 1) % 2], 3 + 3 * ((m - 1) // 2 + 1))
                        sync.dma_start(dram["u_d"][(m - 1) * P:m * P], up[(m - 1) % 2]).then_inc(u_st[(m - 1) % 2], 16)
                m = UNITS_U
                sync.wait_ge(S.bank_free[(m - 1) % 2], 3 + 3 * ((m - 1) // 2 + 1))
                sync.dma_start(dram["u_d"][(m - 1) * P:m * P], up[(m - 1) % 2]).then_inc(u_st[(m - 1) % 2], 16)
                for s in range(2):
                    sync.wait_ge(u_st[s], 16 * UNITS_U // 2)
                with sync.Fori(0, 2) as hf:
                    with sync.Fori(0, BPH) as i:
                        n = BPH * hf + i
                        sync.wait_ge(u_free, 2 * BPH * hf + i + 1)
                        load_u(sync, n)
                    for j in range(UNITS_G // 2):
                        u = UNITS_U + UNITS_G // 2 * hf + j
                        S.load(sync, u, j % 2, dram["s5_units"][bass.ds(u, 1)].rearrange("a p n -> (a p) n"))
                    with sync.Fori(0, BPH) as i:
                        n = BPH * hf + i
                        sync.wait_ge(u_free, 2 * BPH * hf + BPH + i + 1)
                        load_u(sync, n)
                        sync.wait_ge(k_free, 3 * n + 6)
                        kd = dram["kd"][bass.ds(n * GB, GB)].rearrange("g j d i -> j g (d i)")
                        sync.dma_start(kd[:, :, SCH * S5I:(2 * SCH - 1) * S5I],
                                       kst[0:S5I, :, S5I:SCH * S5I]).then_inc(kd_out, 16)
                        sync.dma_start(kd[:, :, 0:(SCH - 1) * S5I],
                                       kst[S5I:2 * S5I, :, 2 * S5I:LAGS * S5I]).then_inc(kd_out, 16)
                        sync.dma_start(kd[:, :, (SCH - 1) * S5I:SCH * S5I],
                                       kst[0:S5I, :, LAGS * S5I:(LAGS + 1) * S5I]).then_inc(kd_out, 16)
                        sync.wait_ge(kd_out, 48 * n + 48)
                        for s in range(SCH):
                            d0 = (SCH - 1 - s) * S5I
                            sync.dma_start(wia[s * S5I:(s + 1) * S5I], kd[:, :, d0:d0 + P]).then_inc(wia_in, 16)
                        sync.wait_ge(y_free, 3 * n + 6)
                        for t in range(SCH):
                            dst = dram["y_d"][bass.ds(n * P, P)].rearrange("(g i) t c -> i g t c", i=S5I)[:, :, t, :]
                            sync.dma_start(dst, yb[t * S5I:(t + 1) * S5I]).then_inc(yb_out, 16)
                        sync.wait_ge(yb_out, 128 * n + 128)
                        sync.sem_inc(half_ready, 1)
                sync.wait_ge(scan_done, 2)
                sync.dma_start(dram["new_s5"], fins[:]).then_inc(fin_out, 16)
                sync.wait_ge(fin_out, 16)

            @block.gpsimd
            def _(pool):
                for u in range(UNITS_U):
                    S.split(pool, u, u % 2, u // 2, 3 * u - 3)
                with pool.Fori(0, 2) as hf:
                    for j in range(UNITS_G // 2):
                        u = UNITS_U + UNITS_G // 2 * hf + j
                        S.split(pool, u, j % 2, UNITS_U // 2 + UNITS_G // 4 * hf + j // 2, 3 * u - 3)

            @block.tensor
            def _(pe):
                for u in range(UNITS_U):
                    S.project(pe, u, u % 2, u // 2, hhi, hlo)
                with pe.Fori(0, 2) as hf:
                    q0 = UNITS_U // 2 + UNITS_G // 4 * hf
                    for par in range(2):
                        pe.wait_ge(S.bank_free[par], 3 * q0 + 3)
                    pe.sem_inc(turn, 1)
                    with pe.Fori(0, BPH) as i:
                        n = BPH * hf + i
                        pe.wait_ge(wt_done, n + 1)
                        for x in range(4):
                            pe.wait_ge(tr_free, 4 * n + x + 1)
                            for y in range(4):
                                g, c = 2 * x + y // 2, y % 2
                                mm = pe.transpose(core.bank[6 + x % 2][:, y * P:(y + 1) * P],
                                                  wt[c][:, g * P:(g + 1) * P], ident[:])
                            mm.then_inc(tr_mm, 1)
                        pe.wait_ge(ub_in, 128 * (2 * BPH * hf + i) + 128)
                        pe.wait_ge(tr_free, 4 * n + 6)
                        for g in range(GB):
                            pe.wait_ge(w_free_f, GB * n + g + 1)
                            pe.wait_ge(w_free_b, GB * n + g + 1)
                            for c in range(2):
                                mm = pe.matmul(core.bank[g % 4][:, c * NCH:(c + 1) * NCH], win[:, 2 * g + c, :],
                                               ub[:, g, :], start=True, stop=True)
                            mm.then_inc(w_mm, 1)
                        pe.wait_ge(w_mm, GB * n + GB)
                        pe.sem_inc(u_free, 1)
                    pe.wait_ge(w_free_f, GB * BPH * hf + GB * BPH + 4)
                    pe.wait_ge(w_free_b, GB * BPH * hf + GB * BPH + 4)
                    for j in range(UNITS_G // 2):
                        S.project(pe, UNITS_U + UNITS_G // 2 * hf + j, j % 2, q0 + j // 2, hhi, hlo)
                    for par in range(2):
                        pe.wait_ge(S.bank_free[par], 3 * q0 + 3 * (UNITS_G // 4) + 3)
                    pe.sem_inc(turn, 1)
                    with pe.Fori(0, BPH) as i:
                        n = BPH * hf + i
                        pe.wait_ge(ca_done, n + 1)
                        cav = [v3(ca[c], LAGS) for c in range(2)]
                        for x, gs in enumerate(((0, 1, 2), (3, 4, 5), (6, 7))):
                            pe.wait_ge(k_free, 3 * n + x + 1)
                            for g in gs:
                                o0 = (g - gs[0]) * (LAGS + 1) * S5I
                                out = core.bank[x][0:32, o0:o0 + LAGS * S5I]
                                for c in range(2):
                                    pe.matmul(out, bblk[c][:, g, :], cav[c][:, g, :, :].rearrange("p a i -> p (a i)"),
                                              start=(c == 0), stop=(c == 1))
                                out = core.bank[x][0:32, o0 + LAGS * S5I:o0 + (LAGS + 1) * S5I]
                                for c in range(2):
                                    mm = pe.matmul(out, bdup[c][:, g, :], cav[c][:, g, 0, :],
                                                   start=(c == 0), stop=(c == 1))
                            mm.then_inc(k_mm, 1)
                        pe.wait_ge(wia_in, 128 * n + 128)
                        pe.wait_ge(hn_done, n + 1)
                        pe.wait_ge(ub_in, 128 * (2 * BPH * hf + BPH + i) + 128)
                        for x, gs in enumerate(((0, 1, 2), (3, 4, 5), (6, 7))):
                            pe.wait_ge(y_free, 3 * n + x + 1)
                            for g in gs:
                                out = core.bank[3 + x][:, (g - gs[0]) * NCH:(g - gs[0] + 1) * NCH]
                                pe.matmul(out, wia[:, g, :], ub[:, g, :], start=True, stop=False)
                                for c in range(2):
                                    mm = pe.matmul(out, cav[c][:, g, 1:LAGS, :].rearrange("p a i -> p (a i)"),
                                                   hn[:, c, g, :], start=False, stop=(c == 1))
                            mm.then_inc(y_mm, 1)
                        pe.wait_ge(y_mm, 3 * n + 3)
                        pe.sem_inc(u_free, 1)
                    pe.wait_ge(k_free, 3 * BPH * hf + 3 * BPH + 3)
                    pe.wait_ge(y_free, 3 * BPH * hf + 3 * BPH + 3)

            @block.scalar
            def _(act):
                act.sem_inc(tr_free, 2)
                act.sem_inc(saved, 1)
                act.sem_inc(w_free_f, 4)
                act.sem_inc(k_free, 3)
                act.sem_inc(y_free, 3)
                act.sem_inc(half_ready, 1)
                act.sem_inc(gate_out[0], 16)
                act.sem_inc(gate_out[1], 16)
                act.wait_ge(p_in, 16 * 16)
                st = Chain(act, act_p)
                st(act.activation(sm[0][:], lam[:, 2, :], ACT.Exp))
                act.wait_ge(trig, 1)
                st(act.activation(sm[1][:], sm[1][:], ACT.Exp))
                act.wait_ge(trig, 2)
                st(act.activation(sm[3][:], sm[2][:], ACT.Sin))
                st(act.activation(sm[4][:], sm[2][:], ACT.Sin, scale=0.5))
                for u in range(UNITS_U):
                    if u >= 2:
                        act.wait_ge(u_st[u % 2], 16 * (u // 2))
                    for b in range(NB):
                        act.wait_ge(S.proj_done, PROJ0 + 3 * u + b + 1)
                        nb = BW // SCH
                        act.activation(up[u % 2][:, :, b * nb:(b + 1) * nb],
                                       core.bank[3 * (u % 2) + b][:, 0:BW].rearrange("p (c s) -> p s c", s=SCH),
                                       ACT.Copy).then_inc(S.bank_free[u % 2], 1)
                for s in range(2):
                    act.wait_ge(u_st[s], 16 * UNITS_U // 2)
                with act.Fori(0, 2) as hf:
                    with act.Fori(0, BPH) as i:
                        n = BPH * hf + i
                        for x in range(4):
                            act.wait_ge(tr_mm, 4 * n + x + 1)
                            act.activation(win[:, 4 * x:4 * x + 4, :],
                                           core.bank[6 + x % 2][:].rearrange("p (a m) -> p a m", a=4),
                                           ACT.Copy).then_inc(tr_free, 1)
                        for g in range(GB):
                            act.wait_ge(w_mm, GB * n + g + 1)
                            act.activation(hs[H1, :, :, bass.ds(GB * i + g, 1)].rearrange("p c r a -> p r (c a)"),
                                           core.bank[g % 4][H1, 0:2 * NCH].rearrange("p (r c) -> p r c", r=2),
                                           ACT.Copy).then_inc(w_free_f, 1)

                    def gate_bank(x, it):
                        par, b = x // 3, x % 3
                        u = UNITS_U + UNITS_G // 2 * hf + 2 * it + par
                        if b == 0:
                            act.wait_ge(gate_out[par], 16 * (UNITS_G // 4 * hf + it) + 16)
                        act.wait_ge(S.proj_done, 3 * u + b + 1 + PROJ0)
                        act.activation(gate[par][:, b * BW:(b + 1) * BW], core.bank[x][:, 0:BW],
                                       ACT.Sigmoid).then_inc(S.bank_free[par], 1)
                        if b == 2:
                            act.wait_ge(S.bank_free[par], 3 * (UNITS_U // 2 + UNITS_G // 4 * hf + it + 1) + 3)
                            gm = UNITS_G // 2 * hf + 2 * it + par
                            act.dma_start(dram["gates"][bass.ds(gm, 1)].rearrange("a p t -> (a p) t"),
                                          gate[par]).then_inc(gate_out[par], 16)

                    with act.Fori(0, NCH // 24) as it:
                        for x in range(6):
                            for y in range(4):
                                k = 4 * x + y
                                m = NCH * hf + 24 * it + k
                                act.wait_ge(w_used, m + 1)
                                act.activation(hs[:, bass.ds(24 * it + k, 1), :, :].rearrange("p a r g -> p (a r) g"),
                                               cur[k % 2][:], ACT.Copy).then_inc(saved, 1)
                            gate_bank(x, it)
                    for par in range(2):
                        act.wait_ge(gate_out[par], 16 * (UNITS_G // 4) * (hf + 1) + 16)
                    act.wait_ge(saved, NCH * hf + NCH + 1)
                    act.sem_inc(turn, 1)
                    with act.Fori(0, BPH) as i:
                        n = BPH * hf + i
                        act.wait_ge(y_free, 3 * n + 3)
                        for r in range(2):
                            act.activation(hn[H1, r], hs[H1, :, r, bass.ds(GB * i, GB)].rearrange("p c g -> p g c"), ACT.Copy)
                            ins = act.activation(hn[H2, r, :, ::-1], hs[H2, :, r, bass.ds(GB * i, GB)].rearrange("p c g -> p g c"),
                                                 ACT.Copy)
                        ins.then_inc(hn_done, 1)
                        for x, gs in enumerate(((0, 3), (3, 6), (6, 8))):
                            act.wait_ge(k_mm, 3 * n + x + 1)
                            act.activation(kst[:, gs[0]:gs[1], :],
                                           core.bank[x][0:32, 0:(gs[1] - gs[0]) * KW].rearrange("p (g a) -> p g a", a=KW),
                                           ACT.Copy).then_inc(k_free, 1)
                        act.wait_ge(half_ready, n + 1)
                        for x, gs in enumerate(((0, 3), (3, 6), (6, 8))):
                            act.wait_ge(y_mm, 3 * n + x + 1)
                            act.activation(yb[:, gs[0]:gs[1], :],
                                           core.bank[3 + x][:, 0:(gs[1] - gs[0]) * NCH].rearrange("p (g c) -> p g c", c=NCH),
                                           ACT.Copy).then_inc(y_free, 1)
                    act.wait_ge(half_ready, BPH * hf + BPH + 1)

            @block.vector
            def _(dve):
                dve.sem_inc(w_free_b, 4)
                dve.sem_inc(u_free, 1)
                st = Chain(dve, ws_s)
                TT, TS_, STT = dve.tensor_tensor, dve.tensor_scalar, dve.scalar_tensor_tensor
                M, A_, SB = ALU.mult, ALU.add, ALU.subtract
                re, im = lam[:, 0, :], lam[:, 1, :]
                s_ = [x[:] for x in sm]
                for c in range(2):
                    st(dve.memset(bblk[c][:], 0.0))
                dve.wait_ge(p_in, 16 * 16)
                dve.wait_ge(act_p, 1)
                st(TT(s_[1], re, s_[0], M))
                dve.sem_inc(trig, 1)
                ROUND = 1.5 * 2.0 ** 23
                C1, C2 = 6.28125, 0.0019350051879882812
                C3 = 2 * np.pi - C1 - C2
                st(TT(s_[2], im, s_[0], M))
                st(TS_(s_[5], s_[2], 1 / (2 * np.pi), ROUND, M, A_))
                st(TS_(s_[5], s_[5], ROUND, None, SB))
                for cst in (C1, C2, C3):
                    st(STT(s_[2], s_[5], -float(cst), s_[2], M, A_))
                st(TS_(s_[2], s_[2], 3.1415925, -3.1415925, ALU.min, ALU.max))
                dve.sem_inc(trig, 1)
                dve.wait_ge(act_p, 4)
                st(TT(s_[4], s_[4], s_[4], M))
                st(TS_(s_[4], s_[4], -2.0, 1.0, M, A_))
                st(dve.memset(pw[0][:, 0, :], 1.0))
                st(dve.memset(pw[1][:, 0, :], 0.0))
                st(TT(pw[0][:, 1, :], s_[1], s_[4], M))
                st(TT(pw[1][:, 1, :], s_[1], s_[3], M))
                ar, ai = pw[0][:, 1, :], pw[1][:, 1, :]
                st(TT(s_[0], re, re, M))
                st(TT(s_[2], im, im, M))
                st(TT(s_[0], s_[0], s_[2], A_))
                st(dve.reciprocal(s_[0], s_[0]))
                st(TS_(s_[1], ar, 1.0, None, SB))
                st(TT(s_[2], s_[1], re, M))
                st(TT(s_[3], ai, im, M))
                st(TT(s_[2], s_[2], s_[3], A_))
                st(TT(s_[6], s_[2], s_[0], M))
                st(TT(s_[2], ai, re, M))
                st(TT(s_[3], s_[1], im, M))
                st(TT(s_[2], s_[2], s_[3], SB))
                st(TT(s_[7], s_[2], s_[0], M))
                NBB = GROUPS * S5I
                fr = s_[6].unsqueeze(2).to_broadcast([P, GROUPS, S5I])
                fi = s_[7].unsqueeze(2).to_broadcast([P, GROUPS, S5I])
                tv = [x[:, 0:NBB].rearrange("p (g i) -> p g i", i=S5I) for x in (tmp, work)]
                st(TT(tv[0], fi, bb[0][:], M))
                st(TT(tv[1], fi, bb[1][:], M))
                for c in range(2):
                    st(TT(bb[c][:], fr, bb[c][:], M))
                st(TT(bb[0][:], bb[0][:], tv[1], SB))
                st(TT(bb[1][:], bb[1][:], tv[0], A_))
                for base, lo, cnt in ((1, 1, 1), (2, 1, 2), (4, 1, 4)):
                    pr = pw[0][:, base:base + 1, :].to_broadcast([P, cnt, GROUPS])
                    pi = pw[1][:, base:base + 1, :].to_broadcast([P, cnt, GROUPS])
                    xr, xi = pw[0][:, lo:lo + cnt, :], pw[1][:, lo:lo + cnt, :]
                    orr, oi = pw[0][:, base + lo:base + lo + cnt, :], pw[1][:, base + lo:base + lo + cnt, :]
                    a = tmp[:, 0:cnt * GROUPS].rearrange("p (a g) -> p a g", g=GROUPS)
                    st(TT(orr, pr, xr, M))
                    st(TT(a, pi, xi, M))
                    st(TT(orr, orr, a, SB))
                    st(TT(oi, pr, xi, M))
                    st(TT(a, pi, xr, M))
                    st(TT(oi, oi, a, A_))
                for b in range(2):
                    st(dve.tensor_copy(coef[:, 0, b, :], pw[0][:, SCH, :]))
                st(TS_(coef[:, 1, 0, :], pw[1][:, SCH, :], -1.0, None, M))
                st(dve.tensor_copy(coef[:, 1, 1, :], pw[1][:, SCH, :]))
                PER_A, PER_S, PER_B = 18, 8, 19
                PER = (PER_A + PER_B) * BPH + PER_S
                with dve.Fori(0, 2) as hf:
                    with dve.Fori(0, BPH) as i:
                        n = BPH * hf + i
                        st = Chain(dve, dve_s, 1, hf * PER + i * PER_A)
                        gs = bass.ds(n * GB, GB)
                        for c in range(2):
                            st(move(dve, ws[c][H1, :, ::-1], pw[c][H1, 0:SCH, gs].rearrange("p l g -> p g l")))
                            st(move(dve, ws[c][H2], pw[c][H2, 0:SCH, gs].rearrange("p l g -> p g l")))
                        dve.wait_ge(y_free, 3 * BPH * hf + 3)
                        dve.wait_ge(tr_free, 4 * n + 2)
                        w4 = [v3(wt[c], SCH) for c in range(2)]
                        x4 = tmp[:, 0:NW].rearrange("p (g a i) -> p g a i", g=GB, a=SCH)
                        wsb = [ws[c][:].unsqueeze(3).to_broadcast([P, GB, SCH, S5I]) for c in range(2)]
                        bbb = [bb[c][:, gs, :].unsqueeze(2).to_broadcast([P, GB, SCH, S5I]) for c in range(2)]
                        st(TT(w4[0], wsb[0], bbb[0], M))
                        st(TT(x4, wsb[1], bbb[1], M))
                        st(TT(w4[0], w4[0], x4, SB))
                        st(TT(w4[1], wsb[0], bbb[1], M))
                        st(TT(x4, wsb[1], bbb[0], M))
                        st(TT(w4[1], w4[1], x4, A_))
                        dve.sem_inc(wt_done, 1)
                        for g in range(GB):
                            dve.wait_ge(w_mm, GB * n + g + 1)
                            st(move(
                                dve,
                                hs[H2, :, :, bass.ds(GB * i + g, 1)].rearrange("p c r a -> p r (c a)"),
                                core.bank[g % 4][H2, 0:2 * NCH].rearrange("p (r c) -> p r c", r=2)[:, :, ::-1]))
                            dve.sem_inc(w_free_b, 1)
                        assert st.n == PER_A, st.n
                    st = Chain(dve, dve_s, 1, hf * PER + BPH * PER_A)
                    dve.wait_ge(w_free_f, GB * BPH * (hf + 1) + 4)
                    gh = bass.ds(GH * hf, GH)
                    dve.wait_ge(saved, NCH * hf + 1)
                    st(dve.memset(cur[0][H1], 0.0))
                    st(move(dve, cur[0][H2], init[H2, :, gh]))
                    st(move(dve, cofs[0][:], coef[:, 0, :, gh]))
                    st(move(dve, cofs[1][:], coef[:, 1, :, gh]))

                    def steps(lo, cnt, it=None):
                        for k in range(lo, lo + cnt):
                            sl = 24 * it + k if it is not None else k
                            m = NCH * hf + sl
                            a, b = cur[k % 2], cur[1 - k % 2]
                            TT(t0[:], cofs[0][:], a[:], M).then_inc(prod, 1)
                            TT(t1[:], cofs[1][:], a[:, ::-1, :], M).then_inc(prod, 1)
                            dve.wait_ge(prod, 2 * m + 1)
                            src = hs[:, bass.ds(sl, 1), :, :].rearrange("p a r g -> p (a r) g") if it is not None else hs[:, sl, :, :]
                            TT(t0[:], t0[:], src, A_).then_inc(w_used, 1)
                            dve.wait_ge(prod, 2 * m + 2)
                            dve.wait_ge(w_used, m + 1)
                            dve.wait_ge(saved, m + 1)
                            TT(b[:], t0[:], t1[:], A_).then_inc(new, 1)
                            dve.wait_ge(new, m + 1)

                    steps(0, NCC)
                    st(move(dve, fins[H1, :, gh], cur[0][H1]))
                    st(move(dve, cur[0][H1], init[H1, :, gh]))
                    steps(NCC, 24 - NCC)
                    dve.sem_inc(turn, 1)
                    with dve.Fori(1, NCH // 24 - 1) as it:
                        steps(0, 24, it)
                    steps(120, NCS - 120)
                    st(dve.memset(cur[0][H2], 0.0))
                    steps(NCS, NCC)
                    st(move(dve, fins[H2, :, gh], cur[0][H2]))
                    dve.sem_inc(scan_done, 1)
                    assert st.n == PER_S, st.n
                    with dve.Fori(0, BPH) as i:
                        n = BPH * hf + i
                        st = Chain(dve, dve_s, 1, hf * PER + BPH * PER_A + PER_S + i * PER_B)
                        gs = bass.ds(n * GB, GB)
                        dve.wait_ge(y_free, 3 * n + 3)
                        for c in range(2):
                            st(move(dve, cq[c][H1], pw[c][H1, :, gs].rearrange("p l g -> p g l")))
                            st(move(dve, cq[c][H2, :, 0:1], pw[c][H2, 0:1, gs].rearrange("p l g -> p g l")))
                            st(move(dve, cq[c][H2, :, SCH:0:-1], pw[c][H2, 1:LAGS, gs].rearrange("p l g -> p g l")))
                            st(move(dve, bblk[c][H1, :, 0:S5I], bb[c][H1, gs, :]))
                            st(move(dve, bblk[c][H2, :, S5I:2 * S5I], bb[c][H2, gs, :]))
                            st(move(dve, bdup[c][:].rearrange("p g (a i) -> p g a i", a=2),
                                               bb[c][:, gs, :].unsqueeze(2).to_broadcast([P, GB, 2, S5I])))
                        c4 = [v3(ca[c], LAGS) for c in range(2)]
                        x4 = v3(tmp[:], LAGS)
                        cqb = [cq[c][:].unsqueeze(3).to_broadcast([P, GB, LAGS, S5I]) for c in range(2)]
                        ccb = [cc[c][:, gs, :].unsqueeze(2).to_broadcast([P, GB, LAGS, S5I]) for c in range(2)]
                        st(TT(c4[0], cqb[0], ccb[0], M))
                        st(TT(x4, cqb[1], ccb[1], M))
                        st(TT(c4[0], c4[0], x4, SB))
                        st(TT(c4[1], cqb[0], ccb[1], M))
                        st(TT(x4, cqb[1], ccb[0], M))
                        st(TT(c4[1], c4[1], x4, A_))
                        st(TS_(ca[1], ca[1], -1.0, None, M))
                        dve.sem_inc(ca_done, 1)
                        assert st.n == PER_B, st.n


def merge(core, mod, x1):
    nc, dram = core.nc, core.dram
    with ExitStack() as ctx:
        ctx.callback(core.end_stage)

        def sb(name, shape, dt=F32):
            return ctx.enter_context(nc.sbuf_tensor(name, shape, dt))

        def sem(name):
            return core.sem(name)

        USED0 = 9
        GLU, LRU, GLA_, S5_, OUT = range(5)
        ORDER = [list(range(8)), [8, 9, 10, 11, 0, 1, 2, 3, 4, 5, 6, 7], [8, 9, 10, 11, 0, 1, 2, 3],
                 [4, 5, 6, 7, 8, 9, 10, 11], list(range(8))]
        USED = [0, 64, 160, 224, 288]
        FILL = [0, 8, 20, 28, 36]
        UNIT = [0, 8, 24, 32, 40]
        S = Stream(core, ctx, "mrg")
        yhi = sb("yhi", [P, LBLK, T], F32R)
        ylo = sb("ylo", [P, LBLK, T], F32R)
        yin = [sb(f"yin{s}", [P, T]) for s in range(4)]
        gt = [sb(f"gt{s}", [P, T]) for s in range(2)]
        dvec = sb("dvec", [P, KD])
        (d_in, used, filled, hi_f, skip_done, nat_done, glu_done, mix_done, dve_s, merged_done) = (
            sem(n) for n in ("d_in", "used", "filled", "hi_f", "skip_done", "nat_done", "glu_done",
                             "mix_done", "dve_s", "merged_done"))
        yin_in = [sem(f"yin_in{s}") for s in range(4)]
        y_out = [sem(f"y_out{s}") for s in range(2)]
        gt_in = [sem(f"gt_in{s}") for s in range(2)]

        loads = []
        for ph, name, off in ((LRU, "y_lru", 1), (GLA_, "y_gla", 2), (S5_, "y_s5", 0)):
            for k, slot in enumerate(ORDER[ph]):
                tile = slot if ph == LRU else k
                loads.append((name, tile + off, slot))

        def last_use(ph, slot):
            k = len(ORDER[ph])
            return USED0 + USED[ph] + 7 * k + ORDER[ph].index(slot) + 1

        free_at = ([None] * 4 + [last_use(GLU, s) for s in range(8)] + [last_use(LRU, s) for s in (8, 9, 10, 11, 0, 1, 2, 3)]
                   + [last_use(LRU, s) for s in (4, 5, 6, 7)] + [last_use(GLA_, s) for s in (8, 9, 10, 11)])

        def issue(act, n):
            if n < len(loads):
                name, tile, _ = loads[n]
                act.dma_start(yin[n % 4][:], dram[name][tile]).then_inc(yin_in[n % 4], 16)

        def fill_act(act, n, src=None, slot=None, f=None):
            if src is None:
                _, _, slot = loads[n]
                f = n + 8
                if n:
                    act.wait_ge(filled, f)
                    issue(act, n + 3)
                act.wait_ge(yin_in[n % 4], 16 * (KD // 2 + n // 4 + 1))
                if free_at[n] is not None:
                    act.wait_ge(used, free_at[n])
                src = yin[n % 4][:]
            act.activation(yhi[:, slot, :], src, ACT.Copy).then_inc(hi_f, 1)

        def fill_dve(dve, n, src=None, slot=None, f=None):
            if src is None:
                _, _, slot = loads[n]
                f, src = n + 8, yin[n % 4][:]
            dve.wait_ge(hi_f, f + 1)
            dve.tensor_tensor(ylo[:, slot, :], src, yhi[:, slot, :].bitcast(F32), ALU.subtract).then_inc(filled, 1)

        with nc.Block() as block:
            @block.sync
            def _(sync):
                S.prime(sync)
                sync.sem_inc(used, USED0)
                sync.dma_start(dvec[:], dram["s5_dvec"]).then_inc(d_in, 16)
                with sync.Fori(0, 4) as i:
                    for j in range(2):
                        S.load(sync, 2 * i + j, j, dram["w_glu"][bass.ds(2 * i + j, 1)].rearrange("a p n -> (a p) n"))

                def tile_of(src, idx, q, par, mixed=None):
                    if mixed is None:
                        sync.wait_ge(S.bank_free[par], 3 * q + 3)
                    else:
                        sync.wait_ge(mix_done, mixed)
                    sync.dma_start(gt[par][:], dram[src][bass.ds(idx, 1)].rearrange("a p n -> (a p) n")).then_inc(gt_in[par], 16)

                for s in range(2):
                    sync.wait_ge(y_out[s], 16 * (KD // 2))
                with sync.Fori(0, 4) as i:
                    for j in range(2):
                        S.load(sync, UNIT[LRU] + 4 * i + 2 * j, 0, dram["w_br_lru"][bass.ds(2 * i + j, 1), :, 0:UW].rearrange("a p n -> (a p) n"))
                        S.load(sync, UNIT[LRU] + 4 * i + 2 * j + 1, 1, dram["w_br_lru"][bass.ds(2 * i + j, 1), :, UW:UW + 4 * P].rearrange("a p n -> (a p) n"), 4 * P)
                        tile_of("gates", 2 * KD + 2 * i + j, 4 + i, j)
                for ph, w, src, t0 in ((GLA_, "w_br_gla", "gates", 0), (S5_, "w_br_s5", "gates", KD), (OUT, "w_out", "x_res", 0)):
                    with sync.Fori(0, 4) as i:
                        for j in range(2):
                            S.load(sync, UNIT[ph] + 2 * i + j, j, dram[w][bass.ds(2 * i + j, 1)].rearrange("a p n -> (a p) n"))
                            tile_of(src, t0 + 2 * i + j, 4 * ph + i, j, None if ph != OUT else 2 * i + j + 1)

            @block.gpsimd
            def _(pool):
                def split(u, par, q, used_at, width=UW):
                    S.split(pool, u, par, q, None, width, (used, used_at + USED0))

                with pool.Fori(0, 4) as i:
                    for j in range(2):
                        split(2 * i + j, j, i, 16 * i + 8 * j - 8)
                with pool.Fori(0, 4) as i:
                    for j in range(2):
                        before = USED[LRU] + 24 * i + 12 * j
                        split(UNIT[LRU] + 4 * i + 2 * j, 0, 4 + 2 * i + j, before - 4)
                        split(UNIT[LRU] + 4 * i + 2 * j + 1, 1, 4 + 2 * i + j, before, 4 * P)
                for ph in (GLA_, S5_, OUT):
                    with pool.Fori(0, 4) as i:
                        for j in range(2):
                            extra = 4 if ph == GLA_ and j == 0 else 0
                            split(UNIT[ph] + 2 * i + j, j, UNIT[ph] // 2 + i, USED[ph] + 16 * i + 8 * j - 8 + extra)

            @block.tensor
            def _(pe):
                def tile_product(ph, i, j):
                    order = ORDER[ph]
                    pe.wait_ge(S.bank_free[j], 12 * ph + 3 * i + 3)
                    for k, slot in enumerate(order):
                        if ph == LRU:
                            u, par, kk = UNIT[ph] + 4 * i + 2 * j + k // 8, k // 8, k % 8
                        else:
                            u, par, kk = UNIT[ph] + 2 * i + j, j, k
                        if kk == 0:
                            pe.wait_ge(S.split_done, u + 3)
                        pe.wait_ge(filled, FILL[ph] + k + 1)
                        for b in range(NB):
                            out = core.bank[3 * j + b][:, 0:BW]
                            cols = slice(b * BW, (b + 1) * BW)
                            w = slice(kk * P, (kk + 1) * P)
                            for n, (wt, r) in enumerate(((S.hi, yhi), (S.hi, ylo), (S.lo, yhi))):
                                mm = pe.matmul(out, wt[par][:, w], r[:, slot, cols], start=(k == 0 and n == 0),
                                               stop=(k == len(order) - 1 and n == 2))
                        mm.then_inc(used, 1)

                for ph in range(5):
                    with pe.Fori(0, 4) as i:
                        for j in range(2):
                            tile_product(ph, i, j)

            @block.scalar
            def _(act):
                def issue_s5(k):
                    act.dma_start(yin[k % 2][:], dram["y_d"][k * P:(k + 1) * P].rearrange("p t c -> p (t c)")).then_inc(yin_in[k % 2], 16)
                    act.dma_start(yin[2 + k % 2][:], dram["u_d"][k * P:(k + 1) * P].rearrange("p t c -> p (t c)")).then_inc(yin_in[2 + k % 2], 16)

                issue_s5(0)
                issue_s5(1)
                for k in range(KD):
                    act.wait_ge(skip_done, k + 1)
                    if k >= 2:
                        act.wait_ge(filled, k - 1)
                    act.activation(gt[k % 2][:].rearrange("p (c t) -> p t c", t=SCH),
                                   yin[k % 2][:].rearrange("p (t c) -> p t c", t=SCH), ACT.Gelu_apprx_tanh).then_inc(nat_done, 1)
                    act.wait_ge(nat_done, k + 1)
                    if k + 2 < KD:
                        issue_s5(k + 2)
                    fill_act(act, None, gt[k % 2][:], k, k)
                for n in range(4):
                    if n < 2:
                        act.wait_ge(nat_done, KD)
                    issue(act, n)
                for m in range(KD):
                    if m < 2:
                        act.wait_ge(filled, KD)
                    else:
                        act.wait_ge(y_out[m % 2], 16 * (m // 2))
                    act.wait_ge(used, USED0 + USED[GLU] + 8 * (m + 1))
                    for b in range(NB):
                        act.activation(gt[m % 2][:, b * BW:(b + 1) * BW], core.bank[3 * (m % 2) + b][:, 0:BW],
                                       ACT.Sigmoid).then_inc(S.bank_free[m % 2], 1)
                    if m < 4:
                        fill_act(act, m)
                    act.wait_ge(glu_done, m + 1)
                    act.dma_start(dram["y_s5"][m], gt[m % 2][:]).then_inc(y_out[m % 2], 16)
                for n in range(4, 12):
                    fill_act(act, n)
                for n in range(12, 28):
                    fill_act(act, n)
                for m in range(KD):
                    act.wait_ge(merged_done, m + 1)
                    if m >= 4:
                        act.wait_ge(used, last_use(S5_, m))
                    fill_act(act, None, x1[:, m, :], m, FILL[OUT] + m)
                for m in range(KD):
                    act.wait_ge(used, USED0 + USED[OUT] + 8 * (m + 1))
                    if m >= 2:
                        act.wait_ge(mix_done, m + 1)
                    mt = yin[m % 2]
                    for b in range(NB):
                        bk = core.bank[3 * (m % 2) + b]
                        if b == 0:
                            act.activation(mt[:, 0:TC], bk[:, 0:TC], ACT.Identity, scale=mod[:, 2 * KD + m, 0:1])
                        c0 = TC if b == 0 else b * BW
                        act.activation(mt[:, c0:(b + 1) * BW], bk[:, c0 - b * BW:BW], ACT.Identity,
                                       scale=mod[:, 2 * KD + m, 1:2]).then_inc(S.bank_free[m % 2], 1)

            @block.vector
            def _(dve):
                st = Chain(dve, dve_s)
                dve.wait_ge(d_in, 16)
                for k in range(KD):
                    for s in (k % 2, 2 + k % 2):
                        dve.wait_ge(yin_in[s], 16 * (k // 2 + 1))
                    dve.scalar_tensor_tensor(yin[k % 2][:], yin[2 + k % 2][:], dvec[:, k:k + 1], yin[k % 2][:],
                                             ALU.mult, ALU.add).then_inc(skip_done, 1)
                    if k:
                        fill_dve(dve, None, gt[(k - 1) % 2][:], k - 1, k - 1)
                fill_dve(dve, None, gt[(KD - 1) % 2][:], KD - 1, KD - 1)
                for m in range(KD):
                    dve.wait_ge(S.bank_free[m % 2], 3 * (m // 2) + 6)
                    gm = gt[m % 2][:]
                    tmp = x1[:, m % 2, :]
                    st(dve.tensor_tensor(tmp, yhi[:, m, :].bitcast(F32), ylo[:, m, :].bitcast(F32), ALU.add))
                    dve.tensor_tensor(gm, gm, tmp, ALU.mult).then_inc(glu_done, 1)
                    dve.wait_ge(glu_done, m + 1)
                    if m < 4:
                        fill_dve(dve, m)
                for n in range(4, 12):
                    fill_dve(dve, n)

                def gated(ph, m):
                    k = len(ORDER[ph])
                    par = m % 2
                    dve.wait_ge(used, USED0 + USED[ph] + k * (m + 1))
                    dve.wait_ge(gt_in[par], 16 * (4 * (ph - 1) + m // 2 + 1))
                    for b in range(NB):
                        cols = slice(b * BW, (b + 1) * BW)
                        bk, dst, g = core.bank[3 * par + b][:, 0:BW], x1[:, m, cols], gt[par][:, cols]
                        if ph == LRU:
                            ins = dve.tensor_tensor(dst, bk, g, ALU.mult)
                            ins.then_inc(S.bank_free[par], 1)
                        else:
                            st(dve.tensor_tensor(g, bk, g, ALU.mult))
                            dve.tensor_tensor(dst, dst, g, ALU.add).then_inc(S.bank_free[par], 1)
                    dve.wait_ge(S.bank_free[par], 3 * (4 * ph + m // 2) + 6)
                    if ph == S5_:
                        dve.sem_inc(merged_done, 1)

                for m in range(KD):
                    if m == KD - 1:
                        for n in range(12, 20):
                            fill_dve(dve, n)
                    gated(LRU, m)
                for m in range(KD):
                    if m == KD - 1:
                        for n in range(24, 28):
                            fill_dve(dve, n)
                    gated(GLA_, m)
                    if m < 4:
                        fill_dve(dve, 20 + m)
                for m in range(KD):
                    gated(S5_, m)
                    if m >= KD - 2:
                        dve.sem_inc(mix_done, 1)
                    if m < 4:
                        fill_dve(dve, None, x1[:, m, :], m, FILL[OUT] + m)
                    if m == KD - 2:
                        for n in range(4, KD - 1):
                            fill_dve(dve, None, x1[:, n, :], n, FILL[OUT] + n)
                fill_dve(dve, None, x1[:, KD - 1, :], KD - 1, FILL[OUT] + KD - 1)
                for m in range(KD):
                    par = m % 2
                    dve.wait_ge(S.bank_free[par], 3 * (4 * OUT + m // 2) + 6)
                    dve.wait_ge(gt_in[par], 16 * (4 * (OUT - 1) + m // 2 + 1))
                    if m == 0:
                        dve.wait_ge(filled, FILL[OUT] + KD)
                    dve.scalar_tensor_tensor(x1[:, m, :], gt[par][:], ALPHA, yin[par][:], ALU.mult, ALU.add).then_inc(mix_done, 1)


def layer_norm(core, x, gain, bias, name, store=None):
    nc, dram = core.nc, core.dram
    with ExitStack() as ctx:
        ctx.callback(core.end_stage)

        def sb(n, shape, dt=F32):
            return ctx.enter_context(nc.sbuf_tensor(f"{name}_{n}", shape, dt))

        def sem(n):
            return core.sem(f"{name}_{n}")

        ones = sb("ones", [P, P])
        eps = sb("eps", [P, 1])
        g, be = sb("g", [P, KD]), sb("b", [P, KD])
        sq = [sb(f"sq{b}", [P, KD, BW]) for b in range(NB)]
        sd = [sb(f"sd{b}", [P, BW]) for b in range(NB)]
        const_done, g_in, mean_mm, cent_done, sq_done, var_mm, sd_done, dve_s, out_done, y_out = (
            sem(n) for n in ("const_done", "g_in", "mean_mm", "cent_done", "sq_done", "var_mm", "sd_done", "dve_s",
                             "out_done", "y_out"))
        with nc.Block() as block:
            @block.gpsimd
            def _(pool):
                pool.memset(ones[:], 1.0 / D).then_inc(const_done, 1)
                pool.memset(eps[:], LN_EPS).then_inc(const_done, 1)

            @block.sync
            def _(sync):
                sync.dma_start(g[:], dram[gain]).then_inc(g_in, 16)
                sync.dma_start(be[:], dram[bias]).then_inc(g_in, 16)
                if store is not None:
                    for b in range(NB):
                        sync.wait_ge(out_done, b + 1)
                        cols = slice(b * BW, (b + 1) * BW)
                        sync.dma_start(dram[store].rearrange("k p t -> p k t")[:, :, cols], x[:, :, cols]).then_inc(y_out, 16)
                    sync.wait_ge(y_out, 16 * NB)

            @block.tensor
            def _(pe):
                pe.wait_ge(const_done, 2)
                for b in range(NB):
                    for k in range(KD):
                        mm = pe.matmul(core.bank[b][:, 0:BW], ones[:], x[:, k, b * BW:(b + 1) * BW],
                                       start=(k == 0), stop=(k == KD - 1))
                    mm.then_inc(mean_mm, 1)
                for b in range(NB):
                    pe.wait_ge(sq_done, b + 1)
                    for k in range(KD):
                        mm = pe.matmul(core.bank[3 + b][:, 0:BW], ones[:], sq[b][:, k, :],
                                       start=(k == 0), stop=(k == KD - 1))
                    mm.then_inc(var_mm, 1)

            @block.scalar
            def _(act):
                act.wait_ge(const_done, 2)
                for b in range(NB):
                    act.wait_ge(cent_done, b + 1)
                    act.activation(sq[b][:], x[:, :, b * BW:(b + 1) * BW], ACT.Square).then_inc(sq_done, 1)
                for b in range(NB):
                    act.wait_ge(var_mm, b + 1)
                    act.activation(sd[b][:], core.bank[3 + b][:, 0:BW], ACT.Sqrt, bias=eps[:, 0:1]).then_inc(sd_done, 1)

            @block.vector
            def _(dve):
                st = Chain(dve, dve_s)
                for b in range(NB):
                    xb = x[:, :, b * BW:(b + 1) * BW]
                    dve.wait_ge(mean_mm, b + 1)
                    dve.tensor_tensor(xb, xb, core.bank[b][:, 0:BW].unsqueeze(1).to_broadcast([P, KD, BW]),
                                      ALU.subtract).then_inc(cent_done, 1)
                dve.wait_ge(g_in, 32)
                for b in range(NB):
                    xb = x[:, :, b * BW:(b + 1) * BW]
                    dve.wait_ge(sd_done, b + 1)
                    dve.wait_ge(sq_done, b + 1)
                    st(dve.reciprocal(sd[b][:], sd[b][:]))
                    st(dve.tensor_tensor(xb, xb, sd[b][:].unsqueeze(1).to_broadcast([P, KD, BW]), ALU.mult))
                    for k in range(KD):
                        st.mark(dve.tensor_scalar(x[:, k, b * BW:(b + 1) * BW], x[:, k, b * BW:(b + 1) * BW],
                                                  g[:, k:k + 1], be[:, k:k + 1], ALU.mult, ALU.add))
                    st.sync()
                    dve.sem_inc(out_done, 1)


def mlp(core, mod, x1):
    nc, dram = core.nc, core.dram
    with ExitStack() as ctx:
        ctx.callback(core.end_stage)

        def sb(name, shape, dt=F32):
            return ctx.enter_context(nc.sbuf_tensor(name, shape, dt))

        def sem(name):
            return core.sem(name)

        UG = 2 * HG
        GPG = NB * (HG + KD)
        S = Stream(core, ctx, "mlp")
        hhi = sb("h2hi", [P, KD, T], F32R)
        hlo = sb("h2lo", [P, KD, T], F32R)
        ahi = sb("ahi", [P, HG, T], F32R)
        alo = sb("alo", [P, HG, T], F32R)
        rl = [sb(f"rl{s}", [P, T]) for s in range(2)]
        sq = sb("mlp_sq", [P, BW])
        (h_done, hi_done, lo_done, scaled, ahi_done, alo_done, alo_free, dve_s) = (
            sem(n) for n in ("h_done", "hi_done", "lo_done", "scaled", "ahi_done", "alo_done", "alo_free", "mlp_dve"))

        out_free = [sem(f"out_free{s}") for s in range(2)]

        def cum(j):
            return NB * (j + 1) if j < HG else NB * HG + 2 * NB * (j - HG + 1)

        with nc.Block() as block:
            @block.sync
            def _(sync):
                S.prime(sync)
                sync.sem_inc(alo_free, 2 * NB)
                sync.sem_inc(out_free[0], NB)
                sync.sem_inc(out_free[1], NB)
                with sync.Fori(0, NHG) as i:
                    for j in range(UG):
                        u = UG * i + j
                        S.load(sync, u, j % 2, dram["mlp_units"][bass.ds(u, 1)].rearrange("a p n -> (a p) n"))

            @block.gpsimd
            def _(pool):
                with pool.Fori(0, NHG) as i:
                    for j in range(UG):
                        before = cum(j - 2) if j >= 2 else (cum(UG + j - 2) - GPG)
                        S.split(pool, UG * i + j, j % 2, UG // 2 * i + j // 2, GPG * i + before)

            @block.tensor
            def _(pe):
                pe.wait_ge(lo_done, KD)
                with pe.Fori(0, NHG) as i:
                    for j in range(HG):
                        free = (out_free[j], NB * KD // 2 * i) if j < 2 else (S.bank_free[j % 2], 3 + NB * HG // 2 * i)
                        S.project(pe, UG * i + j, j % 2, None, hhi, hlo, free=free)
                    for j in range(HG, UG):
                        pe.wait_ge(S.split_done, UG * i + j + 3)
                        for e in range(2):
                            m = 2 * (j - HG) + e
                            if m < 2:
                                pe.wait_ge(S.bank_free[e], 3 + NB * HG // 2 * (i + 1))
                            else:
                                pe.wait_ge(out_free[e], NB * KD // 2 * i + NB * (m // 2) + NB)
                            for k in range(HG):
                                if m == 0:
                                    pe.wait_ge(alo_done, NB * HG * i + NB * (k + 1))
                                w = slice((HG * e + k) * P, (HG * e + k + 1) * P)
                                for b in range(NB):
                                    out = core.bank[3 * e + b][:, 0:BW]
                                    cols = slice(b * BW, (b + 1) * BW)
                                    for n, (wt, r) in enumerate(((S.hi, ahi), (S.hi, alo), (S.lo, ahi))):
                                        mm = pe.matmul(out, wt[j % 2][:, w], r[:, k, cols], start=(k == 0 and n == 0),
                                                       stop=(k == HG - 1 and n == 2))
                                    if k == HG - 1:
                                        mm.then_inc(S.proj_done, 1)

            @block.scalar
            def _(act):
                for k in range(KD):
                    act.wait_ge(h_done, k + 1)
                    act.activation(hhi[:, k, :], rl[k % 2][:], ACT.Copy).then_inc(hi_done, 1)
                act.wait_ge(lo_done, KD)
                with act.Fori(0, NHG) as i:
                    for j in range(HG):
                        for b in range(NB):
                            cols = slice(b * BW, (b + 1) * BW)
                            act.wait_ge(S.proj_done, GPG * i + NB * j + b + 1 + PROJ0)
                            act.wait_ge(alo_free, NB * HG * i + NB * j + b + 1)
                            act.activation(rl[j % 2][:, cols], core.bank[3 * (j % 2) + b][:, 0:BW], ACT.Relu).then_inc(S.bank_free[j % 2], 1)
                            act.wait_ge(S.bank_free[j % 2], 3 + NB * (HG // 2 * i + j // 2) + b + 1)
                            act.activation(ahi[:, j, cols], rl[j % 2][:, cols], ACT.Square).then_inc(ahi_done, 1)

            @block.vector
            def _(dve):
                for k in range(KD):
                    if k >= 2:
                        dve.wait_ge(lo_done, k - 1)
                    for c, cols in ((0, slice(0, TC)), (1, slice(TC, T))):
                        ins = dve.tensor_scalar(rl[k % 2][:, cols], x1[:, k, cols], mod[:, 4 * KD + k, c:c + 1],
                                                mod[:, 3 * KD + k, c:c + 1], ALU.mult, ALU.add)
                    ins.then_inc(h_done, 1)
                    dve.wait_ge(hi_done, k + 1)
                    dve.tensor_tensor(hlo[:, k, :], rl[k % 2][:], hhi[:, k, :].bitcast(F32), ALU.subtract).then_inc(lo_done, 1)
                for k in range(KD):
                    dve.tensor_scalar(x1[:, k, :], x1[:, k, :], ALPHA, None, ALU.mult).then_inc(scaled, 1)
                dve.wait_ge(scaled, KD)
                PER = NB * HG
                with dve.Fori(0, NHG) as i:
                    st = Chain(dve, dve_s, i, PER)
                    for j in range(HG):
                        for b in range(NB):
                            cols = slice(b * BW, (b + 1) * BW)
                            dve.wait_ge(ahi_done, PER * i + NB * j + b + 1)
                            st(dve.tensor_tensor(sq[:], rl[j % 2][:, cols], rl[j % 2][:, cols], ALU.mult))
                            dve.tensor_tensor(alo[:, j, cols], sq[:], ahi[:, j, cols].bitcast(F32),
                                              ALU.subtract).then_inc(alo_done, 1)
                            dve.wait_ge(alo_done, PER * i + NB * j + b + 1)
                            dve.sem_inc(alo_free, 1)
                    st.end()
                    for m in range(KD):
                        par = m % 2
                        for b in range(NB):
                            bk = core.bank[3 * par + b]
                            dve.wait_ge(S.proj_done, GPG * i + NB * HG + NB * m + b + 1 + PROJ0)
                            c0 = b * BW
                            if b == 0:
                                dve.scalar_tensor_tensor(x1[:, m, 0:TC], bk[:, 0:TC], mod[:, 5 * KD + m, 0:1], x1[:, m, 0:TC],
                                                         ALU.mult, ALU.add)
                                c0 = TC
                            dve.scalar_tensor_tensor(x1[:, m, c0:(b + 1) * BW], bk[:, c0 - b * BW:BW],
                                                     mod[:, 5 * KD + m, 1:2], x1[:, m, c0:(b + 1) * BW],
                                                     ALU.mult, ALU.add).then_inc(out_free[par], 1)


def build(nc, dram):
    with ExitStack() as ctx:
        core = Core(nc, ctx, dram)
        mod = ctx.enter_context(nc.sbuf_tensor("mod", [P, 6 * KD, 2], F32))
        with ExitStack() as hctx:
            hhi = hctx.enter_context(nc.sbuf_tensor("hhi", [P, KD, T], F32R))
            hlo = hctx.enter_context(nc.sbuf_tensor("hlo", [P, KD, T], F32R))
            modulate(core, hhi, hlo, mod)
            lru(core, hhi, hlo)
            gla(core, hhi, hlo)
            s5_and_gates(core, hhi, hlo)
        x1 = ctx.enter_context(nc.sbuf_tensor("x1", [P, KD, T], F32))
        merge(core, mod, x1)
        layer_norm(core, x1, "ln1_g", "ln1_b", "ln1")
        mlp(core, mod, x1)
        layer_norm(core, x1, "ln2_g", "ln2_b", "ln2", store="y")


def units(w, tiles):
    k, m = w.shape
    return np.ascontiguousarray(w.reshape(k // P, P, m // P, P).transpose(2, 1, 0, 3)).reshape(m // P, P, k)[tiles]


def tables():
    quarter = D // 4
    omega = 1.0 / (np.float32(10000.0) ** (np.arange(quarter, dtype=np.float32) / np.float32(quarter)))
    omega = omega.astype(np.float32)

    def table(n):
        a = (np.arange(n, dtype=np.float32)[:, None] * omega).astype(np.float32)
        t = np.concatenate([np.sin(a), np.cos(a)], axis=1).astype(np.float32)
        return np.ascontiguousarray(t.T.reshape(KD // 2, P, n).transpose(1, 0, 2))

    s, t = np.arange(P)[:, None], np.arange(P)[None, :]
    same = s // GCH == t // GCH
    keep = np.stack([same & (s <= t), same & (s >= t)], axis=1).astype(np.int32)
    return {"pos_r": table(ROWS), "pos_c": table(GRID_W), "keep": keep, "ident": np.eye(P, dtype=np.float32)}


def layout(a):
    f = {n: np.asarray(v) for n, v in a.items()}
    cols = np.cumsum((0, 512, 512, 1024, 1024, 32, 1024, 1536, 1536, 3072))
    w_in = f["w_in"][0]
    part = [w_in[:, cols[n]:cols[n + 1]] for n in range(9)]
    q, k, v, r, glr, u, lx, ly, gates = part
    out = tables()
    out["cvec"] = np.ascontiguousarray(np.stack([f["c_ctx"], f["c"][0]], axis=1).reshape(KD, P, 2).transpose(1, 0, 2))
    out["bada"] = np.ascontiguousarray(f["b_ada"][0].reshape(6 * KD, P).T)
    out["w_ada"] = units(f["w_ada"][0], slice(None))
    x = np.concatenate([f["x_prompt"][0], f["x_sample"][0]], axis=0)
    out["x_t"] = np.ascontiguousarray(x.T).reshape(KD, P, T)
    ulx, uly, ug = units(lx, slice(None)), units(ly, slice(None)), units(gates, slice(None))
    out["lru_units"] = np.stack([ulx, uly], axis=1).reshape(2 * LBLK, P, UW)
    wa, wi = f["lru_w_a"][0], f["lru_w_i"][0]
    out["lru_w"] = np.ascontiguousarray(np.stack([wa[0], wi[0], wa[1], wi[1]], axis=1).transpose(0, 2, 1, 3)).reshape(LBLK, P, 4 * P)

    def rows(m):
        return m.reshape(-1, LBLK, P)

    prm = np.concatenate([rows(f["lru_conv_w"][0]), rows(f["lru_conv_b"][0]), rows(f["lru_b_a"][0]),
                          rows(f["lru_b_i"][0]), rows(f["lru_lam"][0]), rows(f["state_lru"][0, 0])], axis=0)
    out["lru_params"] = np.ascontiguousarray(prm.transpose(2, 1, 0))
    pad = np.zeros((D, P), np.float32)
    pad[:, 0:RANK], pad[:, 32:32 + RANK] = glr[:, 0:RANK], glr[:, RANK:]
    uq, uk, uv, ur = (units(m, slice(None)) for m in (q, k, v, r))
    out["gla_units"] = np.concatenate([units(pad, slice(None))] + [
        np.stack([uq[h], uk[h], uv[2 * h], uv[2 * h + 1], ur[2 * h], ur[2 * h + 1]]) for h in range(HEADS)])
    wgate = np.zeros((64, HEADS, DK), np.float32)
    for e in range(2):
        wgate[32 * e:32 * e + RANK] = f["gla_w_gate"][0, e].reshape(RANK, HEADS, DK)
    out["gla_wgate"] = wgate
    prm = np.concatenate([f["gla_b_gate"][0].reshape(2, HEADS, P),
                          f["gla_norm_g"][0].reshape(HEADS, 2, P).transpose(1, 0, 2)], axis=0)
    out["gla_params"] = np.ascontiguousarray(prm.transpose(2, 1, 0))
    out["s5_units"] = np.concatenate([units(u, slice(None)), ug])
    out["s5_lam"] = np.ascontiguousarray(np.stack([f["s5_lam_re"][0], f["s5_lam_im"][0]]).transpose(0, 1, 3, 2)).reshape(2, P, GROUPS)
    out["s5_step"] = f["s5_log_step"][0]
    out["s5_b"] = np.ascontiguousarray(np.stack([f["s5_b_re"][0], f["s5_b_im"][0]]).transpose(0, 2, 1, 3))
    out["s5_c"] = np.ascontiguousarray(np.stack([f["s5_c_re"][0], f["s5_c_im"][0]]).transpose(0, 3, 1, 2))
    st = np.stack([f["state_s5_re"][0, 0], f["state_s5_im"][0, 0]])
    out["s5_init"] = np.ascontiguousarray(st.transpose(1, 3, 0, 2)).reshape(P, 2, GROUPS)
    order = [LBLK - HG + k for k in range(HG)] + list(range(LBLK - HG))
    w = f["w_br_lru"][0].reshape(LBLK, P, D)[order].reshape(LBLK * P, D)
    out["w_br_lru"] = units(w, slice(None))
    for name in ("w_br_gla", "w_br_s5", "w_out"):
        out[name] = units(f[name][0], slice(None))
    out["w_glu"] = units(f["s5_w_glu"][0], slice(None))

    def columns(vec):
        return np.ascontiguousarray(vec.reshape(KD, P).T)

    out["s5_dvec"] = columns(f["s5_d"][0])
    for name in ("ln1_g", "ln1_b", "ln2_g", "ln2_b"):
        out[name] = columns(f[name][0])
    win = units(f["w_mlp_in"][0], slice(None)).reshape(NHG, HG, P, UW)
    wout = f["w_mlp_out"][0].reshape(NHG, HG, P, KD, P).transpose(0, 3, 2, 1, 4).reshape(NHG, KD // 2, 2, P, HG * P)
    wout = wout.transpose(0, 1, 3, 2, 4).reshape(NHG, HG, P, UW)
    out["mlp_units"] = np.concatenate([win, wout], axis=1).reshape(NHG * 2 * HG, P, UW)
    out["state_gla"] = f["state_gla"][0, 0].reshape(2 * HEADS, DK, DV)
    return out


SCRATCH = {"x_res": (KD, P, T), "gates": (3 * KD, P, T), "y_lru": (LBLK + 1, P, T), "y_gla": (KD + 2, P, T), "y_s5": (KD, P, T),
           "u_d": (D, SCH, NCH), "y_d": (D, SCH, NCH), "kd": (GROUPS, S5I, 2 * SCH - 1, S5I)}
OUTPUTS = {"new_lru": (P, 2, LBLK), "new_gla": (2 * HEADS, DK, DV), "new_s5": (P, 2, GROUPS), "y": (KD, P, T)}


def kernel(**inputs):
    import concourse.bacc as bacc
    from concourse.bass_utils import run_bass_kernel_spmd

    nc = bacc.Bacc("TRN2", target_bir_lowering=False, num_devices=1)
    arrays, dram = {}, {}
    for name, a in layout(inputs).items():
        arrays[f"in_{name}"] = a
        dram[name] = nc.dram_tensor(f"in_{name}", a.shape, mybir.dt.from_np(a.dtype), kind="ExternalInput").ap()
    for name, shape in SCRATCH.items():
        dram[name] = nc.dram_tensor(f"mid_{name}", shape, F32, kind="Internal").ap()
    for name, shape in OUTPUTS.items():
        dram[name] = nc.dram_tensor(f"out_{name}", shape, F32, kind="ExternalOutput").ap()
    build(nc, dram)
    got = run_bass_kernel_spmd(nc, [arrays], core_ids=[0]).results[0]
    y = np.ascontiguousarray(got["out_y"].reshape(D, T).T)
    s5 = got["out_new_s5"].reshape(2, S5P, 2, GROUPS).transpose(2, 0, 3, 1)[:, None, None]
    return (y[None, 0:TC], y[None, TC:], got["out_new_gla"].reshape(1, 1, 2, HEADS, DK, DV),
            np.ascontiguousarray(s5[0]), np.ascontiguousarray(s5[1]),
            np.ascontiguousarray(got["out_new_lru"].transpose(1, 2, 0)).reshape(1, 1, 2, LBLK * P))
```

```python
from contextlib import ExitStack

import numpy as np

import concourse.bass as bass
from concourse import mybir

F32 = mybir.dt.float32
F32R = mybir.dt.float32r
I32 = mybir.dt.int32

ALU = mybir.AluOpType
ACT = mybir.ActivationFunctionType

P = 128
D = 1024
KD = D // P
TC = 128
TS = 1024
T = TC + TS
NB = 3
BW = T // NB
GRID_W = 64
ROWS = TS // GRID_W
ALPHA = 2.0 ** 0.25
LN_EPS = 1e-5
HEADS = 4
DK = 128
DV = 256
RANK = 16
GLA_TAU = 16.0
GCH = 64
NPAIR = T // P
LBLK = 12
CONV = 4
LRU_C = 8.0
NMOD1 = 2 * KD
LXW = T + 6
LXC = 2
LXS = TC + 5
XCW = LXW - CONV + 1
XCS = LXS - LXC
GROUPS = 64
S5P = 64
S5I = 16
SCH = 8
NCH = T // SCH
NCC = TC // SCH
NCS = TS // SCH
GB = 8
NBATCH = GROUPS // GB
HID = 4 * D
HG = 4
NHG = HID // P // HG

UW = 1024
PROJ0 = 7
(PC_W, PC_B, PC_BA, PC_BI, PC_C, PC_H0, PC_NEG, PC_NEG2) = (0, 4, 5, 7, 9, 11, 13, 15)
NPC = 17


class Chain:

    def __init__(self, eng, sem, i=0, per=0):
        self.eng, self.sem, self.base, self.per, self.n = eng, sem, i * per, per, 0

    def mark(self, ins):
        ins.then_inc(self.sem, 1)
        self.n += 1

    def sync(self):
        self.eng.wait_ge(self.sem, self.base + self.n)

    def __call__(self, ins):
        self.mark(ins)
        self.sync()

    def end(self):
        assert self.n == self.per, (self.n, self.per)


def move(dve, out, in_):
    return dve.tensor_scalar(out, in_, 1.0, None, ALU.mult)


def rev(ap):
    return ap[:, ::-1]


class Core:

    def __init__(self, nc, ctx, dram):
        self.nc, self.ctx, self.dram = nc, ctx, dram
        self.zero = ctx.enter_context(nc.sbuf_tensor("zero", [P, 1], F32))[:, 0:1]
        self.bank = [ctx.enter_context(nc.psum_tensor(f"bank{i}", [P, 512], F32)) for i in range(8)]
        self.stage, self.sems = 1, []

    def sem(self, name):
        self.sems.append(self.nc.alloc_semaphore(name=f"stage{self.stage}_{name}"))
        return self.sems[-1]

    def end_stage(self):
        self.nc.clear_and_free_semaphores(self.sems)
        self.nc.all_engine_barrier()
        self.stage, self.sems = self.stage + 1, []


class Stream:

    def __init__(self, core, ctx, name, raw_width=UW):
        nc = core.nc
        self.core = core
        self.memory = ctx.enter_context(nc.sbuf_tensor(f"{name}_raw", [P, 2 * raw_width], F32))
        self.raw = [self.memory[:, s * raw_width:s * raw_width + UW] for s in range(2)]
        self.hi = [ctx.enter_context(nc.sbuf_tensor(f"{name}_hi{s}", [P, UW], F32R)) for s in range(2)]
        self.lo = [ctx.enter_context(nc.sbuf_tensor(f"{name}_lo{s}", [P, UW], F32R)) for s in range(2)]
        self.raw_in = [core.sem(f"{name}_raw_in{s}") for s in range(2)]
        self.hi_done = core.sem(f"{name}_hi_done")
        self.split_done = core.sem(f"{name}_split_done")
        self.proj_done = core.sem(f"{name}_proj_done")
        self.bank_free = [core.sem(f"{name}_bank_free{s}") for s in range(2)]

    def prime(self, sync):
        sync.sem_inc(self.split_done, 2)
        sync.sem_inc(self.proj_done, PROJ0)
        sync.sem_inc(self.bank_free[0], 3)
        sync.sem_inc(self.bank_free[1], 3)

    def load(self, sync, u, par, src, width=UW):
        sync.wait_ge(self.split_done, u + 1)
        sync.dma_start(self.raw[par][:, 0:width], src).then_inc(self.raw_in[par], 16)

    def split(self, pool, u, par, q, groups_before, width=UW, used=None):
        pool.wait_ge(self.raw_in[par], 16 * q + 16)
        if used is None:
            pool.wait_ge(self.proj_done, groups_before + PROJ0)
        else:
            pool.wait_ge(used[0], used[1])
        w = slice(0, width)
        pool.tensor_tensor(self.hi[par][:, w], self.raw[par][:, w], self.core.zero.to_broadcast([P, width]),
                           ALU.add).then_inc(self.hi_done, 1)
        pool.wait_ge(self.hi_done, u + 1)
        pool.tensor_tensor(self.lo[par][:, w], self.raw[par][:, w], self.hi[par][:, w].bitcast(F32),
                           ALU.subtract).then_inc(self.split_done, 1)

    def project(self, pe, u, par, q, rhi, rlo, set_=None, nk=KD, k0=0, wait_split=True, start=True, stop=True,
                free=None):
        set_ = par if set_ is None else set_
        if wait_split:
            pe.wait_ge(self.split_done, u + 3)
        for b in range(NB):
            if start:
                sem, base = free or (self.bank_free[set_], 3 * q)
                pe.wait_ge(sem, base + b + 1)
            out = self.core.bank[3 * set_ + b][:, 0:BW]
            cols = slice(b * BW, (b + 1) * BW)
            for k in range(nk):
                w = slice((k0 + k) * P, (k0 + k + 1) * P)
                for n, (wt, r) in enumerate(((self.hi, rhi), (self.hi, rlo), (self.lo, rhi))):
                    mm = pe.matmul(out, wt[par][:, w], r[:, k, cols],
                                   start=(start and k == 0 and n == 0), stop=(stop and k == nk - 1 and n == 2))
            mm.then_inc(self.proj_done, 1)


def modulate(core, hhi, hlo, mod, csilu):
    nc, dram = core.nc, core.dram
    with ExitStack() as ctx:
        ctx.callback(core.end_stage)

        def sb(name, shape, dt=F32):
            return ctx.enter_context(nc.sbuf_tensor(name, shape, dt))

        def sem(name):
            return core.sem(name)

        NSLOT = 8
        NADA = NMOD1
        ada = [sb(f"ada{s}", [P, UW]) for s in range(NSLOT)]
        x = sb("x", [P, KD, T])
        h = [sb(f"h{s}", [P, T]) for s in range(2)]
        cvec = sb("cvec", [P, KD, 2])
        bada = sb("bada", [P, 6 * KD])
        pos_r = sb("pos_r", [P, KD // 2, ROWS])
        pos_c = sb("pos_c", [P, KD // 2, GRID_W])
        small_in, x_in, silu_done, mod_mm, pos_done = (
            sem(n) for n in ("small_in", "x_in", "silu_done", "mod_mm", "pos_done"))
        ada_in = [sem(f"ada_in{s}") for s in range(NSLOT)]
        dve_step, h_done, hi_done, lo_done, xres_out = (
            sem(n) for n in ("dve_step", "h_done", "hi_done", "lo_done", "xres_out"))

        with nc.Block() as block:
            @block.sync
            def _(sync):
                sync.dma_start(cvec[:], dram["cvec"]).then_inc(small_in, 16)
                sync.dma_start(bada[:], dram["bada"]).then_inc(small_in, 16)
                sync.dma_start(pos_r[:], dram["pos_r"]).then_inc(small_in, 16)
                sync.dma_start(pos_c[:], dram["pos_c"]).then_inc(small_in, 16)
                for m in range(NADA):
                    if m >= NSLOT:
                        sync.wait_ge(mod_mm, m - NSLOT + 1)
                    sync.dma_start(ada[m % NSLOT][:], dram["w_ada"][m]).then_inc(ada_in[m % NSLOT], 16)
                sync.dma_start(x[:], dram["x_t"].rearrange("k p t -> p k t")).then_inc(x_in, 16)
                sync.wait_ge(pos_done, KD)
                sync.dma_start(dram["x_res"].rearrange("k p t -> p k t"), x[:]).then_inc(xres_out, 16)
                sync.wait_ge(xres_out, 16)

            @block.gpsimd
            def _(pool):
                pool.memset(core.zero, 0.0)

            @block.tensor
            def _(pe):
                pe.wait_ge(silu_done, 1)
                for m in range(NADA):
                    pe.wait_ge(ada_in[m % NSLOT], 16 * (m // NSLOT + 1))
                    for k in range(KD):
                        mm = pe.matmul(core.bank[0][:, 2 * m:2 * m + 2], ada[m % NSLOT][:, k * P:(k + 1) * P],
                                       csilu[:, k, :], start=(k == 0), stop=(k == KD - 1))
                    mm.then_inc(mod_mm, 1)

            @block.scalar
            def _(act):
                act.wait_ge(small_in, 64)
                act.activation(csilu[:], cvec[:], ACT.Silu).then_inc(silu_done, 1)
                for k in range(KD):
                    act.wait_ge(h_done, k + 1)
                    act.activation(hhi[:, k, :], h[k % 2][:], ACT.Copy).then_inc(hi_done, 1)

            @block.vector
            def _(dve):
                step = Chain(dve, dve_step)
                dve.wait_ge(small_in, 64)
                dve.wait_ge(x_in, 16)
                for k in range(KD):
                    xs = x[:, k, TC:].rearrange("p (r c) -> p r c", c=GRID_W)
                    if k < KD // 2:
                        tab = pos_r[:, k, :].unsqueeze(2).to_broadcast([P, ROWS, GRID_W])
                    else:
                        tab = pos_c[:, k - KD // 2, :].unsqueeze(1).to_broadcast([P, ROWS, GRID_W])
                    dve.tensor_tensor(xs, xs, tab, ALU.add).then_inc(pos_done, 1)

                def take(bank, lo, hi):
                    dve.wait_ge(mod_mm, hi)
                    step(dve.tensor_tensor(
                        mod[:, lo:hi, :], core.bank[bank][:, 2 * lo:2 * hi].rearrange("p (m c) -> p m c", c=2),
                        bada[:, lo:hi].unsqueeze(2).to_broadcast([P, hi - lo, 2]), ALU.add))

                take(0, 0, 2 * KD)
                step(dve.tensor_scalar(mod[:, KD:2 * KD, :], mod[:, KD:2 * KD, :], 1.0, None, ALU.add))
                dve.wait_ge(pos_done, KD)
                for k in range(KD + 1):
                    if k < KD:
                        if k >= 2:
                            dve.wait_ge(lo_done, k - 1)
                        for c, cols in ((0, slice(0, TC)), (1, slice(TC, T))):
                            ins = dve.tensor_scalar(h[k % 2][:, cols], x[:, k, cols], mod[:, KD + k, c:c + 1],
                                                    mod[:, k, c:c + 1], ALU.mult, ALU.add)
                        ins.then_inc(h_done, 1)
                    if k:
                        dve.wait_ge(hi_done, k)
                        dve.tensor_tensor(hlo[:, k - 1, :], h[(k - 1) % 2][:], hhi[:, k - 1, :].bitcast(F32),
                                          ALU.subtract).then_inc(lo_done, 1)


def lru(core, hhi, hlo):
    nc, dram = core.nc, core.dram
    with ExitStack() as ctx:
        ctx.callback(core.end_stage)

        def sb(name, shape, dt=F32):
            return ctx.enter_context(nc.sbuf_tensor(name, shape, dt))

        def sem(name):
            return core.sem(name)

        S = Stream(core, ctx, "lru")
        lw_raw = sb("lw_raw", [P, 4 * P])
        lw_hi = sb("lw_hi", [P, 4 * P], F32R)
        lw_lo = sb("lw_lo", [P, 4 * P], F32R)
        params = sb("lru_params", [P, LBLK, NPC])
        prms = [sb(f"lru_prm{s}", [P, NPC]) for s in range(2)]
        z = sb("lru_z", [P, LBLK, 2])
        s1 = sb("lru_s1", [P, LBLK, 2])
        s2 = sb("lru_s2", [P, LBLK, 2])
        acc = sb("lru_acc", [P, LBLK, 2])
        tiny = sb("lru_tiny", [P, 1])
        lx = sb("lx", [P, LXW])
        ly = [sb(f"ly{s}", [P, T]) for s in range(2)]
        xc = [sb(f"xc{s}", [P, XCW]) for s in range(2)]
        xc_hi = sb("xc_hi", [P, T], F32R)
        xc_lo = sb("xc_lo", [P, T], F32R)
        rt = [sb(f"rt{d}", [P, T]) for d in range(2)]
        it = [sb(f"it{d}", [P, T]) for d in range(2)]
        at = [sb(f"at{d}", [P, T]) for d in range(2)]
        ht = [sb(f"ht{d}", [P, T]) for d in range(2)]
        y = sb("lru_y", [P, T])
        fin = sb("lru_fin", [P, 2, LBLK])
        (params_in, head_s, front_s, tail_s, act_s, lw_in, lw_hi_done, lw_done, conv_done, xh_done, xl_done,
         lru_mm, lbank_free, s_done, f_done, b_done, dir_done, y_done, y_out, fin_out, zero_done, z_done, c_done) = (
            sem(n) for n in (
                "params_in", "head_s", "front_s", "tail_s", "act_s", "lw_in", "lw_hi_done", "lw_done",
                "conv_done", "xh_done", "xl_done", "lru_mm", "lbank_free", "s_done", "f_done", "b_done", "dir_done", "y_done",
                "y_out", "fin_out", "zero_done", "z_done", "c_done"))
        with nc.Block() as block:
            @block.sync
            def _(sync):
                S.prime(sync)
                sync.sem_inc(lw_done, 1)
                sync.sem_inc(lru_mm, 2)
                sync.dma_start(params[:, :, 0:PC_NEG], dram["lru_params"]).then_inc(params_in, 16)

                def loads(i):
                    S.load(sync, 2 * i, 0, dram["lru_units"][bass.ds(2 * i, 1)].rearrange("a p n -> (a p) n"))
                    sync.wait_ge(lw_done, i + 1)
                    sync.dma_start(lw_raw[:], dram["lru_w"][bass.ds(i, 1)].rearrange("a p n -> (a p) n")).then_inc(lw_in, 16)
                    S.load(sync, 2 * i + 1, 1, dram["lru_units"][bass.ds(2 * i + 1, 1)].rearrange("a p n -> (a p) n"))

                with sync.Fori(0, LBLK) as i:
                    loads(i)
                sync.wait_ge(y_done, LBLK + 1)
                sync.dma_start(dram["new_lru"], fin[:]).then_inc(fin_out, 16)
                sync.wait_ge(fin_out, 16)

            @block.gpsimd
            def _(pool):
                pool.memset(lx[:], 0.0).then_inc(zero_done, 1)
                pool.memset(tiny[:], 1e-30).then_inc(zero_done, 1)
                with pool.Fori(0, LBLK) as i:
                    for j in range(2):
                        S.split(pool, 2 * i + j, j, i, 3 * (2 * i + j) - 3)
                    pool.wait_ge(lw_in, 16 * i + 16)
                    pool.wait_ge(lru_mm, 12 * i + 2)
                    pool.tensor_tensor(lw_hi[:], lw_raw[:], core.zero.to_broadcast([P, 4 * P]),
                                       ALU.add).then_inc(lw_hi_done, 1)
                    pool.wait_ge(lw_hi_done, i + 1)
                    pool.tensor_tensor(lw_lo[:], lw_raw[:], lw_hi[:].bitcast(F32),
                                       ALU.subtract).then_inc(lw_done, 1)

            @block.tensor
            def _(pe):
                def products(i):
                    for j in range(2):
                        S.project(pe, 2 * i + j, j, i, hhi, hlo)
                    pe.wait_ge(lw_done, i + 2)
                    pe.wait_ge(xl_done, i + 1)
                    for g in range(12):
                        w = slice((g // NB) * P, (g // NB + 1) * P)
                        cols = slice(g % NB * BW, (g % NB + 1) * BW)
                        pe.wait_ge(lbank_free, 12 * i + g + 1)
                        out = core.bank[6 + g % 2][:, 0:BW]
                        pe.matmul(out, lw_hi[:, w], xc_hi[:, cols], start=True, stop=False)
                        pe.matmul(out, lw_hi[:, w], xc_lo[:, cols], start=False, stop=False)
                        pe.matmul(out, lw_lo[:, w], xc_hi[:, cols], start=False, stop=True).then_inc(lru_mm, 1)

                with pe.Fori(0, LBLK) as i:
                    products(i)

            @block.scalar
            def _(act):
                act.sem_inc(lbank_free, 2)
                act.sem_inc(b_done, 2)
                act.sem_inc(dir_done, 2)
                act.wait_ge(params_in, 16)
                lam = params[:, :, PC_C:PC_C + 2]
                st = Chain(act, act_s)
                st(act.activation(z[:], lam, ACT.Abs))
                act.activation(z[:], z[:], ACT.Exp, scale=-1.0).then_inc(z_done, 1)
                HEAD, PER = 1, 6

                def front_x(i):
                    proj = 6 * i + PROJ0
                    act.wait_ge(conv_done, i + 1)
                    act.wait_ge(S.proj_done, proj + 1)
                    act.activation(lx[:, LXC:LXC + TC], core.bank[0][:, 0:TC], ACT.Copy)
                    act.activation(lx[:, LXS:LXS + BW - TC], core.bank[0][:, TC:BW], ACT.Copy).then_inc(S.bank_free[0], 1)
                    for b in (1, 2):
                        act.wait_ge(S.proj_done, proj + b + 1)
                        c0 = LXS + b * BW - TC
                        act.activation(lx[:, c0:c0 + BW], core.bank[b][:, 0:BW], ACT.Copy).then_inc(S.bank_free[0], 1)

                def front_y(i, par):
                    proj = 6 * i + PROJ0
                    if not isinstance(i, int) or i:
                        act.wait_ge(y_done, i)
                    for b in range(NB):
                        act.wait_ge(S.proj_done, proj + 3 + b + 1)
                        act.activation(ly[par][:, b * BW:(b + 1) * BW], core.bank[3 + b][:, 0:BW],
                                       ACT.Gelu_apprx_tanh).then_inc(S.bank_free[1], 1)
                        if b == 0:
                            act.wait_ge(conv_done, i + 2)
                            act.wait_ge(lru_mm, 12 * i + 2)
                            act.activation(xc_hi[:, 0:TC], xc[par][:, 0:TC], ACT.Copy)
                            act.activation(xc_hi[:, TC:T], xc[par][:, XCS:XCS + TS], ACT.Copy).then_inc(xh_done, 1)

                def tail(i, par, last=False):
                    st = Chain(act, act_s, i, PER)
                    st.base = st.base + HEAD
                    prm = prms[par]
                    for g in range(12):
                        q = g // NB
                        d = q // 2
                        if g % 6 == 0:
                            act.wait_ge(b_done, 2 * i + d + 1)
                        elif g % 6 == 3:
                            act.wait_ge(dir_done, 2 * i + d + 1)
                        dst = rt[d] if q % 2 == 0 else it[d]
                        col = (PC_BA if q % 2 == 0 else PC_BI) + d
                        act.wait_ge(lru_mm, 12 * i + g + 3)
                        act.activation(dst[:, g % NB * BW:(g % NB + 1) * BW], core.bank[6 + g % 2][:, 0:BW],
                                       ACT.Sigmoid, bias=prm[:, col:col + 1]).then_inc(lbank_free, 1)
                    act.wait_ge(lbank_free, 12 * i + 14)
                    act.wait_ge(y_done, i + 1)
                    act.dma_start(dram["y_lru"][bass.ds(i, 1)].rearrange("a p n -> (a p) n"), y[:]).then_inc(y_out, 16)
                    for d in range(2):
                        st(act.activation(at[d][:], rt[d][:], ACT.Exp, scale=prm[:, PC_NEG + d:PC_NEG + d + 1]))
                        st(act.activation(ht[d][:], rt[d][:], ACT.Exp, scale=prm[:, PC_NEG2 + d:PC_NEG2 + d + 1]))
                    for d in range(2):
                        st(act.activation(rt[d][:], rt[d][:], ACT.Tanh, scale=prm[:, PC_C + d:PC_C + d + 1]))
                    if not last:
                        front_x(i + 1)
                    for d in range(2):
                        act.wait_ge(s_done, 2 * i + d + 1)
                        act.activation(rt[d][:], ht[d][:], ACT.Sqrt, bias=tiny[:, 0:1]).then_inc(f_done, 1)
                    st.end()
                    if not last:
                        front_y(i + 1, 1 - par)

                act.wait_ge(zero_done, 2)
                act.wait_ge(c_done, 1)
                front_x(0)
                front_y(0, 0)
                with act.Fori(0, LBLK // 2 - 1) as ii:
                    for r in range(2):
                        tail(2 * ii + r, r)
                tail(LBLK - 2, 0)
                tail(LBLK - 1, 1, True)
                act.wait_ge(y_done, LBLK + 1)
                act.dma_start(dram["y_lru"][LBLK], y[:]).then_inc(y_out, 16)
                act.wait_ge(y_out, 16 * LBLK + 16)

            @block.vector
            def _(dve):
                st = Chain(dve, head_s)
                dve.wait_ge(z_done, 1)
                dve.wait_ge(params_in, 16)
                lam = params[:, :, PC_C:PC_C + 2]
                st(dve.tensor_scalar(s1[:], z[:], 2.0, None, ALU.add))
                st(dve.reciprocal(s1[:], s1[:]))
                st(dve.tensor_tensor(s1[:], s1[:], z[:], ALU.mult))
                st(dve.tensor_tensor(s2[:], s1[:], s1[:], ALU.mult))
                st(dve.tensor_scalar(acc[:], s2[:], 1.0 / 17, 1.0 / 15, ALU.mult, ALU.add))
                for n in (13, 11, 9, 7, 5, 3, 1):
                    st(dve.tensor_tensor(acc[:], acc[:], s2[:], ALU.mult))
                    st(dve.tensor_scalar(acc[:], acc[:], 1.0 / n, None, ALU.add))
                st(dve.scalar_tensor_tensor(acc[:], acc[:], 2.0, s1[:], ALU.mult, ALU.mult))
                st(dve.tensor_scalar(s2[:], lam, -1.0, 0.0, ALU.mult, ALU.max))
                st(dve.tensor_tensor(acc[:], acc[:], s2[:], ALU.add))
                st(dve.tensor_scalar(lam, acc[:], LRU_C, None, ALU.mult))
                st(dve.tensor_scalar(params[:, :, PC_NEG:PC_NEG + 2], acc[:], -LRU_C, None, ALU.mult))
                st(dve.tensor_scalar(params[:, :, PC_NEG2:PC_NEG2 + 2], acc[:], -2 * LRU_C, None, ALU.mult))
                dve.sem_inc(c_done, 1)
                st(dve.memset(y[:], 0.0))
                dve.sem_inc(y_done, 1)
                dve.sem_inc(conv_done, 1)
                dve.wait_ge(zero_done, 2)
                FRONT, TAIL = 4, 13

                def convolve(i, par):
                    st = Chain(dve, front_s, i, FRONT)
                    prm, x = prms[par], xc[par]
                    st(dve.tensor_copy(prm[:], params[:, bass.ds(i, 1), :].rearrange("p a n -> p (a n)")))
                    dve.wait_ge(S.bank_free[0], 3 * i + 6)
                    st(dve.tensor_scalar(x[:], lx[:, 0:XCW], prm[:, PC_W:PC_W + 1], prm[:, PC_B:PC_B + 1],
                                         ALU.mult, ALU.add))
                    for n in (1, 2, 3):
                        ins = dve.scalar_tensor_tensor(x[:], lx[:, n:n + XCW], prm[:, PC_W + n:PC_W + n + 1], x[:],
                                                       ALU.mult, ALU.add)
                        if n < 3:
                            st(ins)
                    ins.then_inc(conv_done, 1)
                    st.end()

                def low_part(i, par):
                    dve.wait_ge(xh_done, i + 1)
                    dve.tensor_tensor(xc_lo[:, 0:TC], xc[par][:, 0:TC], xc_hi[:, 0:TC].bitcast(F32), ALU.subtract)
                    dve.tensor_tensor(xc_lo[:, TC:T], xc[par][:, XCS:XCS + TS], xc_hi[:, TC:T].bitcast(F32),
                                      ALU.subtract).then_inc(xl_done, 1)

                def tail(i, par, last=False):
                    prm = prms[par]
                    for d in range(2):
                        dve.wait_ge(act_s, 6 * i + d + 5 + 1)
                        ins = dve.scalar_tensor_tensor(ht[d][:], ht[d][:], 1.0, rt[d][:], ALU.add, ALU.mult)
                        ins.then_inc(s_done, 1)
                    if not last:
                        convolve(i + 1, 1 - par)
                    st = Chain(dve, tail_s, i, TAIL)
                    for d in range(2):
                        dve.wait_ge(f_done, 2 * i + d + 1)
                        st(dve.tensor_tensor(it[d][:], it[d][:], rt[d][:], ALU.mult))
                        dve.sem_inc(b_done, 1)
                        st(dve.tensor_tensor(it[d][:, 0:TC], it[d][:, 0:TC], xc[par][:, 0:TC], ALU.mult))
                        st(dve.tensor_tensor(it[d][:, TC:T], it[d][:, TC:T], xc[par][:, XCS:XCS + TS], ALU.mult))
                        if d == 0 and not last:
                            low_part(i + 1, 1 - par)
                        for lo, hi, init in ((0, TC, 0.0), (TC, T, prm[:, PC_H0 + d:PC_H0 + d + 1])):
                            a, b, o = (v[d][:, lo:hi] for v in (at, it, ht))
                            if d:
                                a, b, o = rev(a), rev(b), rev(o)
                            st(dve.tensor_tensor_scan(o, a, b, init, ALU.mult, ALU.add))
                        dve.sem_inc(dir_done, 1)
                    for d, at_t in ((0, TC - 1), (1, 0)):
                        st(dve.tensor_copy(fin[:, d, bass.ds(i, 1)], ht[d][:, at_t:at_t + 1]))
                    dve.wait_ge(y_out, 16 * i + 16)
                    st(dve.tensor_tensor(y[:], ht[0][:], ht[1][:], ALU.add))
                    dve.wait_ge(S.bank_free[1], 3 * i + 6)
                    dve.tensor_tensor(y[:], y[:], ly[par][:], ALU.mult).then_inc(y_done, 1)
                    dve.wait_ge(y_done, i + 2)
                    st.end()

                convolve(0, 0)
                low_part(0, 0)
                with dve.Fori(0, LBLK // 2 - 1) as ii:
                    for r in range(2):
                        tail(2 * ii + r, r)
                tail(LBLK - 2, 0)
                tail(LBLK - 1, 1, True)


def gla(core, hhi, hlo):
    nc, dram = core.nc, core.dram
    with ExitStack() as ctx:
        ctx.callback(core.end_stage)

        def sb(name, shape, dt=F32):
            return ctx.enter_context(nc.sbuf_tensor(name, shape, dt))

        def sem(name):
            return core.sem(name)

        S = Stream(core, ctx, "gla")
        glr = sb("glr", [P, T])
        wgate = sb("wgate", [P, HEADS, DK])
        wg = sb("wg", [P, DK])
        params = sb("gla_params", [P, HEADS, 4])
        prm = sb("gla_prm", [P, 4])
        q, k = sb("q", [P, T]), sb("k", [P, T])
        v, r = sb("v", [P, 2, T]), sb("r", [P, 2, T])
        qd = [sb(f"qd{d}", [P, T]) for d in range(2)]
        ki = [sb(f"ki{d}", [P, T]) for d in range(2)]
        ke = [sb(f"ke{d}", [P, T]) for d in range(2)]
        dec = [sb(f"dec{d}", [P, T // GCH]) for d in range(2)]
        tok = sb("tok", [P, NPAIR, 2 * DV])
        o = sb("o", [P, 2, T])
        state = [sb(f"state{s}", [P, DV]) for s in range(6)]
        cached = [sb(f"cached{d}", [P, DV]) for d in range(2)]
        final = [sb(f"final{d}", [P, DV]) for d in range(2)]
        probs = [[sb(f"probs{d}{s}", [P, P]) for s in range(2)] for d in range(2)]
        keep = sb("keep", [P, 2, P], I32)
        ident = sb("ident", [P, P])
        ones = sb("ones", [P, P])
        run = sb("run", [P, T], mybir.dt.bfloat16)
        eps = sb("gla_eps", [P, 1])
        (small_in, state_in, lg_mm, lg_free, ln_done, cum_done, ec_done, gated, tp_mm, tp_free, sc_mm, st_done,
         o_mm, o_done, ns_mm, ns_free, sq_done, y_done, y_out, head_ready, act_s, dve_s, const_done, final_done,
         ) = (
            sem(n) for n in (
                "small_in", "state_in", "lg_mm", "lg_free", "ln_done", "cum_done", "ec_done", "gated", "tp_mm",
                "tp_free", "sc_mm", "st_done", "o_mm", "o_done", "ns_mm", "ns_free", "sq_done", "y_done", "y_out",
                "head_ready", "act_s", "dve_s", "const_done", "final_done"))
        copy_turn = sem("copy_turn")
        final_out = [sem(f"final_out{d}") for d in range(2)]
        UPH = 6
        NSTEP = 2 * NPAIR
        STEPS = [(0, n) for n in range(NPAIR)] + [(1, 0)] + [(1, n) for n in range(NPAIR - 1, 0, -1)]

        def unit(h, j):
            return UPH * h + 1 + j, (1 + j) % 2, 3 * h + (j + 1) // 2

        def start_state(s, c):
            d, n = STEPS[s]
            if c == 0 and n == 0:
                return None
            if c == 0 and STEPS[s - 1][1] == 0:
                return cached[d]
            return state[(2 * s + c) % 6]

        def end_state(s, c):
            d, n = STEPS[s]
            if c == 1 and n == 0:
                return final[d]
            if c == 1 and (s + 1 == NSTEP or STEPS[s + 1][0] != d):
                return None
            return state[(2 * s + c + 1) % 6]

        def update(s, c):
            return core.bank[3 * (s % 2) + 1 - c][:, P:P + DV]

        with nc.Block() as block:
            @block.sync
            def _(sync):
                S.prime(sync)
                sync.dma_start(wgate[0:64], dram["gla_wgate"]).then_inc(small_in, 16)
                sync.dma_start(params[:], dram["gla_params"]).then_inc(small_in, 16)
                sync.dma_start(keep[:], dram["keep"]).then_inc(small_in, 16)
                sync.dma_start(ident[:], dram["ident"]).then_inc(small_in, 16)
                S.load(sync, 0, 0, dram["gla_units"][0])
                with sync.Fori(0, HEADS) as h:
                    for j in range(UPH):
                        u, par, _ = unit(h, j)
                        S.load(sync, u, par, dram["gla_units"][bass.ds(u, 1)].rearrange("a p n -> (a p) n"))
                        if j == 1:
                            sync.wait_ge(y_done, h + 1)
                            sync.dma_start(dram["y_gla"][bass.ds(2 * h, 2)].rearrange("a p n -> p a n"), o[:]).then_inc(y_out, 16)
                            for d in range(2):
                                sync.dma_start(cached[d][:], dram["state_gla"][bass.ds(HEADS * d + h, 1)]
                                               .rearrange("a p n -> (a p) n")).then_inc(state_in, 16)
                    for d in range(2):
                        sync.wait_ge(final_done, 2 * h + d + 1)
                        sync.dma_start(dram["new_gla"][bass.ds(HEADS * d + h, 1)].rearrange("a p n -> (a p) n"),
                                       final[d][:]).then_inc(final_out[d], 16)
                sync.wait_ge(y_done, HEADS + 1)
                sync.dma_start(dram["y_gla"][2 * HEADS:2 * HEADS + 2].rearrange("a p n -> p a n"), o[:]).then_inc(y_out, 16)
                sync.wait_ge(y_out, 16 * HEADS + 16)
                for d in range(2):
                    sync.wait_ge(final_out[d], 16 * HEADS + 16)

            @block.gpsimd
            def _(pool):
                pool.memset(ones[:], 1.0 / DV).then_inc(const_done, 1)
                pool.memset(eps[:], 1e-5).then_inc(const_done, 1)
                for d in range(2):
                    for s in range(2):
                        pool.memset(probs[d][s][:], 0.0).then_inc(const_done, 1)
                S.split(pool, 0, 0, 0, -3)
                with pool.Fori(0, HEADS) as h:
                    for j in range(UPH):
                        u, par, q_ = unit(h, j)
                        S.split(pool, u, par, q_, 3 * u - 3)

            @block.tensor
            def _(pe):
                pe.wait_ge(const_done, 6)
                S.project(pe, 0, 0, 0, hhi, hlo)
                with pe.Fori(0, HEADS) as h:
                    pe.wait_ge(head_ready, h + 1)
                    pe.wait_ge(S.bank_free[0], 9 * h + 6)
                    for g in range(6):
                        d = g // NB
                        pe.wait_ge(lg_free, 6 * h + g + 1)
                        pe.matmul(core.bank[6 + g % 2][:, 0:BW], wg[32 * d:32 * d + RANK, :],
                                  glr[32 * d:32 * d + RANK, g % NB * BW:(g % NB + 1) * BW],
                                  start=True, stop=True).then_inc(lg_mm, 1)
                    for j in range(UPH):
                        u, par, q_ = unit(h, j)
                        S.project(pe, u, par, q_, hhi, hlo)
                    pe.wait_ge(S.bank_free[1], 9 * h + 9)
                    pe.wait_ge(S.bank_free[0], 9 * h + 12)
                    pe.wait_ge(gated, 2 * h + 2)
                    pe.wait_ge(lg_free, 6 * h + 8)
                    for n in range(NPAIR):
                        cols = slice(n * P, (n + 1) * P)
                        pe.wait_ge(tp_free, NPAIR * h + n + 1)
                        out = core.bank[6 + n % 2]
                        for c, src in enumerate((v[:, 0, cols], v[:, 1, cols], ke[0][:, cols], ke[1][:, cols])):
                            mm = pe.transpose(out[:, c * P:(c + 1) * P], src, ident[:])
                        mm.then_inc(tp_mm, 1)

                    def scores(s):
                        d, n = STEPS[s]
                        cols = slice(n * P, (n + 1) * P)
                        if s < 2:
                            pe.wait_ge(S.bank_free[1], 9 * h + 12)
                            pe.wait_ge(S.bank_free[0], 9 * h + 15)
                            pe.wait_ge(tp_free, NPAIR * h + NPAIR + 2)
                        else:
                            pe.wait_ge(st_done, NSTEP * h + s - 1)
                        pe.matmul(core.bank[3 * (s % 2)][:, 0:P], ki[d][:, cols], qd[d][:, cols], start=True, stop=True)
                        for c in range(2):
                            if end_state(s, c) is None:
                                continue
                            half = c if d == 0 else 1 - c
                            rows = slice(GCH * half, GCH * half + GCH)
                            mm = pe.matmul(update(s, c),
                                           tok[rows, n, DV + d * DK:DV + (d + 1) * DK], tok[rows, n, 0:DV],
                                           start=True, stop=True)
                        mm.then_inc(sc_mm, 1)

                    scores(0)
                    for s, (d, n) in enumerate(STEPS):
                        if s + 1 < NSTEP:
                            scores(s + 1)
                        if s == 0:
                            pe.wait_ge(state_in, 32 * h + 32)
                        pe.wait_ge(st_done, NSTEP * h + s + 1)
                        if s >= 2:
                            pe.wait_ge(o_done, NSTEP * h + s - 1)
                        for vt in range(2):
                            out = core.bank[3 * (s % 2) + 2][:, vt * P:(vt + 1) * P]
                            vc = slice(vt * P, (vt + 1) * P)
                            inter = [c for c in range(2) if start_state(s, c) is not None]
                            mm = pe.matmul(out, tok[:, n, vc], probs[d][s % 2][:], start=True, stop=not inter)
                            for c in inter:
                                half = c if d == 0 else 1 - c
                                t0 = n * P + half * GCH
                                mm = pe.matmul(out[:, half * GCH:(half + 1) * GCH], start_state(s, c)[:, vc],
                                               qd[d][:, t0:t0 + GCH], start=False, stop=(c == inter[-1]))
                        mm.then_inc(o_mm, 1)
                    pe.wait_ge(o_done, NSTEP * h + NSTEP)
                    for g in range(6):
                        b = g % NB
                        cols = slice(b * BW, (b + 1) * BW)
                        src = o if g < NB else v
                        if g >= 2:
                            pe.wait_ge(ns_free, 6 * h + g - 1)
                        if g >= NB:
                            pe.wait_ge(sq_done, NB * h + b + 1)
                        out = core.bank[6 + g % 2][:, 0:BW]
                        pe.matmul(out, ones[:], src[:, 0, cols], start=True, stop=False)
                        pe.matmul(out, ones[:], src[:, 1, cols], start=False, stop=True).then_inc(ns_mm, 1)
                    pe.wait_ge(ns_free, 6 * h + 6)

            @block.scalar
            def _(act):
                act.sem_inc(lg_free, 2)
                act.sem_inc(final_out[0], 16)
                act.sem_inc(final_out[1], 16)
                act.sem_inc(tp_free, 2)
                act.wait_ge(const_done, 6)
                for b in range(NB):
                    act.wait_ge(S.proj_done, PROJ0 + b + 1)
                    act.activation(glr[:, b * BW:(b + 1) * BW], core.bank[b][:, 0:BW], ACT.Copy).then_inc(S.bank_free[0], 1)
                PER = 6
                with act.Fori(0, HEADS) as h:
                    st = Chain(act, act_s, h, PER)

                    def evac(j, dst, func, scale=1.0):
                        u, par, _ = unit(h, j)
                        for b in range(NB):
                            act.wait_ge(S.proj_done, 3 * u + b + 1 + PROJ0)
                            act.activation(dst[:, b * BW:(b + 1) * BW], core.bank[3 * par + b][:, 0:BW], func,
                                           scale=scale).then_inc(S.bank_free[par], 1)

                    for g in range(6):
                        act.wait_ge(lg_mm, 6 * h + g + 1)
                        act.activation(qd[g // NB][:, g % NB * BW:(g % NB + 1) * BW], core.bank[6 + g % 2][:, 0:BW],
                                       ACT.Identity, bias=prm[:, g // NB:g // NB + 1]).then_inc(lg_free, 1)
                    act.wait_ge(lg_free, 6 * h + 8)
                    for d in range(2):
                        st(act.activation(ki[d][:], qd[d][:], ACT.Abs))
                        st(act.activation(ki[d][:], ki[d][:], ACT.Exp, scale=-1.0))
                        act.activation(ki[d][:], ki[d][:], ACT.Ln, bias=1.0).then_inc(ln_done, 1)
                    act.wait_ge(y_done, h + 1)
                    evac(0, q, ACT.Copy, DK ** -0.5)
                    evac(1, k, ACT.Copy)
                    for d in range(2):
                        act.wait_ge(cum_done, 2 * h + d + 1)
                        st(act.activation(qd[d][:], ki[d][:], ACT.Exp, scale=1.0 / GLA_TAU))
                        act.activation(ki[d][:], ki[d][:], ACT.Exp, scale=-1.0 / GLA_TAU).then_inc(ec_done, 1)
                    evac(2, v[:, 0, :], ACT.Copy)
                    evac(3, v[:, 1, :], ACT.Copy)
                    evac(4, r[:, 0, :], ACT.Silu)
                    evac(5, r[:, 1, :], ACT.Silu)
                    for n in range(NPAIR):
                        act.wait_ge(tp_mm, NPAIR * h + n + 1)
                        act.activation(tok[:, n, :], core.bank[6 + n % 2][:, :], ACT.Copy).then_inc(tp_free, 1)
                    for b in range(NB):
                        cols = slice(b * BW, (b + 1) * BW)
                        act.wait_ge(ns_free, 6 * h + b + 1)
                        act.activation(v[:, :, cols], o[:, :, cols], ACT.Square).then_inc(sq_done, 1)
                    for b in range(NB):
                        act.wait_ge(ns_mm, 6 * h + NB + b + 1)
                        act.activation(k[:, b * BW:(b + 1) * BW], core.bank[6 + (NB + b) % 2][:, 0:BW], ACT.Sqrt,
                                       bias=eps[:, 0:1]).then_inc(ns_free, 1)
                    st.end()

            @block.vector
            def _(dve):
                st = Chain(dve, dve_s)
                st(dve.memset(run[:], 1.0))
                st(dve.memset(run[:, ::GCH], 0.0))
                st(dve.memset(o[:], 0.0))
                dve.sem_inc(y_done, 1)
                dve.wait_ge(small_in, 64)
                dve.wait_ge(const_done, 6)
                head = st.n
                PER = 64
                with dve.Fori(0, HEADS) as h:
                    st = Chain(dve, dve_s, h, PER)
                    st.base = st.base + head
                    st(dve.tensor_copy(prm[:], params[:, bass.ds(h, 1), :].rearrange("p a n -> p (a n)")))
                    dve.tensor_copy(wg[0:64, :], wgate[0:64, bass.ds(h, 1), :].rearrange("p a n -> p (a n)")).then_inc(head_ready, 1)
                    for d in range(2):
                        dve.wait_ge(ln_done, 2 * h + d + 1)
                        st(dve.scalar_tensor_tensor(qd[d][:], qd[d][:], 0.0, ki[d][:], ALU.min, ALU.subtract))
                        a, c = qd[d][:], ki[d][:]
                        if d:
                            a, c = rev(a), rev(c)
                        dve.tensor_tensor_scan(c, run[:], a, 0.0, ALU.mult, ALU.add).then_inc(cum_done, 1)
                    dve.wait_ge(S.bank_free[1], 9 * h + 6)
                    dve.wait_ge(S.bank_free[0], 9 * h + 9)
                    for d in range(2):
                        dve.wait_ge(ec_done, 2 * h + d + 1)
                        last = slice(GCH - 1, T, GCH) if d == 0 else slice(0, T, GCH)
                        st(dve.tensor_copy(dec[d][:], qd[d][:, last]))
                        st(dve.tensor_tensor(ki[d][:], k[:], ki[d][:], ALU.mult))
                        st(dve.tensor_tensor(ke[d][:].rearrange("p (c t) -> p c t", t=GCH),
                                             ki[d][:].rearrange("p (c t) -> p c t", t=GCH),
                                             dec[d][:].unsqueeze(2).to_broadcast([P, T // GCH, GCH]), ALU.mult))
                        dve.tensor_tensor(qd[d][:], q[:], qd[d][:], ALU.mult).then_inc(gated, 1)

                    def collect(s):
                        d, n = STEPS[s]
                        dve.wait_ge(o_mm, NSTEP * h + s + 1)
                        ov = o[:, :, n * P:(n + 1) * P]
                        psum = core.bank[3 * (s % 2) + 2][:, 0:2 * P].rearrange("p (v t) -> p v t", v=2)
                        if d == 0:
                            dve.tensor_copy(ov, psum).then_inc(o_done, 1)
                        else:
                            dve.tensor_tensor(ov, ov, psum, ALU.add).then_inc(o_done, 1)

                    dve.wait_ge(y_out, 16 * h + 16)
                    dve.wait_ge(state_in, 32 * h + 32)
                    for s, (d, n) in enumerate(STEPS):
                        dve.wait_ge(sc_mm, NSTEP * h + s + 1)
                        if s >= 2:
                            dve.wait_ge(o_mm, NSTEP * h + s - 1)
                        dve.sem_inc(copy_turn, 1)
                        st(dve.copy_predicated(probs[d][s % 2][:], keep[:, d, :], core.bank[3 * (s % 2)][:, 0:P]))
                        for c in range(2):
                            dst = end_state(s, c)
                            if dst is None:
                                continue
                            half = c if d == 0 else 1 - c
                            ch = 2 * n + half
                            upd = update(s, c)
                            src = start_state(s, c)
                            if src is None:
                                st(dve.tensor_copy(dst[:], upd))
                            else:
                                if c == 1 and n == 0:
                                    dve.wait_ge(final_out[d], 16 * h + 16)
                                st(dve.scalar_tensor_tensor(dst[:], src[:], dec[d][:, ch:ch + 1], upd,
                                                            ALU.mult, ALU.add))
                        dve.sem_inc(st_done, 1)
                        if n == 0:
                            dve.sem_inc(final_done, 1)
                        if s:
                            collect(s - 1)
                    collect(NSTEP - 1)
                    dve.wait_ge(o_done, NSTEP * h + NSTEP)
                    for b in range(NB):
                        ov = o[:, :, b * BW:(b + 1) * BW]
                        dve.wait_ge(ns_mm, 6 * h + b + 1)
                        mean = core.bank[6 + b % 2][:, 0:BW].unsqueeze(1).to_broadcast([P, 2, BW])
                        dve.tensor_tensor(ov, ov, mean, ALU.subtract).then_inc(ns_free, 1)
                    dve.wait_ge(ns_free, 6 * h + 6)
                    st(dve.reciprocal(q[:], k[:]))
                    for vt in range(2):
                        st(dve.scalar_tensor_tensor(o[:, vt, :], o[:, vt, :], prm[:, 2 + vt:3 + vt], q[:],
                                                    ALU.mult, ALU.mult))
                    dve.tensor_tensor(o[:], o[:], r[:], ALU.mult).then_inc(y_done, 1)
                    dve.wait_ge(y_done, h + 2)
                    st.end()


def s5_and_gates(core, hhi, hlo, mod, csilu):
    nc, dram = core.nc, core.dram
    with ExitStack() as ctx:
        ctx.callback(core.end_stage)

        def sb(name, shape, dt=F32):
            return ctx.enter_context(nc.sbuf_tensor(name, shape, dt))

        def sem(name):
            return core.sem(name)

        GH = GROUPS // 2
        BPH = GH // GB
        LAGS = SCH + 1
        H1, H2 = slice(0, S5P), slice(S5P, P)
        UNITS_U, UNITS_G = KD, 3 * KD
        S = Stream(core, ctx, "s5", GB * LAGS * S5I)
        pw = [sb(f"pw{c}", [P, LAGS, GROUPS]) for c in "ri"]
        coef = sb("coef", [P, 2, 2, GROUPS])
        bb = [sb(f"bb{c}", [P, GROUPS, S5I]) for c in "ri"]
        cc = [sb(f"cc{c}", [P, GROUPS, S5I]) for c in "ri"]
        init = sb("s5_init", [P, 2, GROUPS])
        fins = sb("s5_fins", [P, 2, GROUPS])
        cur = [sb(f"cur{s}", [P, 2, GH]) for s in range(2)]
        cofs = [sb(f"cofs{n}", [P, 2, GH]) for n in range(2)]
        t01 = sb("t01", [P, 2, 2 * GH])
        t0, t1 = (t01[:, n, :].rearrange("p (r g) -> p r g", r=2) for n in range(2))
        skip = t01[0:S5I].rearrange("p a x -> p (a x)").rearrange("p (g i) -> p g i", i=S5I)
        hs = sb("hs", [P, NCH, 2, GH])
        ub = sb("ub", [P, GB, NCH])
        work = sb("work", [P, 2 * GB * LAGS * S5I + 2 * GB * NCH])
        NW = GB * SCH * S5I
        wt = [work[:, c * NW:(c + 1) * NW] for c in range(2)]
        win = work[:, 2 * NW:4 * NW].rearrange("p (x m) -> p x m", m=P)
        lam = work[:, 2 * UW:2 * UW + 3 * GROUPS].rearrange("p (n g) -> p n g", g=GROUPS)
        sm = [work[:, 2 * UW + (3 + n) * GROUPS:2 * UW + (4 + n) * GROUPS] for n in range(8)]
        NCA = GB * LAGS * S5I
        ca_set = [[mem[:, c * NCA:(c + 1) * NCA] for c in range(2)] for mem in (work, S.memory)]
        hn = work[:, 2 * NCA:2 * NCA + 2 * GB * NCH].rearrange("p (r g c) -> p r g c", r=2, g=GB)
        tmp = sb("s5tmp", [P, NCA])
        ws = [sb(f"ws{c}", [P, GB, SCH]) for c in "ri"]
        cq = [sb(f"cq{c}", [P, GB, LAGS]) for c in "ri"]
        bblk = [sb(f"bblk{c}", [P, GB, 2 * S5I]) for c in "ri"]
        bdup = [sb(f"bdup{c}", [P, GB, 2 * S5I]) for c in "ri"]
        wias = [sb(f"wia{s}", [P, GB, P]) for s in range(2)]
        KW = (LAGS + 1) * S5I
        stage = sb("stage", [P, T + GB * KW])
        gate = [stage[:, s * T:(s + 1) * T] for s in range(2)]
        yb = stage[:, 0:T].rearrange("p (g c) -> p g c", g=GB)
        kst = stage[0:32, T:T + GB * KW].rearrange("p (g a) -> p g a", a=KW)
        ident = sb("s5_ident", [P, P])
        up = [gate[s].rearrange("p (s c) -> p s c", s=SCH) for s in range(2)]
        (p_in, act_p, trig, u_out, ub_in, wt_done, tr_mm, tr_free, w_mm, w_free_f, w_free_b, w_used, new, prod,
         saved, dve_s, act_s, ca_done, k_mm, k_free, kd_out, hn_done, y_mm, y_free, yb_out, u_free,
         half_ready, scan_done, fin_out, up_ready, ws_s) = (
            sem(n) for n in (
                "p_in", "act_p", "trig", "u_out", "ub_in", "wt_done", "tr_mm", "tr_free", "w_mm",
                "w_free_f", "w_free_b", "w_used", "new", "prod", "saved", "dve_s", "act_s", "ca_done", "k_mm", "k_free",
                "kd_out", "hn_done", "y_mm", "y_free", "yb_out", "u_free", "half_ready", "scan_done",
                "fin_out", "up_ready", "ws_s"))
        wia_in = [sem(f"wia_in{s}") for s in range(2)]
        d_in, d_added = sem("d_in"), sem("d_added")
        kst_free = sem("kst_free")
        turn = sem("turn")
        NA = (6 * KD - NMOD1) // 2
        ada = [work[:, s * UW:(s + 1) * UW] for s in range(4)]
        bada = sb("s5_bada", [P, 6 * KD])
        ada_in = [sem(f"s5_ada_in{s}") for s in range(4)]
        ada_used, bada_in, bias_done = sem("ada_used"), sem("bada_in"), sem("bias_done")

        def ada_after(j):
            many = NA - UNITS_G // 2
            return range(2 * j, 2 * j + 2) if j < many else range(many + j, many + j + 1)

        gate_out = [sem(f"s5_gate_out{s}") for s in range(2)]
        u_st = [sem(f"u_st{s}") for s in range(2)]

        def v3(ap, a):
            return ap.rearrange("p (g a i) -> p g a i", g=GB, a=a)

        def load_u(eng, n):
            for s in range(SCH):
                src = dram["u_d"][bass.ds(n * P, P)].rearrange("(g j) s c -> j g s c", j=S5I)[:, :, s, :]
                eng.dma_start(ub[s * S5I:(s + 1) * S5I, :, :], src).then_inc(ub_in, 16)

        with nc.Block() as block:
            @block.sync
            def _(sync):
                S.prime(sync)
                for e in range(2):
                    half = slice(e * S5P, (e + 1) * S5P)
                    sync.dma_start(lam[half, 0, :], dram["s5_lam"][0, half]).then_inc(p_in, 16)
                    sync.dma_start(lam[half, 1, :], dram["s5_lam"][1, half]).then_inc(p_in, 16)
                    sync.dma_start(lam[half, 2, :], dram["s5_step"][e].partition_broadcast(S5P)).then_inc(p_in, 16)
                    for c in range(2):
                        sync.dma_start(bb[c][half], dram["s5_b"][c]).then_inc(p_in, 16)
                        sync.dma_start(cc[c][half], dram["s5_c"][c]).then_inc(p_in, 16)
                sync.dma_start(init[:], dram["s5_init"]).then_inc(p_in, 16)
                sync.dma_start(ident[:], dram["ident"]).then_inc(p_in, 16)
                sync.dma_start(bada[:], dram["bada"]).then_inc(bada_in, 16)
                sync.sem_inc(ada_used, 4)
                for m in range(UNITS_U):
                    S.load(sync, m, m % 2, dram["s5_units"][m])
                    if m >= 1:
                        sync.wait_ge(S.bank_free[(m - 1) % 2], 3 + 3 * ((m - 1) // 2 + 1))
                        sync.dma_start(dram["u_d"][(m - 1) * P:m * P], up[(m - 1) % 2]).then_inc(u_st[(m - 1) % 2], 16)
                m = UNITS_U
                sync.wait_ge(S.bank_free[(m - 1) % 2], 3 + 3 * ((m - 1) // 2 + 1))
                sync.dma_start(dram["u_d"][(m - 1) * P:m * P], up[(m - 1) % 2]).then_inc(u_st[(m - 1) % 2], 16)
                for s in range(2):
                    sync.wait_ge(u_st[s], 16 * UNITS_U // 2)
                with sync.Fori(0, 2) as hf:
                    with sync.Fori(0, BPH) as i:
                        n = BPH * hf + i
                        sync.wait_ge(u_free, 2 * BPH * hf + i + 1)
                        load_u(sync, n)
                    for j in range(UNITS_G // 2):
                        u = UNITS_U + UNITS_G // 2 * hf + j
                        S.load(sync, u, j % 2, dram["s5_units"][bass.ds(u, 1)].rearrange("a p n -> (a p) n"))
                        for a in ada_after(j):
                            if a == 0:
                                sync.wait_ge(u_free, 2 * BPH * hf + BPH + 1)
                            sync.wait_ge(ada_used, NA * hf + a + 1)
                            sync.dma_start(ada[a % 4], dram["w_ada"][bass.ds(NMOD1 + NA * hf + a, 1)]
                                           .rearrange("a p n -> (a p) n")).then_inc(ada_in[a % 4], 16)

                    def lag_blocks_out(n):
                        sync.dma_start(skip, dram["s5_skip"][bass.ds(n, 1)].rearrange("a j g i -> (a j) g i")).then_inc(d_in, 16)
                        sync.wait_ge(d_added, n + 1)
                        sync.sem_inc(turn, 1)
                        kd = dram["kd"][bass.ds(n * GB, GB)].rearrange("g j d i -> j g (d i)")
                        sync.dma_start(kd[:, :, SCH * S5I:(2 * SCH - 1) * S5I],
                                       kst[0:S5I, :, S5I:SCH * S5I]).then_inc(kd_out, 16)
                        sync.dma_start(kd[:, :, 0:(SCH - 1) * S5I],
                                       kst[S5I:2 * S5I, :, 2 * S5I:LAGS * S5I]).then_inc(kd_out, 16)
                        sync.dma_start(kd[:, :, (SCH - 1) * S5I:SCH * S5I],
                                       kst[0:S5I, :, LAGS * S5I:(LAGS + 1) * S5I]).then_inc(kd_out, 16)
                        sync.wait_ge(kd_out, 48 * n + 48)
                        sync.sem_inc(kst_free, 1)

                    def toeplitz_in(n, par):
                        kd = dram["kd"][bass.ds(n * GB, GB)].rearrange("g j d i -> j g (d i)")
                        for s in range(SCH):
                            d0 = (SCH - 1 - s) * S5I
                            sync.dma_start(wias[par][s * S5I:(s + 1) * S5I], kd[:, :, d0:d0 + P]).then_inc(wia_in[par], 16)

                    def outputs(n):
                        sync.wait_ge(y_free, 3 * n + 6)
                        for t in range(SCH):
                            dst = dram["y_d"][bass.ds(n * P, P)].rearrange("(g i) t c -> i g t c", i=S5I)[:, :, t, :]
                            sync.dma_start(dst, yb[t * S5I:(t + 1) * S5I]).then_inc(yb_out, 16)
                        sync.wait_ge(yb_out, 128 * n + 128)
                        sync.sem_inc(half_ready, 1)

                    sync.wait_ge(u_free, 2 * BPH * hf + BPH + 1)
                    load_u(sync, BPH * hf)
                    sync.wait_ge(scan_done, hf + 1)
                    sync.sem_inc(turn, 1)
                    for b in range(BPH):
                        n = BPH * hf + b
                        if b % 2 == 0:
                            for e in range(2):
                                lag_blocks_out(n + e)
                                if b and not e:
                                    sync.wait_ge(u_free, 2 * BPH * hf + BPH + b + 1)
                                toeplitz_in(n + e, e)
                                if b and not e:
                                    load_u(sync, n)
                        else:
                            sync.wait_ge(u_free, 2 * BPH * hf + BPH + b + 1)
                            load_u(sync, n)
                        if b % 2:
                            outputs(n - 1)
                            outputs(n)
                sync.wait_ge(scan_done, 2)
                sync.dma_start(dram["new_s5"], fins[:]).then_inc(fin_out, 16)
                sync.wait_ge(fin_out, 16)

            @block.gpsimd
            def _(pool):
                for u in range(UNITS_U):
                    S.split(pool, u, u % 2, u // 2, 3 * u - 3)
                with pool.Fori(0, 2) as hf:
                    for j in range(UNITS_G // 2):
                        u = UNITS_U + UNITS_G // 2 * hf + j
                        S.split(pool, u, j % 2, UNITS_U // 2 + UNITS_G // 4 * hf + j // 2, 3 * u - 3)
                    for b in range(BPH):
                        n = BPH * hf + b
                        pool.wait_ge(d_in, 16 * n + 16)
                        pool.wait_ge(k_free, 3 * n + 6)
                        lag0 = kst[0:S5I, :, LAGS * S5I:(LAGS + 1) * S5I]
                        pool.tensor_tensor(lag0, lag0, skip, ALU.add).then_inc(d_added, 1)

            @block.tensor
            def _(pe):
                for u in range(UNITS_U):
                    S.project(pe, u, u % 2, u // 2, hhi, hlo)
                with pe.Fori(0, 2) as hf:
                    q0 = UNITS_U // 2 + UNITS_G // 4 * hf
                    for par in range(2):
                        pe.wait_ge(S.bank_free[par], 3 * q0 + 3)
                    pe.sem_inc(turn, 1)
                    with pe.Fori(0, BPH) as i:
                        n = BPH * hf + i
                        pe.wait_ge(wt_done, n + 1)
                        for x in range(4):
                            pe.wait_ge(tr_free, 4 * n + x + 1)
                            for y in range(4):
                                g, c = 2 * x + y // 2, y % 2
                                mm = pe.transpose(core.bank[6 + x % 2][:, y * P:(y + 1) * P],
                                                  wt[c][:, g * P:(g + 1) * P], ident[:])
                            mm.then_inc(tr_mm, 1)
                        pe.wait_ge(ub_in, 128 * (2 * BPH * hf + i) + 128)
                        pe.wait_ge(tr_free, 4 * n + 6)
                        for g in range(GB):
                            pe.wait_ge(w_free_f, GB * n + g + 1)
                            pe.wait_ge(w_free_b, GB * n + g + 1)
                            for c in range(2):
                                mm = pe.matmul(core.bank[g % 4][:, c * NCH:(c + 1) * NCH], win[:, 2 * g + c, :],
                                               ub[:, g, :], start=True, stop=True)
                            mm.then_inc(w_mm, 1)
                        pe.wait_ge(w_mm, GB * n + GB)
                        pe.sem_inc(u_free, 1)
                    pe.wait_ge(w_free_f, GB * BPH * hf + GB * BPH + 4)
                    pe.wait_ge(w_free_b, GB * BPH * hf + GB * BPH + 4)
                    for j in range(UNITS_G // 2):
                        S.project(pe, UNITS_U + UNITS_G // 2 * hf + j, j % 2, q0 + j // 2, hhi, hlo)
                        for a in ada_after(j):
                            pe.wait_ge(ada_in[a % 4], 16 * (NA // 4) * hf + 16 * (a // 4 + 1))
                            for k in range(KD):
                                mm = pe.matmul(core.bank[6][:, 2 * a:2 * a + 2], ada[a % 4][:, k * P:(k + 1) * P],
                                               csilu[:, k, :], start=(k == 0), stop=(k == KD - 1))
                            mm.then_inc(ada_used, 1)
                    for par in range(2):
                        pe.wait_ge(S.bank_free[par], 3 * q0 + 3 * (UNITS_G // 4) + 3)

                    def lag_blocks(n, par):
                        pe.wait_ge(ca_done, n + 1)
                        cav = [v3(x, LAGS) for x in ca_set[par]]
                        for x, gs in enumerate(((0, 1, 2), (3, 4, 5), (6, 7))):
                            pe.wait_ge(k_free, 3 * n + x + 1)
                            for g in gs:
                                o0 = (g - gs[0]) * (LAGS + 1) * S5I
                                out = core.bank[x][0:32, o0:o0 + LAGS * S5I]
                                for c in range(2):
                                    pe.matmul(out, bblk[c][:, g, :], cav[c][:, g, :, :].rearrange("p a i -> p (a i)"),
                                              start=(c == 0), stop=(c == 1))
                                out = core.bank[x][0:32, o0 + LAGS * S5I:o0 + (LAGS + 1) * S5I]
                                for c in range(2):
                                    mm = pe.matmul(out, bdup[c][:, g, :], cav[c][:, g, 0, :],
                                                   start=(c == 0), stop=(c == 1))
                            mm.then_inc(k_mm, 1)

                    for b in range(BPH):
                        n = BPH * hf + b
                        if b % 2 == 0:
                            lag_blocks(n, 0)
                            lag_blocks(n + 1, 1)
                        cav = [v3(x, LAGS) for x in ca_set[b % 2]]
                        pe.wait_ge(wia_in[b % 2], 128 * (BPH // 2 * hf + b // 2) + 128)
                        pe.wait_ge(hn_done, n + 1)
                        pe.wait_ge(ub_in, 128 * (2 * BPH * hf + BPH + b) + 128)
                        for x, gs in enumerate(((0, 1, 2), (3, 4, 5), (6, 7))):
                            pe.wait_ge(y_free, 3 * n + x + 1)
                            for g in gs:
                                out = core.bank[3 + x][:, (g - gs[0]) * NCH:(g - gs[0] + 1) * NCH]
                                pe.matmul(out, wias[b % 2][:, g, :], ub[:, g, :], start=True, stop=False)
                                for c in range(2):
                                    mm = pe.matmul(out, cav[c][:, g, 1:LAGS, :].rearrange("p a i -> p (a i)"),
                                                   hn[:, c, g, :], start=False, stop=(c == 1))
                            mm.then_inc(y_mm, 1)
                        pe.wait_ge(y_mm, 3 * n + 3)
                        pe.sem_inc(u_free, 1)
                    pe.wait_ge(k_free, 3 * BPH * hf + 3 * BPH + 3)
                    pe.wait_ge(y_free, 3 * BPH * hf + 3 * BPH + 3)

            @block.scalar
            def _(act):
                act.sem_inc(tr_free, 2)
                act.sem_inc(saved, 1)
                act.sem_inc(w_free_f, 4)
                act.sem_inc(k_free, 3)
                act.sem_inc(kst_free, 1)
                act.sem_inc(y_free, 3)
                act.sem_inc(half_ready, 1)
                act.sem_inc(gate_out[0], 16)
                act.sem_inc(gate_out[1], 16)
                act.wait_ge(p_in, 16 * 16)
                st = Chain(act, act_p)
                st(act.activation(sm[0][:], lam[:, 2, :], ACT.Exp))
                act.wait_ge(trig, 1)
                st(act.activation(sm[1][:], sm[1][:], ACT.Exp))
                act.wait_ge(trig, 2)
                st(act.activation(sm[3][:], sm[2][:], ACT.Sin))
                st(act.activation(sm[4][:], sm[2][:], ACT.Sin, scale=0.5))
                for u in range(UNITS_U):
                    if u >= 2:
                        act.wait_ge(u_st[u % 2], 16 * (u // 2))
                    for b in range(NB):
                        act.wait_ge(S.proj_done, PROJ0 + 3 * u + b + 1)
                        nb = BW // SCH
                        act.activation(up[u % 2][:, :, b * nb:(b + 1) * nb],
                                       core.bank[3 * (u % 2) + b][:, 0:BW].rearrange("p (c s) -> p s c", s=SCH),
                                       ACT.Copy).then_inc(S.bank_free[u % 2], 1)
                for s in range(2):
                    act.wait_ge(u_st[s], 16 * UNITS_U // 2)
                with act.Fori(0, 2) as hf:
                    with act.Fori(0, BPH) as i:
                        n = BPH * hf + i
                        for x in range(4):
                            act.wait_ge(tr_mm, 4 * n + x + 1)
                            act.activation(win[:, 4 * x:4 * x + 4, :],
                                           core.bank[6 + x % 2][:].rearrange("p (a m) -> p a m", a=4),
                                           ACT.Copy).then_inc(tr_free, 1)
                        for g in range(GB):
                            act.wait_ge(w_mm, GB * n + g + 1)
                            act.activation(hs[H1, :, :, bass.ds(GB * i + g, 1)].rearrange("p c r a -> p r (c a)"),
                                           core.bank[g % 4][H1, 0:2 * NCH].rearrange("p (r c) -> p r c", r=2),
                                           ACT.Copy).then_inc(w_free_f, 1)

                    def gate_bank(x, it):
                        par, b = x // 3, x % 3
                        u = UNITS_U + UNITS_G // 2 * hf + 2 * it + par
                        if b == 0:
                            act.wait_ge(gate_out[par], 16 * (UNITS_G // 4 * hf + it) + 16)
                        act.wait_ge(S.proj_done, 3 * u + b + 1 + PROJ0)
                        act.activation(gate[par][:, b * BW:(b + 1) * BW], core.bank[x][:, 0:BW],
                                       ACT.Sigmoid).then_inc(S.bank_free[par], 1)
                        if b == 2:
                            act.wait_ge(S.bank_free[par], 3 * (UNITS_U // 2 + UNITS_G // 4 * hf + it + 1) + 3)
                            gm = UNITS_G // 2 * hf + 2 * it + par
                            act.dma_start(dram["gates"][bass.ds(gm, 1)].rearrange("a p t -> (a p) t"),
                                          gate[par]).then_inc(gate_out[par], 16)

                    with act.Fori(0, NCH // 24) as it:
                        for x in range(6):
                            for y in range(4):
                                k = 4 * x + y
                                m = NCH * hf + 24 * it + k
                                act.wait_ge(w_used, m + 1)
                                act.activation(hs[:, bass.ds(24 * it + k, 1), :, :].rearrange("p a r g -> p (a r) g"),
                                               cur[k % 2][:], ACT.Copy).then_inc(saved, 1)
                            gate_bank(x, it)
                    for par in range(2):
                        act.wait_ge(gate_out[par], 16 * (UNITS_G // 4) * (hf + 1) + 16)
                    act.wait_ge(saved, NCH * hf + NCH + 1)
                    act.wait_ge(ada_used, NA * hf + NA + 4)
                    act.activation(mod[:, bass.ds(NMOD1 + NA * hf, NA), :],
                                   core.bank[6][:, 0:2 * NA].rearrange("p (m c) -> p m c", c=2), ACT.Copy)

                    def lag_evac(n):
                        act.wait_ge(kst_free, n + 1)
                        for x, gs in enumerate(((0, 3), (3, 6), (6, 8))):
                            act.wait_ge(k_mm, 3 * n + x + 1)
                            act.activation(kst[:, gs[0]:gs[1], :],
                                           core.bank[x][0:32, 0:(gs[1] - gs[0]) * KW].rearrange("p (g a) -> p g a", a=KW),
                                           ACT.Copy).then_inc(k_free, 1)

                    for b in range(BPH):
                        n = BPH * hf + b
                        gs = slice(GB * b, GB * (b + 1))
                        if b % 2 == 0:
                            lag_evac(n)
                        act.wait_ge(y_mm if b else y_free, 3 * n if b else 3 * n + 3)
                        for r in range(2):
                            act.activation(hn[H1, r], hs[H1, :, r, gs].rearrange("p c g -> p g c"), ACT.Copy)
                            ins = act.activation(hn[H2, r, :, ::-1], hs[H2, :, r, gs].rearrange("p c g -> p g c"), ACT.Copy)
                        ins.then_inc(hn_done, 1)
                        if b % 2 == 0:
                            lag_evac(n + 1)
                        act.wait_ge(half_ready, n + 1)
                        for x, gs in enumerate(((0, 3), (3, 6), (6, 8))):
                            act.wait_ge(y_mm, 3 * n + x + 1)
                            act.activation(yb[:, gs[0]:gs[1], :],
                                           core.bank[3 + x][:, 0:(gs[1] - gs[0]) * NCH].rearrange("p (g c) -> p g c", c=NCH),
                                           ACT.Gelu_apprx_tanh).then_inc(y_free, 1)
                    act.wait_ge(half_ready, BPH * hf + BPH + 1)

            @block.vector
            def _(dve):
                dve.sem_inc(w_free_b, 4)
                dve.sem_inc(u_free, 1)
                st = Chain(dve, ws_s)
                TT, TS_, STT = dve.tensor_tensor, dve.tensor_scalar, dve.scalar_tensor_tensor
                M, A_, SB = ALU.mult, ALU.add, ALU.subtract
                re, im = lam[:, 0, :], lam[:, 1, :]
                s_ = sm
                for c in range(2):
                    st(dve.memset(bblk[c][:], 0.0))
                dve.wait_ge(p_in, 16 * 16)
                dve.wait_ge(act_p, 1)
                st(TT(s_[1], re, s_[0], M))
                dve.sem_inc(trig, 1)
                ROUND = 1.5 * 2.0 ** 23
                C1, C2 = 6.28125, 0.0019350051879882812
                C3 = 2 * np.pi - C1 - C2
                st(TT(s_[2], im, s_[0], M))
                st(TS_(s_[5], s_[2], 1 / (2 * np.pi), ROUND, M, A_))
                st(TS_(s_[5], s_[5], ROUND, None, SB))
                for cst in (C1, C2, C3):
                    st(STT(s_[2], s_[5], -float(cst), s_[2], M, A_))
                st(TS_(s_[2], s_[2], 3.1415925, -3.1415925, ALU.min, ALU.max))
                dve.sem_inc(trig, 1)
                dve.wait_ge(act_p, 4)
                st(TT(s_[4], s_[4], s_[4], M))
                st(TS_(s_[4], s_[4], -2.0, 1.0, M, A_))
                st(dve.memset(pw[0][:, 0, :], 1.0))
                st(dve.memset(pw[1][:, 0, :], 0.0))
                st(TT(pw[0][:, 1, :], s_[1], s_[4], M))
                st(TT(pw[1][:, 1, :], s_[1], s_[3], M))
                ar, ai = pw[0][:, 1, :], pw[1][:, 1, :]
                st(TT(s_[0], re, re, M))
                st(TT(s_[2], im, im, M))
                st(TT(s_[0], s_[0], s_[2], A_))
                st(dve.reciprocal(s_[0], s_[0]))
                st(TS_(s_[1], ar, 1.0, None, SB))
                st(TT(s_[2], s_[1], re, M))
                st(TT(s_[3], ai, im, M))
                st(TT(s_[2], s_[2], s_[3], A_))
                st(TT(s_[6], s_[2], s_[0], M))
                st(TT(s_[2], ai, re, M))
                st(TT(s_[3], s_[1], im, M))
                st(TT(s_[2], s_[2], s_[3], SB))
                st(TT(s_[7], s_[2], s_[0], M))
                NBB = GROUPS * S5I
                fr = s_[6].unsqueeze(2).to_broadcast([P, GROUPS, S5I])
                fi = s_[7].unsqueeze(2).to_broadcast([P, GROUPS, S5I])
                tv = [x[:, 0:NBB].rearrange("p (g i) -> p g i", i=S5I) for x in (tmp, work)]
                st(TT(tv[0], fi, bb[0][:], M))
                st(TT(tv[1], fi, bb[1][:], M))
                for c in range(2):
                    st(TT(bb[c][:], fr, bb[c][:], M))
                st(TT(bb[0][:], bb[0][:], tv[1], SB))
                st(TT(bb[1][:], bb[1][:], tv[0], A_))
                for base, lo, cnt in ((1, 1, 1), (2, 1, 2), (4, 1, 4)):
                    pr = pw[0][:, base:base + 1, :].to_broadcast([P, cnt, GROUPS])
                    pi = pw[1][:, base:base + 1, :].to_broadcast([P, cnt, GROUPS])
                    xr, xi = pw[0][:, lo:lo + cnt, :], pw[1][:, lo:lo + cnt, :]
                    orr, oi = pw[0][:, base + lo:base + lo + cnt, :], pw[1][:, base + lo:base + lo + cnt, :]
                    a = tmp[:, 0:cnt * GROUPS].rearrange("p (a g) -> p a g", g=GROUPS)
                    st(TT(orr, pr, xr, M))
                    st(TT(a, pi, xi, M))
                    st(TT(orr, orr, a, SB))
                    st(TT(oi, pr, xi, M))
                    st(TT(a, pi, xr, M))
                    st(TT(oi, oi, a, A_))
                for b in range(2):
                    st(dve.tensor_copy(coef[:, 0, b, :], pw[0][:, SCH, :]))
                st(TS_(coef[:, 1, 0, :], pw[1][:, SCH, :], -1.0, None, M))
                st(dve.tensor_copy(coef[:, 1, 1, :], pw[1][:, SCH, :]))
                PER_A, PER_S, PER_B = 18, 8, 19
                PER = (PER_A + PER_B) * BPH + PER_S
                with dve.Fori(0, 2) as hf:
                    with dve.Fori(0, BPH) as i:
                        n = BPH * hf + i
                        st = Chain(dve, dve_s, 1, hf * PER + i * PER_A)
                        gs = bass.ds(n * GB, GB)
                        for c in range(2):
                            st(move(dve, ws[c][H1, :, ::-1], pw[c][H1, 0:SCH, gs].rearrange("p l g -> p g l")))
                            st(move(dve, ws[c][H2], pw[c][H2, 0:SCH, gs].rearrange("p l g -> p g l")))
                        dve.wait_ge(y_free, 3 * BPH * hf + 3)
                        dve.wait_ge(tr_free, 4 * n + 2)
                        w4 = [v3(wt[c], SCH) for c in range(2)]
                        x4 = tmp[:, 0:NW].rearrange("p (g a i) -> p g a i", g=GB, a=SCH)
                        wsb = [ws[c][:].unsqueeze(3).to_broadcast([P, GB, SCH, S5I]) for c in range(2)]
                        bbb = [bb[c][:, gs, :].unsqueeze(2).to_broadcast([P, GB, SCH, S5I]) for c in range(2)]
                        st(TT(w4[0], wsb[0], bbb[0], M))
                        st(TT(x4, wsb[1], bbb[1], M))
                        st(TT(w4[0], w4[0], x4, SB))
                        st(TT(w4[1], wsb[0], bbb[1], M))
                        st(TT(x4, wsb[1], bbb[0], M))
                        st(TT(w4[1], w4[1], x4, A_))
                        dve.sem_inc(wt_done, 1)
                        for g in range(GB):
                            dve.wait_ge(w_mm, GB * n + g + 1)
                            st(move(
                                dve,
                                hs[H2, :, :, bass.ds(GB * i + g, 1)].rearrange("p c r a -> p r (c a)"),
                                core.bank[g % 4][H2, 0:2 * NCH].rearrange("p (r c) -> p r c", r=2)[:, :, ::-1]))
                            dve.sem_inc(w_free_b, 1)
                        assert st.n == PER_A, st.n
                    st = Chain(dve, dve_s, 1, hf * PER + BPH * PER_A)
                    dve.wait_ge(w_free_f, GB * BPH * (hf + 1) + 4)
                    gh = bass.ds(GH * hf, GH)
                    dve.wait_ge(saved, NCH * hf + 1)
                    st(dve.memset(cur[0][H1], 0.0))
                    st(move(dve, cur[0][H2], init[H2, :, gh]))
                    st(move(dve, cofs[0][:], coef[:, 0, :, gh]))
                    st(move(dve, cofs[1][:], coef[:, 1, :, gh]))

                    def steps(lo, cnt, it=None):
                        for k in range(lo, lo + cnt):
                            sl = 24 * it + k if it is not None else k
                            m = NCH * hf + sl
                            a, b = cur[k % 2], cur[1 - k % 2]
                            TT(t0, cofs[0][:], a[:], M).then_inc(prod, 1)
                            TT(t1, cofs[1][:], a[:, ::-1, :], M).then_inc(prod, 1)
                            dve.wait_ge(prod, 2 * m + 1)
                            src = hs[:, bass.ds(sl, 1), :, :].rearrange("p a r g -> p (a r) g") if it is not None else hs[:, sl, :, :]
                            TT(t0, t0, src, A_).then_inc(w_used, 1)
                            dve.wait_ge(prod, 2 * m + 2)
                            dve.wait_ge(w_used, m + 1)
                            dve.wait_ge(saved, m + 1)
                            TT(b[:], t0, t1, A_).then_inc(new, 1)
                            dve.wait_ge(new, m + 1)

                    steps(0, NCC)
                    st(move(dve, fins[H1, :, gh], cur[0][H1]))
                    st(move(dve, cur[0][H1], init[H1, :, gh]))
                    steps(NCC, 24 - NCC)
                    dve.sem_inc(turn, 1)
                    with dve.Fori(1, NCH // 24 - 1) as it:
                        steps(0, 24, it)
                    steps(120, NCS - 120)
                    st(dve.memset(cur[0][H2], 0.0))
                    steps(NCS, NCC)
                    st(move(dve, fins[H2, :, gh], cur[0][H2]))
                    dve.sem_inc(scan_done, 1)
                    assert st.n == PER_S, st.n
                    dve.wait_ge(ada_used, NA * hf + NA + 4)
                    dve.wait_ge(S.proj_done, PROJ0 + 3 * UNITS_U + 3 * UNITS_G // 2 * (hf + 1))
                    for b in range(BPH):
                        n = BPH * hf + b
                        ca = ca_set[b % 2]
                        st = Chain(dve, dve_s, 1, hf * PER + BPH * PER_A + PER_S + b * PER_B)
                        gs = bass.ds(n * GB, GB)
                        dve.wait_ge(k_free, 3 * n + 3)
                        dve.wait_ge(y_free, 3 * n if b >= 2 else 3 * BPH * hf + 3)
                        for c in range(2):
                            st(move(dve, cq[c][H1], pw[c][H1, :, gs].rearrange("p l g -> p g l")))
                            st(move(dve, cq[c][H2, :, 0:1], pw[c][H2, 0:1, gs].rearrange("p l g -> p g l")))
                            st(move(dve, cq[c][H2, :, SCH:0:-1], pw[c][H2, 1:LAGS, gs].rearrange("p l g -> p g l")))
                            st(move(dve, bblk[c][H1, :, 0:S5I], bb[c][H1, gs, :]))
                            st(move(dve, bblk[c][H2, :, S5I:2 * S5I], bb[c][H2, gs, :]))
                            st(move(dve, bdup[c][:].rearrange("p g (a i) -> p g a i", a=2),
                                               bb[c][:, gs, :].unsqueeze(2).to_broadcast([P, GB, 2, S5I])))
                        c4 = [v3(ca[c], LAGS) for c in range(2)]
                        x4 = v3(tmp[:], LAGS)
                        cqb = [cq[c][:].unsqueeze(3).to_broadcast([P, GB, LAGS, S5I]) for c in range(2)]
                        ccb = [cc[c][:, gs, :].unsqueeze(2).to_broadcast([P, GB, LAGS, S5I]) for c in range(2)]
                        st(TT(c4[0], cqb[0], ccb[0], M))
                        st(TT(x4, cqb[1], ccb[1], M))
                        st(TT(c4[0], c4[0], x4, SB))
                        st(TT(c4[1], cqb[0], ccb[1], M))
                        st(TT(x4, cqb[1], ccb[0], M))
                        st(TT(c4[1], c4[1], x4, A_))
                        st(TS_(ca[1], ca[1], -1.0, None, M))
                        dve.sem_inc(ca_done, 1)
                        assert st.n == PER_B, st.n
                dve.wait_ge(bada_in, 16)
                dve.wait_ge(hn_done, NBATCH)
                rest = mod[:, NMOD1:6 * KD, :]
                dve.tensor_tensor(rest, rest, bada[:, NMOD1:6 * KD].unsqueeze(2).to_broadcast([P, 6 * KD - NMOD1, 2]),
                                  ALU.add).then_inc(bias_done, 1)
                dve.wait_ge(bias_done, 1)
                dve.tensor_scalar(mod[:, 4 * KD:5 * KD, :], mod[:, 4 * KD:5 * KD, :], 1.0, None, ALU.add)


def merge(core, mod, x1):
    nc, dram = core.nc, core.dram
    with ExitStack() as ctx:
        ctx.callback(core.end_stage)

        def sb(name, shape, dt=F32):
            return ctx.enter_context(nc.sbuf_tensor(name, shape, dt))

        def sem(name):
            return core.sem(name)

        USED0 = 9
        GLU, LRU, GLA_, S5_, OUT = range(5)
        ORDER = [list(range(8)), [8, 9, 10, 11, 0, 1, 2, 3, 4, 5, 6, 7], [8, 9, 10, 11, 0, 1, 2, 3],
                 [4, 5, 6, 7, 8, 9, 10, 11], list(range(8))]
        USED = [0, 64, 160, 224, 288]
        FILL = [0, 8, 20, 28, 36]
        UNIT = [0, 8, 24, 32, 40]
        S = Stream(core, ctx, "mrg")
        yhi = sb("yhi", [P, LBLK, T], F32R)
        ylo = sb("ylo", [P, LBLK, T], F32R)
        yin = [sb(f"yin{s}", [P, T]) for s in range(4)]
        gt = [sb(f"gt{s}", [P, T]) for s in range(2)]
        (used, filled, hi_f, glu_done, mix_done, dve_s, merged_done) = (
            sem(n) for n in ("used", "filled", "hi_f", "glu_done", "mix_done", "dve_s", "merged_done"))
        yin_in = [sem(f"yin_in{s}") for s in range(4)]
        y_out = [sem(f"y_out{s}") for s in range(2)]
        gt_in = [sem(f"gt_in{s}") for s in range(2)]

        loads = []
        for ph, name, off in ((LRU, "y_lru", 1), (GLA_, "y_gla", 2), (S5_, "y_s5", 0)):
            for k, slot in enumerate(ORDER[ph]):
                tile = slot if ph == LRU else k
                loads.append((name, tile + off, slot))

        def last_use(ph, slot):
            k = len(ORDER[ph])
            return USED0 + USED[ph] + 7 * k + ORDER[ph].index(slot) + 1

        free_at = ([None] * 4 + [last_use(GLU, s) for s in range(8)] + [last_use(LRU, s) for s in (8, 9, 10, 11, 0, 1, 2, 3)]
                   + [last_use(LRU, s) for s in (4, 5, 6, 7)] + [last_use(GLA_, s) for s in (8, 9, 10, 11)])

        def turned(tile):
            return tile[:].rearrange("p (t c) -> p c t", t=SCH)

        def issue(act, n):
            if n < len(loads):
                name, tile, _ = loads[n]
                act.dma_start(yin[n % 4][:], dram[name][tile]).then_inc(yin_in[n % 4], 16)

        def fill_act(act, n, src=None, slot=None, f=None):
            if src is None:
                _, _, slot = loads[n]
                f = n + 8
                if n:
                    act.wait_ge(filled, f)
                    issue(act, n + 3)
                act.wait_ge(yin_in[n % 4], 16 * (KD // 4 + n // 4 + 1))
                if free_at[n] is not None:
                    act.wait_ge(used, free_at[n])
                src = yin[n % 4][:]
            dst = yhi[:, slot, :]
            if len(src.shape) == 3:
                dst = dst.rearrange("p (c t) -> p c t", t=SCH)
            act.activation(dst, src, ACT.Copy).then_inc(hi_f, 1)

        def fill_dve(dve, n, src=None, slot=None, f=None):
            if src is None:
                _, _, slot = loads[n]
                f, src = n + 8, yin[n % 4][:]
            dve.wait_ge(hi_f, f + 1)
            lo, hi = ylo[:, slot, :], yhi[:, slot, :].bitcast(F32)
            if len(src.shape) == 3:
                lo, hi = (x.rearrange("p (c t) -> p c t", t=SCH) for x in (lo, hi))
            dve.tensor_tensor(lo, src, hi, ALU.subtract).then_inc(filled, 1)

        with nc.Block() as block:
            @block.sync
            def _(sync):
                S.prime(sync)
                sync.sem_inc(used, USED0)
                with sync.Fori(0, 4) as i:
                    for j in range(2):
                        S.load(sync, 2 * i + j, j, dram["w_glu"][bass.ds(2 * i + j, 1)].rearrange("a p n -> (a p) n"))

                def tile_of(src, idx, q, par, mixed=None):
                    if mixed is None:
                        sync.wait_ge(S.bank_free[par], 3 * q + 3)
                    else:
                        sync.wait_ge(mix_done, mixed)
                    sync.dma_start(gt[par][:], dram[src][bass.ds(idx, 1)].rearrange("a p n -> (a p) n")).then_inc(gt_in[par], 16)

                for s in range(2):
                    sync.wait_ge(y_out[s], 16 * (KD // 2))
                with sync.Fori(0, 4) as i:
                    for j in range(2):
                        S.load(sync, UNIT[LRU] + 4 * i + 2 * j, 0, dram["w_br_lru"][bass.ds(2 * i + j, 1), :, 0:UW].rearrange("a p n -> (a p) n"))
                        S.load(sync, UNIT[LRU] + 4 * i + 2 * j + 1, 1, dram["w_br_lru"][bass.ds(2 * i + j, 1), :, UW:UW + 4 * P].rearrange("a p n -> (a p) n"), 4 * P)
                        tile_of("gates", 2 * KD + 2 * i + j, 4 + i, j)
                for ph, w, src, t0 in ((GLA_, "w_br_gla", "gates", 0), (S5_, "w_br_s5", "gates", KD), (OUT, "w_out", "x_res", 0)):
                    with sync.Fori(0, 4) as i:
                        for j in range(2):
                            S.load(sync, UNIT[ph] + 2 * i + j, j, dram[w][bass.ds(2 * i + j, 1)].rearrange("a p n -> (a p) n"))
                            tile_of(src, t0 + 2 * i + j, 4 * ph + i, j, None if ph != OUT else 2 * i + j + 1)

            @block.gpsimd
            def _(pool):
                def split(u, par, q, used_at, width=UW):
                    S.split(pool, u, par, q, None, width, (used, used_at + USED0))

                with pool.Fori(0, 4) as i:
                    for j in range(2):
                        split(2 * i + j, j, i, 16 * i + 8 * j - 8)
                with pool.Fori(0, 4) as i:
                    for j in range(2):
                        before = USED[LRU] + 24 * i + 12 * j
                        split(UNIT[LRU] + 4 * i + 2 * j, 0, 4 + 2 * i + j, before - 4)
                        split(UNIT[LRU] + 4 * i + 2 * j + 1, 1, 4 + 2 * i + j, before, 4 * P)
                for ph in (GLA_, S5_, OUT):
                    with pool.Fori(0, 4) as i:
                        for j in range(2):
                            extra = 4 if ph == GLA_ and j == 0 else 0
                            split(UNIT[ph] + 2 * i + j, j, UNIT[ph] // 2 + i, USED[ph] + 16 * i + 8 * j - 8 + extra)

            @block.tensor
            def _(pe):
                def tile_product(ph, i, j):
                    order = ORDER[ph]
                    pe.wait_ge(S.bank_free[j], 12 * ph + 3 * i + 3)
                    for k, slot in enumerate(order):
                        if ph == LRU:
                            u, par, kk = UNIT[ph] + 4 * i + 2 * j + k // 8, k // 8, k % 8
                        else:
                            u, par, kk = UNIT[ph] + 2 * i + j, j, k
                        if kk == 0:
                            pe.wait_ge(S.split_done, u + 3)
                        pe.wait_ge(filled, FILL[ph] + k + 1)
                        for b in range(NB):
                            out = core.bank[3 * j + b][:, 0:BW]
                            cols = slice(b * BW, (b + 1) * BW)
                            w = slice(kk * P, (kk + 1) * P)
                            for n, (wt, r) in enumerate(((S.hi, yhi), (S.hi, ylo), (S.lo, yhi))):
                                mm = pe.matmul(out, wt[par][:, w], r[:, slot, cols], start=(k == 0 and n == 0),
                                               stop=(k == len(order) - 1 and n == 2))
                        mm.then_inc(used, 1)

                for ph in range(5):
                    with pe.Fori(0, 4) as i:
                        for j in range(2):
                            tile_product(ph, i, j)

            @block.scalar
            def _(act):
                def issue_s5(k):
                    act.dma_start(yin[k % 4][:], dram["y_d"][k * P:(k + 1) * P].rearrange("p t c -> p (t c)")).then_inc(yin_in[k % 4], 16)

                for k in range(4):
                    issue_s5(k)
                for k in range(KD):
                    if k >= 2 and k + 2 < KD:
                        act.wait_ge(filled, k - 1)
                        issue_s5(k + 2)
                    act.wait_ge(yin_in[k % 4], 16 * (k // 4 + 1))
                    fill_act(act, None, turned(yin[k % 4]), k, k)
                for n in range(4):
                    act.wait_ge(filled, n + 5)
                    issue(act, n)
                for m in range(KD):
                    if m < 2:
                        act.wait_ge(filled, KD)
                    else:
                        act.wait_ge(y_out[m % 2], 16 * (m // 2))
                    act.wait_ge(used, USED0 + USED[GLU] + 8 * (m + 1))
                    for b in range(NB):
                        act.activation(gt[m % 2][:, b * BW:(b + 1) * BW], core.bank[3 * (m % 2) + b][:, 0:BW],
                                       ACT.Sigmoid).then_inc(S.bank_free[m % 2], 1)
                    if m < 4:
                        fill_act(act, m)
                    act.wait_ge(glu_done, m + 1)
                    act.dma_start(dram["y_s5"][m], gt[m % 2][:]).then_inc(y_out[m % 2], 16)
                for n in range(4, 12):
                    fill_act(act, n)
                for n in range(12, 28):
                    fill_act(act, n)
                for m in range(KD):
                    act.wait_ge(merged_done, m + 1)
                    if m >= 4:
                        act.wait_ge(used, last_use(S5_, m))
                    fill_act(act, None, x1[:, m, :], m, FILL[OUT] + m)
                for m in range(KD):
                    act.wait_ge(used, USED0 + USED[OUT] + 8 * (m + 1))
                    if m >= 2:
                        act.wait_ge(mix_done, m + 1)
                    mt = yin[m % 2]
                    for b in range(NB):
                        bk = core.bank[3 * (m % 2) + b]
                        if b == 0:
                            act.activation(mt[:, 0:TC], bk[:, 0:TC], ACT.Identity, scale=mod[:, 2 * KD + m, 0:1])
                        c0 = TC if b == 0 else b * BW
                        act.activation(mt[:, c0:(b + 1) * BW], bk[:, c0 - b * BW:BW], ACT.Identity,
                                       scale=mod[:, 2 * KD + m, 1:2]).then_inc(S.bank_free[m % 2], 1)

            @block.vector
            def _(dve):
                st = Chain(dve, dve_s)
                for k in range(KD):
                    dve.wait_ge(yin_in[k % 4], 16 * (k // 4 + 1))
                    fill_dve(dve, None, turned(yin[k % 4]), k, k)
                for m in range(KD):
                    dve.wait_ge(S.bank_free[m % 2], 3 * (m // 2) + 6)
                    gm = gt[m % 2][:]
                    tmp = x1[:, m % 2, :]
                    st(dve.tensor_tensor(tmp, yhi[:, m, :].bitcast(F32), ylo[:, m, :].bitcast(F32), ALU.add))
                    dve.tensor_tensor(gm, gm, tmp, ALU.mult).then_inc(glu_done, 1)
                    dve.wait_ge(glu_done, m + 1)
                    if m < 4:
                        fill_dve(dve, m)
                for n in range(4, 12):
                    fill_dve(dve, n)

                def gated(ph, m):
                    k = len(ORDER[ph])
                    par = m % 2
                    dve.wait_ge(used, USED0 + USED[ph] + k * (m + 1))
                    dve.wait_ge(gt_in[par], 16 * (4 * (ph - 1) + m // 2 + 1))
                    for b in range(NB):
                        cols = slice(b * BW, (b + 1) * BW)
                        bk, dst, g = core.bank[3 * par + b][:, 0:BW], x1[:, m, cols], gt[par][:, cols]
                        if ph == LRU:
                            ins = dve.tensor_tensor(dst, bk, g, ALU.mult)
                            ins.then_inc(S.bank_free[par], 1)
                        else:
                            st(dve.tensor_tensor(g, bk, g, ALU.mult))
                            dve.tensor_tensor(dst, dst, g, ALU.add).then_inc(S.bank_free[par], 1)
                    dve.wait_ge(S.bank_free[par], 3 * (4 * ph + m // 2) + 6)
                    if ph == S5_:
                        dve.sem_inc(merged_done, 1)

                for m in range(KD):
                    if m == KD - 1:
                        for n in range(12, 20):
                            fill_dve(dve, n)
                    gated(LRU, m)
                for m in range(KD):
                    if m == KD - 1:
                        for n in range(24, 28):
                            fill_dve(dve, n)
                    gated(GLA_, m)
                    if m < 4:
                        fill_dve(dve, 20 + m)
                for m in range(KD):
                    gated(S5_, m)
                    if m >= KD - 2:
                        dve.sem_inc(mix_done, 1)
                    if m < 4:
                        fill_dve(dve, None, x1[:, m, :], m, FILL[OUT] + m)
                    if m == KD - 2:
                        for n in range(4, KD - 1):
                            fill_dve(dve, None, x1[:, n, :], n, FILL[OUT] + n)
                fill_dve(dve, None, x1[:, KD - 1, :], KD - 1, FILL[OUT] + KD - 1)
                for m in range(KD):
                    par = m % 2
                    dve.wait_ge(S.bank_free[par], 3 * (4 * OUT + m // 2) + 6)
                    dve.wait_ge(gt_in[par], 16 * (4 * (OUT - 1) + m // 2 + 1))
                    if m == 0:
                        dve.wait_ge(filled, FILL[OUT] + KD)
                    dve.scalar_tensor_tensor(x1[:, m, :], gt[par][:], ALPHA, yin[par][:], ALU.mult, ALU.add).then_inc(mix_done, 1)


def layer_norm(core, x, gain, bias, name, store=None):
    nc, dram = core.nc, core.dram
    with ExitStack() as ctx:
        ctx.callback(core.end_stage)

        def sb(n, shape, dt=F32):
            return ctx.enter_context(nc.sbuf_tensor(f"{name}_{n}", shape, dt))

        def sem(n):
            return core.sem(f"{name}_{n}")

        ones = sb("ones", [P, P])
        eps = sb("eps", [P, 1])
        g, be = sb("g", [P, KD]), sb("b", [P, KD])
        sq = [sb(f"sq{b}", [P, KD, BW]) for b in range(NB)]
        sd = [sb(f"sd{b}", [P, BW]) for b in range(NB)]
        const_done, g_in, mean_mm, cent_done, sq_done, var_mm, sd_done, dve_s, out_done, y_out = (
            sem(n) for n in ("const_done", "g_in", "mean_mm", "cent_done", "sq_done", "var_mm", "sd_done", "dve_s",
                             "out_done", "y_out"))
        with nc.Block() as block:
            @block.gpsimd
            def _(pool):
                pool.memset(ones[:], 1.0 / D).then_inc(const_done, 1)
                pool.memset(eps[:], LN_EPS).then_inc(const_done, 1)

            @block.sync
            def _(sync):
                sync.dma_start(g[:], dram[gain]).then_inc(g_in, 16)
                sync.dma_start(be[:], dram[bias]).then_inc(g_in, 16)
                if store is not None:
                    for b in range(NB):
                        sync.wait_ge(out_done, b + 1)
                        cols = slice(b * BW, (b + 1) * BW)
                        sync.dma_start(dram[store].rearrange("k p t -> p k t")[:, :, cols], x[:, :, cols]).then_inc(y_out, 16)
                    sync.wait_ge(y_out, 16 * NB)

            @block.tensor
            def _(pe):
                pe.wait_ge(const_done, 2)
                for b in range(NB):
                    for k in range(KD):
                        mm = pe.matmul(core.bank[b][:, 0:BW], ones[:], x[:, k, b * BW:(b + 1) * BW],
                                       start=(k == 0), stop=(k == KD - 1))
                    mm.then_inc(mean_mm, 1)
                for b in range(NB):
                    pe.wait_ge(sq_done, b + 1)
                    for k in range(KD):
                        mm = pe.matmul(core.bank[3 + b][:, 0:BW], ones[:], sq[b][:, k, :],
                                       start=(k == 0), stop=(k == KD - 1))
                    mm.then_inc(var_mm, 1)

            @block.scalar
            def _(act):
                act.wait_ge(const_done, 2)
                for b in range(NB):
                    act.wait_ge(cent_done, b + 1)
                    act.activation(sq[b][:], x[:, :, b * BW:(b + 1) * BW], ACT.Square).then_inc(sq_done, 1)
                for b in range(NB):
                    act.wait_ge(var_mm, b + 1)
                    act.activation(sd[b][:], core.bank[3 + b][:, 0:BW], ACT.Sqrt, bias=eps[:, 0:1]).then_inc(sd_done, 1)

            @block.vector
            def _(dve):
                st = Chain(dve, dve_s)
                for b in range(NB):
                    xb = x[:, :, b * BW:(b + 1) * BW]
                    dve.wait_ge(mean_mm, b + 1)
                    dve.tensor_tensor(xb, xb, core.bank[b][:, 0:BW].unsqueeze(1).to_broadcast([P, KD, BW]),
                                      ALU.subtract).then_inc(cent_done, 1)
                dve.wait_ge(g_in, 32)
                for b in range(NB):
                    xb = x[:, :, b * BW:(b + 1) * BW]
                    dve.wait_ge(sd_done, b + 1)
                    dve.wait_ge(sq_done, b + 1)
                    st(dve.reciprocal(sd[b][:], sd[b][:]))
                    st(dve.tensor_tensor(xb, xb, sd[b][:].unsqueeze(1).to_broadcast([P, KD, BW]), ALU.mult))
                    for k in range(KD):
                        st.mark(dve.tensor_scalar(x[:, k, b * BW:(b + 1) * BW], x[:, k, b * BW:(b + 1) * BW],
                                                  g[:, k:k + 1], be[:, k:k + 1], ALU.mult, ALU.add))
                    st.sync()
                    dve.sem_inc(out_done, 1)


def mlp(core, mod, x1):
    nc, dram = core.nc, core.dram
    with ExitStack() as ctx:
        ctx.callback(core.end_stage)

        def sb(name, shape, dt=F32):
            return ctx.enter_context(nc.sbuf_tensor(name, shape, dt))

        def sem(name):
            return core.sem(name)

        UG = 2 * HG
        GPG = NB * (HG + KD)
        S = Stream(core, ctx, "mlp")
        hhi = sb("h2hi", [P, KD, T], F32R)
        hlo = sb("h2lo", [P, KD, T], F32R)
        ahi = sb("ahi", [P, HG, T], F32R)
        alo = sb("alo", [P, HG, T], F32R)
        rl = [sb(f"rl{s}", [P, T]) for s in range(2)]
        sq = sb("mlp_sq", [P, BW])
        (h_done, hi_done, lo_done, scaled, ahi_done, alo_done, alo_free, dve_s) = (
            sem(n) for n in ("h_done", "hi_done", "lo_done", "scaled", "ahi_done", "alo_done", "alo_free", "mlp_dve"))

        out_free = [sem(f"out_free{s}") for s in range(2)]

        def cum(j):
            return NB * (j + 1) if j < HG else NB * HG + 2 * NB * (j - HG + 1)

        with nc.Block() as block:
            @block.sync
            def _(sync):
                S.prime(sync)
                sync.sem_inc(alo_free, 2 * NB)
                sync.sem_inc(out_free[0], NB)
                sync.sem_inc(out_free[1], NB)
                with sync.Fori(0, NHG) as i:
                    for j in range(UG):
                        u = UG * i + j
                        S.load(sync, u, j % 2, dram["mlp_units"][bass.ds(u, 1)].rearrange("a p n -> (a p) n"))

            @block.gpsimd
            def _(pool):
                with pool.Fori(0, NHG) as i:
                    for j in range(UG):
                        before = cum(j - 2) if j >= 2 else (cum(UG + j - 2) - GPG)
                        S.split(pool, UG * i + j, j % 2, UG // 2 * i + j // 2, GPG * i + before)

            @block.tensor
            def _(pe):
                pe.wait_ge(lo_done, KD)
                with pe.Fori(0, NHG) as i:
                    for j in range(HG):
                        free = (out_free[j], NB * KD // 2 * i) if j < 2 else (S.bank_free[j % 2], 3 + NB * HG // 2 * i)
                        S.project(pe, UG * i + j, j % 2, None, hhi, hlo, free=free)
                    for j in range(HG, UG):
                        pe.wait_ge(S.split_done, UG * i + j + 3)
                        for e in range(2):
                            m = 2 * (j - HG) + e
                            if m < 2:
                                pe.wait_ge(S.bank_free[e], 3 + NB * HG // 2 * (i + 1))
                            else:
                                pe.wait_ge(out_free[e], NB * KD // 2 * i + NB * (m // 2) + NB)
                            for k in range(HG):
                                if m == 0:
                                    pe.wait_ge(alo_done, NB * HG * i + NB * (k + 1))
                                w = slice((HG * e + k) * P, (HG * e + k + 1) * P)
                                for b in range(NB):
                                    out = core.bank[3 * e + b][:, 0:BW]
                                    cols = slice(b * BW, (b + 1) * BW)
                                    for n, (wt, r) in enumerate(((S.hi, ahi), (S.hi, alo), (S.lo, ahi))):
                                        mm = pe.matmul(out, wt[j % 2][:, w], r[:, k, cols], start=(k == 0 and n == 0),
                                                       stop=(k == HG - 1 and n == 2))
                                    if k == HG - 1:
                                        mm.then_inc(S.proj_done, 1)

            @block.scalar
            def _(act):
                for k in range(KD):
                    act.wait_ge(h_done, k + 1)
                    act.activation(hhi[:, k, :], rl[k % 2][:], ACT.Copy).then_inc(hi_done, 1)
                act.wait_ge(lo_done, KD)
                with act.Fori(0, NHG) as i:
                    for j in range(HG):
                        for b in range(NB):
                            cols = slice(b * BW, (b + 1) * BW)
                            act.wait_ge(S.proj_done, GPG * i + NB * j + b + 1 + PROJ0)
                            act.wait_ge(alo_free, NB * HG * i + NB * j + b + 1)
                            act.activation(rl[j % 2][:, cols], core.bank[3 * (j % 2) + b][:, 0:BW], ACT.Relu).then_inc(S.bank_free[j % 2], 1)
                            act.wait_ge(S.bank_free[j % 2], 3 + NB * (HG // 2 * i + j // 2) + b + 1)
                            act.activation(ahi[:, j, cols], rl[j % 2][:, cols], ACT.Square).then_inc(ahi_done, 1)

            @block.vector
            def _(dve):
                for k in range(KD):
                    if k >= 2:
                        dve.wait_ge(lo_done, k - 1)
                    for c, cols in ((0, slice(0, TC)), (1, slice(TC, T))):
                        ins = dve.tensor_scalar(rl[k % 2][:, cols], x1[:, k, cols], mod[:, 4 * KD + k, c:c + 1],
                                                mod[:, 3 * KD + k, c:c + 1], ALU.mult, ALU.add)
                    ins.then_inc(h_done, 1)
                    dve.wait_ge(hi_done, k + 1)
                    dve.tensor_tensor(hlo[:, k, :], rl[k % 2][:], hhi[:, k, :].bitcast(F32), ALU.subtract).then_inc(lo_done, 1)
                for k in range(KD):
                    dve.tensor_scalar(x1[:, k, :], x1[:, k, :], ALPHA, None, ALU.mult).then_inc(scaled, 1)
                dve.wait_ge(scaled, KD)
                PER = NB * HG
                with dve.Fori(0, NHG) as i:
                    st = Chain(dve, dve_s, i, PER)
                    for j in range(HG):
                        for b in range(NB):
                            cols = slice(b * BW, (b + 1) * BW)
                            dve.wait_ge(ahi_done, PER * i + NB * j + b + 1)
                            st(dve.tensor_tensor(sq[:], rl[j % 2][:, cols], rl[j % 2][:, cols], ALU.mult))
                            dve.tensor_tensor(alo[:, j, cols], sq[:], ahi[:, j, cols].bitcast(F32),
                                              ALU.subtract).then_inc(alo_done, 1)
                            dve.wait_ge(alo_done, PER * i + NB * j + b + 1)
                            dve.sem_inc(alo_free, 1)
                    st.end()
                    for m in range(KD):
                        par = m % 2
                        for b in range(NB):
                            bk = core.bank[3 * par + b]
                            dve.wait_ge(S.proj_done, GPG * i + NB * HG + NB * m + b + 1 + PROJ0)
                            c0 = b * BW
                            if b == 0:
                                dve.scalar_tensor_tensor(x1[:, m, 0:TC], bk[:, 0:TC], mod[:, 5 * KD + m, 0:1], x1[:, m, 0:TC],
                                                         ALU.mult, ALU.add)
                                c0 = TC
                            dve.scalar_tensor_tensor(x1[:, m, c0:(b + 1) * BW], bk[:, c0 - b * BW:BW],
                                                     mod[:, 5 * KD + m, 1:2], x1[:, m, c0:(b + 1) * BW],
                                                     ALU.mult, ALU.add).then_inc(out_free[par], 1)


def build(nc, dram):
    with ExitStack() as ctx:
        core = Core(nc, ctx, dram)
        mod = ctx.enter_context(nc.sbuf_tensor("mod", [P, 6 * KD, 2], F32))
        csilu = ctx.enter_context(nc.sbuf_tensor("csilu", [P, KD, 2], F32))
        with ExitStack() as hctx:
            hhi = hctx.enter_context(nc.sbuf_tensor("hhi", [P, KD, T], F32R))
            hlo = hctx.enter_context(nc.sbuf_tensor("hlo", [P, KD, T], F32R))
            modulate(core, hhi, hlo, mod, csilu)
            lru(core, hhi, hlo)
            gla(core, hhi, hlo)
            s5_and_gates(core, hhi, hlo, mod, csilu)
        x1 = ctx.enter_context(nc.sbuf_tensor("x1", [P, KD, T], F32))
        merge(core, mod, x1)
        layer_norm(core, x1, "ln1_g", "ln1_b", "ln1")
        mlp(core, mod, x1)
        layer_norm(core, x1, "ln2_g", "ln2_b", "ln2", store="y")


def units(w, tiles):
    k, m = w.shape
    return np.ascontiguousarray(w.reshape(k // P, P, m // P, P).transpose(2, 1, 0, 3)).reshape(m // P, P, k)[tiles]


def tables():
    quarter = D // 4
    omega = 1.0 / (np.float32(10000.0) ** (np.arange(quarter, dtype=np.float32) / np.float32(quarter)))
    omega = omega.astype(np.float32)

    def table(n):
        a = (np.arange(n, dtype=np.float32)[:, None] * omega).astype(np.float32)
        t = np.concatenate([np.sin(a), np.cos(a)], axis=1).astype(np.float32)
        return np.ascontiguousarray(t.T.reshape(KD // 2, P, n).transpose(1, 0, 2))

    s, t = np.arange(P)[:, None], np.arange(P)[None, :]
    same = s // GCH == t // GCH
    keep = np.stack([same & (s <= t), same & (s >= t)], axis=1).astype(np.int32)
    return {"pos_r": table(ROWS), "pos_c": table(GRID_W), "keep": keep, "ident": np.eye(P, dtype=np.float32)}


def layout(a):
    f = {n: np.asarray(v) for n, v in a.items()}
    cols = np.cumsum((0, 512, 512, 1024, 1024, 32, 1024, 1536, 1536, 3072))
    w_in = f["w_in"][0]
    part = [w_in[:, cols[n]:cols[n + 1]] for n in range(9)]
    q, k, v, r, glr, u, lx, ly, gates = part
    out = tables()
    out["cvec"] = np.ascontiguousarray(np.stack([f["c_ctx"], f["c"][0]], axis=1).reshape(KD, P, 2).transpose(1, 0, 2))
    out["bada"] = np.ascontiguousarray(f["b_ada"][0].reshape(6 * KD, P).T)
    out["w_ada"] = units(f["w_ada"][0], slice(None))
    x = np.concatenate([f["x_prompt"][0], f["x_sample"][0]], axis=0)
    out["x_t"] = np.ascontiguousarray(x.T).reshape(KD, P, T)
    ulx, uly, ug = units(lx, slice(None)), units(ly, slice(None)), units(gates, slice(None))
    out["lru_units"] = np.stack([ulx, uly], axis=1).reshape(2 * LBLK, P, UW)
    wa, wi = f["lru_w_a"][0], f["lru_w_i"][0]
    out["lru_w"] = np.ascontiguousarray(np.stack([wa[0], wi[0], wa[1], wi[1]], axis=1).transpose(0, 2, 1, 3)).reshape(LBLK, P, 4 * P)

    def rows(m):
        return m.reshape(-1, LBLK, P)

    prm = np.concatenate([rows(f["lru_conv_w"][0]), rows(f["lru_conv_b"][0]), rows(f["lru_b_a"][0]),
                          rows(f["lru_b_i"][0]), rows(f["lru_lam"][0]), rows(f["state_lru"][0, 0])], axis=0)
    out["lru_params"] = np.ascontiguousarray(prm.transpose(2, 1, 0))
    pad = np.zeros((D, P), np.float32)
    pad[:, 0:RANK], pad[:, 32:32 + RANK] = glr[:, 0:RANK], glr[:, RANK:]
    uq, uk, uv, ur = (units(m, slice(None)) for m in (q, k, v, r))
    out["gla_units"] = np.concatenate([units(pad, slice(None))] + [
        np.stack([uq[h], uk[h], uv[2 * h], uv[2 * h + 1], ur[2 * h], ur[2 * h + 1]]) for h in range(HEADS)])
    wgate = np.zeros((64, HEADS, DK), np.float32)
    for e in range(2):
        wgate[32 * e:32 * e + RANK] = f["gla_w_gate"][0, e].reshape(RANK, HEADS, DK)
    out["gla_wgate"] = wgate
    prm = np.concatenate([f["gla_b_gate"][0].reshape(2, HEADS, P),
                          f["gla_norm_g"][0].reshape(HEADS, 2, P).transpose(1, 0, 2)], axis=0)
    out["gla_params"] = np.ascontiguousarray(prm.transpose(2, 1, 0))
    out["s5_units"] = np.concatenate([units(u, slice(None)), ug])
    out["s5_lam"] = np.ascontiguousarray(np.stack([f["s5_lam_re"][0], f["s5_lam_im"][0]]).transpose(0, 1, 3, 2)).reshape(2, P, GROUPS)
    out["s5_step"] = f["s5_log_step"][0]
    out["s5_b"] = np.ascontiguousarray(np.stack([f["s5_b_re"][0], f["s5_b_im"][0]]).transpose(0, 2, 1, 3))
    out["s5_c"] = np.ascontiguousarray(np.stack([f["s5_c_re"][0], f["s5_c_im"][0]]).transpose(0, 3, 1, 2))
    skip = np.zeros((NBATCH, S5I, GB, S5I), np.float32)
    for i in range(S5I):
        skip[:, i, :, i] = f["s5_d"][0].reshape(NBATCH, GB, S5I)[:, :, i]
    out["s5_skip"] = skip
    st = np.stack([f["state_s5_re"][0, 0], f["state_s5_im"][0, 0]])
    out["s5_init"] = np.ascontiguousarray(st.transpose(1, 3, 0, 2)).reshape(P, 2, GROUPS)
    order = [LBLK - HG + k for k in range(HG)] + list(range(LBLK - HG))
    w = f["w_br_lru"][0].reshape(LBLK, P, D)[order].reshape(LBLK * P, D)
    out["w_br_lru"] = units(w, slice(None))
    for name in ("w_br_gla", "w_br_s5", "w_out"):
        out[name] = units(f[name][0], slice(None))
    out["w_glu"] = units(f["s5_w_glu"][0], slice(None))

    def columns(vec):
        return np.ascontiguousarray(vec.reshape(KD, P).T)

    for name in ("ln1_g", "ln1_b", "ln2_g", "ln2_b"):
        out[name] = columns(f[name][0])
    win = units(f["w_mlp_in"][0], slice(None)).reshape(NHG, HG, P, UW)
    wout = f["w_mlp_out"][0].reshape(NHG, HG, P, KD, P).transpose(0, 3, 2, 1, 4).reshape(NHG, KD // 2, 2, P, HG * P)
    wout = wout.transpose(0, 1, 3, 2, 4).reshape(NHG, HG, P, UW)
    out["mlp_units"] = np.concatenate([win, wout], axis=1).reshape(NHG * 2 * HG, P, UW)
    out["state_gla"] = f["state_gla"][0, 0].reshape(2 * HEADS, DK, DV)
    return out


SCRATCH = {"x_res": (KD, P, T), "gates": (3 * KD, P, T), "y_lru": (LBLK + 1, P, T), "y_gla": (KD + 2, P, T), "y_s5": (KD, P, T),
           "u_d": (D, SCH, NCH), "y_d": (D, SCH, NCH), "kd": (GROUPS, S5I, 2 * SCH - 1, S5I)}
OUTPUTS = {"new_lru": (P, 2, LBLK), "new_gla": (2 * HEADS, DK, DV), "new_s5": (P, 2, GROUPS), "y": (KD, P, T)}


def kernel(**inputs):
    import concourse.bacc as bacc
    from concourse.bass_utils import run_bass_kernel_spmd

    nc = bacc.Bacc("TRN2", target_bir_lowering=False, num_devices=1)
    arrays, dram = {}, {}
    for name, a in layout(inputs).items():
        arrays[f"in_{name}"] = a
        dram[name] = nc.dram_tensor(f"in_{name}", a.shape, mybir.dt.from_np(a.dtype), kind="ExternalInput").ap()
    for name, shape in SCRATCH.items():
        dram[name] = nc.dram_tensor(f"mid_{name}", shape, F32, kind="Internal").ap()
    for name, shape in OUTPUTS.items():
        dram[name] = nc.dram_tensor(f"out_{name}", shape, F32, kind="ExternalOutput").ap()
    build(nc, dram)
    got = run_bass_kernel_spmd(nc, [arrays], core_ids=[0]).results[0]
    y = np.ascontiguousarray(got["out_y"].reshape(D, T).T)
    s5 = got["out_new_s5"].reshape(2, S5P, 2, GROUPS).transpose(2, 0, 3, 1)[:, None, None]
    return (y[None, 0:TC], y[None, TC:], got["out_new_gla"].reshape(1, 1, 2, HEADS, DK, DV),
            np.ascontiguousarray(s5[0]), np.ascontiguousarray(s5[1]),
            np.ascontiguousarray(got["out_new_lru"].transpose(1, 2, 0)).reshape(1, 1, 2, LBLK * P))
```
